# Optimizing a Trainium2 kernel written in Bass

```python
import math
import jax, jax.numpy as jnp
from jax import lax
import numpy as np

D_MODEL = 1024
BATCH = 1
SEQ = 1024
DEPTH = 2
DEC_BATCH = 8
DEC_SEQ = 1
PAST_LEN = 256
PAGE_SIZE = 128

N_EVEN = (DEPTH + 1) // 2
N_ODD = DEPTH // 2
MIX_WIDTH = D_MODEL
A_WIDTH = MIX_WIDTH // 2
A_GROUPS = 4
A_GROUP_DIM = A_WIDTH // A_GROUPS
A_CHUNK = 128
B_HEADS = 4
B_HEAD_DIM = (MIX_WIDTH // 2) // B_HEADS
B_WIDTH = B_HEADS * B_HEAD_DIM
B_CONV = 4
B_CHUNK = 64
C_HEADS = 8
C_HEAD_DIM = MIX_WIDTH // (2 * C_HEADS)
C_VDIM = 2 * C_HEAD_DIM
C_QBLOCK = 128
D_FF = ((8 * D_MODEL // 3 + 127) // 128) * 128
FFN_CONV = 3
EPS = 1e-6

EVEN_IN = 2 * A_WIDTH + 4 * B_WIDTH + 2 * B_HEADS
EVEN_SPLITS = [A_WIDTH, 2 * A_WIDTH, 2 * A_WIDTH + 3 * B_WIDTH, 2 * A_WIDTH + 4 * B_WIDTH, 2 * A_WIDTH + 4 * B_WIDTH + B_HEADS]
ODD_IN = 3 * MIX_WIDTH

kernel_name = "hybrid_gmlp_gdn_diffattn_step"

def rmsnorm(x, g):
    xf = x.astype(jnp.float32)
    y = xf * lax.rsqrt(jnp.mean(xf * xf, axis=-1, keepdims=True) + EPS)
    return (y * g.astype(jnp.float32)).astype(x.dtype)

def l2norm(x):
    xf = x.astype(jnp.float32)
    return (xf * lax.rsqrt(jnp.sum(xf * xf, axis=-1, keepdims=True) + EPS)).astype(x.dtype)

def causal_dwconv(x, w, buf):
    width = w.shape[0]
    T = x.shape[1]
    xx = jnp.concatenate([buf.astype(x.dtype), x], axis=1)
    y = sum(xx[:, j:j + T] * w[j] for j in range(width))
    return y, xx[:, -(width - 1):]

def chunk_spatial_gate(u, v, w_s, b_s):
    Bn, T, _ = u.shape
    c = min(T, A_CHUNK)
    n = T // c
    vg = v.reshape(Bn, n, c, A_GROUPS, A_GROUP_DIM)
    w = jnp.tril(w_s[:, :c, :c])
    mixed = jnp.einsum('gts,bnsgd->bntgd', w, vg) + b_s[:, :c].T[None, None, :, :, None]
    return u * mixed.reshape(Bn, T, A_WIDTH)

def gated_delta_rule(q, k, v, g, beta, s0):
    Bn, T, H, DK = q.shape
    DV = v.shape[-1]
    c = min(T, B_CHUNK)
    n = T // c

    def blocks(a):
        a = a.astype(jnp.float32).reshape((Bn, n, c) + a.shape[2:])
        return jnp.swapaxes(jnp.moveaxis(a, 1, 0), 2, 3)

    xs = tuple(blocks(a) for a in (q, k, v, g, beta))
    incl = jnp.tril(jnp.ones((c, c), bool))
    strict = jnp.tril(jnp.ones((c, c), bool), -1)
    eye = jnp.eye(c, dtype=jnp.float32)

    def step(S, blk):
        qc, kc, vc, gc, bc = blk
        G = jnp.cumsum(gc, axis=-1)
        diff = G[..., :, None] - G[..., None, :]
        decay = jnp.where(incl, jnp.exp(jnp.where(incl, diff, 0.0)), 0.0)
        kk = jnp.einsum('bhtd,bhid->bhti', kc, kc)
        A = jnp.where(strict, bc[..., :, None] * decay * kk, 0.0)
        eG = jnp.exp(G)
        rhs = bc[..., None] * (vc - eG[..., None] * jnp.einsum('bhtd,bhde->bhte', kc, S))
        U = lax.linalg.triangular_solve(A + eye, rhs, left_side=True, lower=True, unit_diagonal=True)
        qk = jnp.einsum('bhtd,bhid->bhti', qc, kc) * decay
        o = eG[..., None] * jnp.einsum('bhtd,bhde->bhte', qc, S) + jnp.einsum('bhti,bhie->bhte', qk, U)
        w_end = jnp.exp(G[..., -1:] - G)
        S_new = eG[..., -1, None, None] * S + jnp.einsum('bhid,bhie->bhde', kc * w_end[..., None], U)
        return S_new, o

    S_fin, o = lax.scan(step, s0.astype(jnp.float32), xs)
    o = jnp.swapaxes(jnp.moveaxis(o, 0, 1), 2, 3).reshape(Bn, T, H, DV)
    return o.astype(v.dtype), S_fin

def diff_attention_block(q, k, v, q_pos, k_pos, lam, slopes):
    s = jnp.einsum('bqhcd,bkhcd->bhcqk', q, k).astype(jnp.float32)
    dist = (q_pos[:, None] - k_pos[None, :]).astype(jnp.float32)
    s = s - slopes[None, :, None, None, None] * dist
    s = jnp.where(dist >= 0, s, -jnp.inf)
    p = jax.nn.softmax(s, axis=-1)
    w = p[:, :, 0] - lam * p[:, :, 1]
    return jnp.einsum('bhqk,bkhe->bqhe', w.astype(v.dtype), v)

def prompt_attention(q, k, v, lam, slopes):
    Bn, T = q.shape[:2]
    nq = T // C_QBLOCK
    qb = jnp.moveaxis(q.reshape(Bn, nq, C_QBLOCK, C_HEADS, 2, C_HEAD_DIM), 1, 0)
    k_pos = jnp.arange(T)

    def one(args):
        qi, i = args
        q_pos = i * C_QBLOCK + jnp.arange(C_QBLOCK)
        return diff_attention_block(qi, k, v, q_pos, k_pos, lam, slopes)

    out = lax.map(one, (qb, jnp.arange(nq)))
    return jnp.moveaxis(out, 0, 1).reshape(Bn, T, C_HEADS, C_VDIM)

def conv_ffn(h, w_gate, w_up, w_conv, b_conv, w_down, buf):
    g = h @ w_gate
    g, new_buf = causal_dwconv(g, w_conv, buf)
    a = jax.nn.gelu(g + b_conv) * (h @ w_up)
    return a @ w_down, new_buf

def setup_inputs(seed: int = 0) -> dict:
    key = jax.random.key(seed)
    keys = iter(jax.random.split(key, 48))
    f32 = jnp.float32

    def nrm(shape, scale):
        return jax.random.normal(next(keys), shape, f32) * scale

    def gain(shape):
        return 1.0 + nrm(shape, 0.05)

    n_pages = PAST_LEN // PAGE_SIZE
    n_pool = (5 * DEC_BATCH * n_pages + 3) // 4
    perm = jax.random.permutation(next(keys), n_pool)
    page_table = perm[:DEC_BATCH * n_pages].reshape(DEC_BATCH, n_pages).astype(jnp.int32)
    dt = jnp.exp(jax.random.uniform(next(keys), (N_EVEN, B_HEADS), f32, math.log(1e-3), math.log(1e-1)))
    return {
        "x_prompt": nrm((BATCH, SEQ, D_MODEL), 1.0),
        "x_sample": nrm((DEC_BATCH, DEC_SEQ, D_MODEL), 1.0),
        "cache_k": nrm((N_ODD, n_pool, PAGE_SIZE, C_HEADS, 2, C_HEAD_DIM), 1.0),
        "cache_v": nrm((N_ODD, n_pool, PAGE_SIZE, C_HEADS, C_VDIM), 1.0),
        "page_table": page_table,
        "state_gdn": nrm((N_EVEN, DEC_BATCH, B_HEADS, B_HEAD_DIM, B_HEAD_DIM), 0.1),
        "state_gdn_conv": nrm((N_EVEN, DEC_BATCH, B_CONV - 1, 3 * B_WIDTH), 1.0),
        "state_ffn_conv": nrm((DEPTH, DEC_BATCH, FFN_CONV - 1, D_FF), 1.0),
        "norm_mix_pre": gain((DEPTH, D_MODEL)),
        "norm_mix_post": gain((DEPTH, D_MODEL)),
        "norm_ffn_pre": gain((DEPTH, D_MODEL)),
        "norm_ffn_post": gain((DEPTH, D_MODEL)),
        "w_in_even": nrm((N_EVEN, D_MODEL, EVEN_IN), D_MODEL ** -0.5),
        "a_v_norm": gain((N_EVEN, A_WIDTH)),
        "a_w_s": nrm((N_EVEN, A_GROUPS, A_CHUNK, A_CHUNK), A_CHUNK ** -0.5),
        "a_b_s": 1.0 + nrm((N_EVEN, A_GROUPS, A_CHUNK), 0.02),
        "b_conv_w": nrm((N_EVEN, B_CONV, 3 * B_WIDTH), B_CONV ** -0.5),
        "b_a_log": jnp.log(jax.random.uniform(next(keys), (N_EVEN, B_HEADS), f32, 1.0, 16.0)),
        "b_dt_bias": dt + jnp.log(-jnp.expm1(-dt)),
        "b_out_norm": gain((N_EVEN, B_HEAD_DIM)),
        "w_out_even": nrm((N_EVEN, MIX_WIDTH, D_MODEL), MIX_WIDTH ** -0.5),
        "w_in_odd": nrm((N_ODD, D_MODEL, ODD_IN), D_MODEL ** -0.5),
        "c_lambda": nrm((N_ODD, 4, C_HEAD_DIM), 0.1),
        "c_subln": gain((N_ODD, C_VDIM)),
        "w_out_odd": nrm((N_ODD, MIX_WIDTH, D_MODEL), MIX_WIDTH ** -0.5),
        "w_ffn_gate": nrm((DEPTH, D_MODEL, D_FF), D_MODEL ** -0.5),
        "w_ffn_up": nrm((DEPTH, D_MODEL, D_FF), D_MODEL ** -0.5),
        "w_ffn_conv": nrm((DEPTH, FFN_CONV, D_FF), FFN_CONV ** -0.5),
        "b_ffn_conv": nrm((DEPTH, D_FF), 0.01),
        "w_ffn_down": nrm((DEPTH, D_FF, D_MODEL), D_FF ** -0.5),
    }

def reference(x_prompt, x_sample, cache_k, cache_v, page_table, state_gdn, state_gdn_conv, state_ffn_conv,
              norm_mix_pre, norm_mix_post, norm_ffn_pre, norm_ffn_post,
              w_in_even, a_v_norm, a_w_s, a_b_s, b_conv_w, b_a_log, b_dt_bias, b_out_norm, w_out_even,
              w_in_odd, c_lambda, c_subln, w_out_odd,
              w_ffn_gate, w_ffn_up, w_ffn_conv, b_ffn_conv, w_ffn_down):
    f32 = jnp.float32
    slopes = jnp.exp2(-8.0 * jnp.arange(1, C_HEADS + 1, dtype=f32) / C_HEADS)

    def run_group(x, sample):
        Bn, T, _ = x.shape
        gdn_s, gdn_c, chunk_v, k_rows, v_rows, ffn_b = [], [], [], [], [], []
        for layer in range(DEPTH):
            j = layer // 2
            h = rmsnorm(x, norm_mix_pre[layer])
            if layer % 2 == 0:
                proj = h @ w_in_even[j]
                a_u, a_v, b_qkv, b_z, b_beta, b_alpha = jnp.split(proj, EVEN_SPLITS, axis=-1)
                a_u = jax.nn.gelu(a_u)
                a_v = rmsnorm(jax.nn.gelu(a_v), a_v_norm[j])
                a_out = chunk_spatial_gate(a_u, a_v, a_w_s[j], a_b_s[j])
                if sample:
                    conv0, s0 = state_gdn_conv[j], state_gdn[j]
                else:
                    conv0 = jnp.zeros((Bn, B_CONV - 1, 3 * B_WIDTH), x.dtype)
                    s0 = jnp.zeros((Bn, B_HEADS, B_HEAD_DIM, B_HEAD_DIM), f32)
                qkv, conv_new = causal_dwconv(b_qkv, b_conv_w[j], conv0)
                qkv = jax.nn.silu(qkv).reshape(Bn, T, 3, B_HEADS, B_HEAD_DIM)
                q = l2norm(qkv[:, :, 0]) * (B_HEAD_DIM ** -0.5)
                k = l2norm(qkv[:, :, 1])
                v = qkv[:, :, 2]
                beta = jax.nn.sigmoid(b_beta.astype(f32))
                g = -jnp.exp(b_a_log[j].astype(f32)) * jax.nn.softplus(b_alpha.astype(f32) + b_dt_bias[j].astype(f32))
                o, s_new = gated_delta_rule(q, k, v, g, beta, s0)
                o = rmsnorm(o, b_out_norm[j]) * jax.nn.silu(b_z.reshape(Bn, T, B_HEADS, B_HEAD_DIM))
                mix = jnp.concatenate([a_out, o.reshape(Bn, T, B_WIDTH)], axis=-1) @ w_out_even[j]
                gdn_s.append(s_new)
                gdn_c.append(conv_new)
                if sample:
                    chunk_v.append(a_v)
            else:
                proj = h @ w_in_odd[j]
                q, k, v = jnp.split(proj, 3, axis=-1)
                q = q.reshape(Bn, T, C_HEADS, 2, C_HEAD_DIM) * (C_HEAD_DIM ** -0.5)
                k = k.reshape(Bn, T, C_HEADS, 2, C_HEAD_DIM)
                v = v.reshape(Bn, T, C_HEADS, C_VDIM)
                lam_init = 0.8 - 0.6 * math.exp(-0.3 * layer)
                lq = c_lambda[j].astype(f32)
                lam = jnp.exp(jnp.sum(lq[0] * lq[1])) - jnp.exp(jnp.sum(lq[2] * lq[3])) + lam_init
                if sample:
                    n_past = page_table.shape[1] * PAGE_SIZE
                    k_past = cache_k[j, page_table].reshape(Bn, n_past, C_HEADS, 2, C_HEAD_DIM).astype(k.dtype)
                    v_past = cache_v[j, page_table].reshape(Bn, n_past, C_HEADS, C_VDIM).astype(v.dtype)
                    att = diff_attention_block(q, jnp.concatenate([k_past, k], axis=1),
                                               jnp.concatenate([v_past, v], axis=1),
                                               n_past + jnp.arange(T), jnp.arange(n_past + T), lam, slopes)
                else:
                    att = prompt_attention(q, k, v, lam, slopes)
                att = rmsnorm(att, c_subln[j]) * (1.0 - lam_init)
                mix = att.reshape(Bn, T, MIX_WIDTH) @ w_out_odd[j]
                k_rows.append(k)
                v_rows.append(v)
            x = x + rmsnorm(mix, norm_mix_post[layer])
            h = rmsnorm(x, norm_ffn_pre[layer])
            buf0 = state_ffn_conv[layer] if sample else jnp.zeros((Bn, FFN_CONV - 1, D_FF), x.dtype)
            f, buf_new = conv_ffn(h, w_ffn_gate[layer], w_ffn_up[layer], w_ffn_conv[layer], b_ffn_conv[layer],
                                  w_ffn_down[layer], buf0)
            ffn_b.append(buf_new)
            x = x + rmsnorm(f, norm_ffn_post[layer])
        return x, gdn_s, gdn_c, chunk_v, k_rows, v_rows, ffn_b

    y_p, gs_p, gc_p, _, k_p, v_p, fb_p = run_group(x_prompt, False)
    y_s, gs_s, gc_s, cv_s, k_s, v_s, fb_s = run_group(x_sample, True)
    return (y_p, y_s,
            jnp.stack(gs_p), jnp.stack(gs_s),
            jnp.stack(gc_p), jnp.stack(gc_s),
            jnp.stack(cv_s),
            jnp.stack(k_p), jnp.stack(v_p),
            jnp.stack(k_s), jnp.stack(v_s),
            jnp.stack(fb_p), jnp.stack(fb_s))


_drawn_inputs = setup_inputs


def setup_inputs(seed=0):
    import zlib

    import numpy as np

    out = dict(_drawn_inputs(seed))
    spreads = {}
    factors = {'a_b_s': 4.288, 'c_lambda': 4.676, 'b_ffn_conv': 6.662}
    for name, (base, spread) in spreads.items():
        noise = np.random.default_rng([zlib.crc32(name.encode()), seed]).standard_normal(out[name].shape)
        drawn = base * np.exp(spread * noise) if base else spread * noise
        out[name] = __import__('jax').numpy.asarray(drawn.astype(out[name].dtype))
    for name, factor in factors.items():
        out[name] = (out[name] * factor).astype(out[name].dtype)
    return out
```

```python
import math
from contextlib import ExitStack

import numpy as np

import concourse.bass as bass
from concourse import mybir

ALU = mybir.AluOpType
ACT = mybir.ActivationFunctionType
F32 = mybir.dt.float32
F32R = mybir.dt.float32r
I32 = mybir.dt.int32
AX_X = mybir.AxisListType.X

P = 128
D = 1024
KD = D // P
PROMPT = 1024
SAMPLES = 8
TOK = PROMPT + SAMPLES
CH = TOK // 3
NCHUNK = PROMPT // P
FF = 2816
FT = FF // P
GROUPS = FT // 2
HEADS_B = 4
HEADS_C = 8
EPS = 1e-6
MASKED = -1e30
PAGES = 2
PAST = PAGES * P
LAM_INIT = 0.8 - 0.6 * math.exp(-0.3)

C_ID, C_INCL, C_STRICT, C_ONE = 0, 128, 256, 384
C_LEVEL = 512
C_SEL = C_LEVEL + 7 * 128
C_RESET = C_SEL + 8 * 128
C_DIST = C_RESET + PROMPT
C_SLOPE = C_DIST + PROMPT
C_SBIAS = C_SLOPE + HEADS_C
C_PAIR = C_SBIAS + PAST + 1
C_HALF = C_PAIR + 64
C_END = C_HALF + 2


def shape_constants():
    c = np.zeros((P, C_END), np.float32)
    i = np.arange(P)
    c[:, C_ID:C_ID + P] = np.eye(P)
    c[:, C_INCL:C_INCL + P] = i[:, None] <= i[None, :]
    c[:, C_STRICT:C_STRICT + P] = i[:, None] < i[None, :]
    c[:, C_ONE:C_ONE + P] = 1.0
    for n, s in enumerate((1, 2, 4, 8, 16, 32, 64)):
        col, row = i[:, None] // s, i[None, :] // s
        c[:, C_LEVEL + n * P:C_LEVEL + (n + 1) * P] = (row % 2 == 1) & (col == row - 1)
    for n in range(8):
        c[n if n < 4 else 32 + n - 4, C_SEL + n * P:C_SEL + (n + 1) * P] = 1.0
    c[:, C_RESET:C_RESET + PROMPT] = np.arange(PROMPT) % P != 0
    dist = (np.arange(PROMPT) - (PROMPT - P))[None, :] - i[:, None]
    c[:, C_DIST:C_DIST + PROMPT] = np.where(dist <= 0, dist, MASKED)
    slopes = np.exp2(-8.0 * np.arange(1, HEADS_C + 1, dtype=np.float32) / HEADS_C).astype(np.float32)
    c[:, C_SLOPE:C_SLOPE + HEADS_C] = slopes
    head = (i // SAMPLES) % HEADS_C
    c[:, C_SBIAS:C_SBIAS + PAST + 1] = slopes[head][:, None] * (np.arange(PAST + 1) - PAST)[None, :]
    c[:, C_PAIR:C_PAIR + 64] = (i % 64)[:, None] == np.arange(64)[None, :]
    c[:64, C_HALF] = 1.0
    c[64:, C_HALF + 1] = 1.0
    return c


class Steps:

    def __init__(self, eng, sem, base=0):
        self.eng, self.sem, self.base, self.n = eng, sem, base, 0

    def note(self, ins):
        ins.then_inc(self.sem, 1)
        self.n += 1
        return self.base + self.n

    def done(self, ins):
        self.eng.wait_ge(self.sem, self.note(ins))


class Trunk:
    pass


def one(t, i):
    if isinstance(i, int):
        return t[:, i, :]
    return t[:, bass.ds(i, 1), :].rearrange("p a w -> p (a w)")


def region(ps, r):
    return ps[:, 3 * r:3 * r + 3, 0:CH]


def chunks(ap):
    return ap.rearrange("p (c n) -> p c n", c=3)


def product(pe, ps, r, wh, wl, hh, hl, first, last):
    for n, (w, h) in enumerate(((wh, hh), (wh, hl), (wl, hh))):
        for c in range(3):
            ins = pe.matmul(ps[:, 3 * r + c, 0:CH], w, h[:, c * CH:(c + 1) * CH],
                            start=first and n == 0, stop=last and n == 2)
    return ins


class SquareSums:

    def __init__(self, sem, name, sq, sqh, sql, onesr, ps, r):
        self.squared, self.split, self.added = sem(name + "_squared"), sem(name + "_split"), sem(name + "_added")
        self.sq, self.sqh, self.sql, self.onesr, self.ps, self.r = sq, sqh, sql, onesr, ps, r

    def scalar(self, act, k, src):
        if k >= 2:
            act.wait_ge(self.split, 2 * (k - 1))
        act.activation(self.sq[:, k % 2, :], src, ACT.Square).then_inc(self.squared, 1)

    def vector(self, dve, k):
        dve.wait_ge(self.squared, k + 1)
        if k >= 2:
            dve.wait_ge(self.added, k - 1)
        dve.tensor_copy(self.sqh[:, k % 2, :], self.sq[:, k % 2, :]).then_inc(self.split, 1)
        dve.wait_ge(self.split, 2 * k + 1)
        dve.tensor_tensor(self.sql[:, k % 2, :], self.sq[:, k % 2, :], self.sqh[:, k % 2, :],
                          ALU.subtract).then_inc(self.split, 1)

    def tensor(self, pe, k, first, last):
        pe.wait_ge(self.split, 2 * (k + 1))
        for n, h in enumerate((self.sqh, self.sql)):
            for c in range(3):
                ins = pe.matmul(self.ps[:, 3 * self.r + c, 0:CH], self.onesr,
                                h[:, k % 2, c * CH:(c + 1) * CH], start=first and n == 0, stop=last and n == 1)
        ins.then_inc(self.added, 1)


def rsqrt_of(act, steps, out, sums, scale, eps_col):
    steps.done(act.activation(out, sums, ACT.Ln, scale=scale, bias=eps_col))
    return act.activation(out, out, ACT.Exp, scale=-0.5)


def stage_load_x(nc, T, x_prompt, x_sample, gains, consts):
    with ExitStack() as ctx:
        sb = lambda n, s, d=F32: ctx.enter_context(nc.sbuf_tensor("ld_" + n, s, d))
        sem = lambda n: nc.alloc_semaphore("ld_" + n)
        xin, xs, grow = sb("xin", [P, 2, D]), sb("xs", [SAMPLES, D]), sb("grow", [8, D])
        const_in, small_in, landed = sem("const_in"), sem("small_in"), [sem("landed0"), sem("landed1")]
        turned, moved = [sem("turned0"), sem("turned1")], [sem("moved0"), sem("moved1")]
        small_turned, prepared = sem("small_turned"), sem("prepared")
        src = x_prompt.rearrange("b (t p) d -> (b t) p d", p=P)
        with nc.Block() as block:
            @block.sync
            def _(sp):
                sp.dma_start(T.con[:], consts[:, 0:512]).then_inc(const_in, 16)
                with sp.Fori(0, NCHUNK // 2) as i:
                    for r in range(2):
                        sp.wait_ge(turned[r], i)
                        sp.dma_start(xin[:, r, :], src[bass.ds(2 * i + r, 1), :, :].rearrange("a p d -> p (a d)")
                                     ).then_inc(landed[r], 16)
                sp.dma_start(xs[:], x_sample.rearrange("b s d -> (b s) d")).then_inc(small_in, 16)
                for n, g in enumerate(gains):
                    sp.dma_start(grow[2 * n:2 * n + 2, :], g).then_inc(small_in, 16)

            @block.tensor
            def _(pe):
                pe.wait_ge(const_in, 16)
                with pe.Fori(0, NCHUNK // 2) as i:
                    for r in range(2):
                        pe.wait_ge(landed[r], 16 * i + 16)
                        pe.wait_ge(moved[r], i)
                        for k in range(KD):
                            ins = pe.transpose(T.ps[:, 2 * r + k // 4, P * (k % 4):P * (k % 4) + P],
                                               xin[:, r, P * k:P * k + P], T.ident)
                        ins.then_inc(turned[r], 1)
                pe.wait_ge(small_in, 16 * (1 + len(gains)))
                for k in range(KD):
                    pe.transpose(T.ps[:, 6, 8 * k:8 * k + 8], xs[:, P * k:P * k + P], T.ident[0:8, 0:8])
                for k in range(KD):
                    ins = pe.transpose(T.ps[:, 7, 8 * k:8 * k + 8], grow[:, P * k:P * k + P], T.ident[0:8, 0:8])
                ins.then_inc(small_turned, 1)

            @block.vector
            def _(dve):
                with dve.Fori(0, NCHUNK // 2) as i:
                    for r in range(2):
                        dve.wait_ge(turned[r], i + 1)
                        dve.tensor_copy(T.acc[:, :, bass.ds((2 * i + r) * P, P)],
                                        T.ps[:, 2 * r:2 * r + 2, :].rearrange("p b (k n) -> p (b k) n", n=P)
                                        ).then_inc(moved[r], 1)
                dve.wait_ge(small_turned, 1)
                dve.tensor_copy(T.acc[:, :, PROMPT:TOK], T.ps[:, 6, 0:64].rearrange("p (k n) -> p k n", n=8))
                dve.tensor_copy(T.gain[:], T.ps[:, 7, 0:64].rearrange("p (k n) -> p k n", n=8))
                dve.wait_ge(const_in, 16)
                dve.tensor_copy(T.onesr[:], T.con[:, C_ONE:C_ONE + P])
                dve.memset(T.one[:], 1.0)
                dve.memset(T.eps[:], EPS).then_inc(prepared, 1)


def stage_norm(nc, T, name, post_row, pre_row, x_scratch, want_h=True):
    with ExitStack() as ctx:
        sb = lambda n, s, d=F32: ctx.enter_context(nc.sbuf_tensor(name + n, s, d))
        sem = lambda n: nc.alloc_semaphore(name + n)
        post = post_row is not None
        sq = T.wraw[:, 0:2 * TOK].rearrange("p (a n) -> p a n", a=2)
        xold = T.wraw[:, 2 * TOK:4 * TOK].rearrange("p (a n) -> p a n", a=2)
        sqh = T.wh[:, 0:2 * TOK].rearrange("p (a n) -> p a n", a=2)
        sql = T.wl[:, 0:2 * TOK].rearrange("p (a n) -> p a n", a=2)
        rstd = T.wraw[:, 4 * TOK:5 * TOK]
        rs2 = sb("rs2", [P, TOK])
        ss1 = SquareSums(sem, "s1", sq, sqh, sql, T.onesr[:], T.ps, 0)
        ss2 = SquareSums(sem, "s2", sq, sqh, sql, T.onesr[:], T.ps, 1)
        root1, root2, act_own = sem("root1"), sem("root2"), sem("act_own")
        x_in = [sem("x_in0"), sem("x_in1")]
        x_new, x_out, dve_own = sem("x_new"), sem("x_out"), sem("dve_own")
        scaled, hi_done, lo_done = sem("scaled"), sem("hi_done"), sem("lo_done")
        xs = x_scratch.rearrange("(k p) n -> k p n", p=P)
        with nc.Block() as block:
            @block.sync
            def _(sp):
                for k in range(KD if post else 0):
                    if k >= 2:
                        sp.wait_ge(x_new, k - 1)
                    sp.dma_start(xold[:, k % 2, :], xs[k]).then_inc(x_in[k % 2], 16)
                for k in range(KD):
                    if post:
                        sp.wait_ge(x_new, k + 1)
                    sp.dma_start(xs[k], T.acc[:, k, :]).then_inc(x_out, 16)
                sp.wait_ge(x_out, 16 * KD)

            @block.scalar
            def _(act):
                steps = Steps(act, act_own)
                if post:
                    for k in range(KD):
                        ss1.scalar(act, k, T.acc[:, k, :])
                    act.wait_ge(ss1.added, KD)
                    rsqrt_of(act, steps, chunks(rstd), region(T.ps, 0), 1.0 / D, T.eps[:]).then_inc(root1, 1)
                if not want_h:
                    return
                for k in range(KD):
                    if post:
                        act.wait_ge(x_new, k + 1)
                        act.wait_ge(ss1.split, 2 * KD)
                    ss2.scalar(act, k, T.acc[:, k, :])
                act.wait_ge(ss2.added, KD)
                rsqrt_of(act, steps, chunks(rs2[:]), region(T.ps, 1), 1.0 / D, T.eps[:]).then_inc(root2, 1)
                for k in range(KD):
                    act.wait_ge(scaled, k + 1)
                    act.activation(T.hh[:, k, :], sq[:, k % 2, :], ACT.Copy).then_inc(hi_done, 1)

            @block.vector
            def _(dve):
                steps = Steps(dve, dve_own)
                if post:
                    for k in range(KD):
                        ss1.vector(dve, k)
                    dve.wait_ge(root1, 1)
                    for k in range(KD):
                        steps.done(dve.tensor_tensor(T.acc[:, k, :], T.acc[:, k, :], rstd, ALU.mult))
                        dve.wait_ge(x_in[k % 2], 16 * (k // 2 + 1))
                        dve.scalar_tensor_tensor(out=T.acc[:, k, :], in0=T.acc[:, k, :],
                                                 scalar=T.gain[:, k, post_row:post_row + 1],
                                                 in1=xold[:, k % 2, :], op0=ALU.mult, op1=ALU.add).then_inc(x_new, 1)
                        if want_h:
                            if k == 0:
                                dve.wait_ge(ss1.added, KD)
                            ss2.vector(dve, k)
                elif want_h:
                    for k in range(KD):
                        ss2.vector(dve, k)
                if want_h:
                    dve.wait_ge(root2, 1)
                    for k in range(KD):
                        if k >= 2:
                            dve.wait_ge(lo_done, k - 1)
                        dve.scalar_tensor_tensor(out=sq[:, k % 2, :], in0=T.acc[:, k, :],
                                                 scalar=T.gain[:, k, pre_row:pre_row + 1], in1=rs2[:],
                                                 op0=ALU.mult, op1=ALU.mult).then_inc(scaled, 1)

            @block.gpsimd
            def _(pool):
                for k in range(KD if want_h else 0):
                    pool.wait_ge(hi_done, k + 1)
                    pool.tensor_tensor(T.hl[:, k, :], sq[:, k % 2, :], T.hh[:, k, :], ALU.subtract).then_inc(lo_done, 1)

            @block.tensor
            def _(pe):
                if post:
                    for k in range(KD):
                        ss1.tensor(pe, k, k == 0, k == KD - 1)
                for k in range(KD if want_h else 0):
                    ss2.tensor(pe, k, k == 0, k == KD - 1)


def stage_project(nc, T, name, w, m_tiles, out_scratch=None, tail=None):
    BODY = 4
    n_iter = m_tiles // BODY
    with ExitStack() as ctx:
        sb = lambda n, s, d=F32: ctx.enter_context(nc.sbuf_tensor(name + n, s, d))
        sem = lambda n: nc.alloc_semaphore(name + n)
        out = sb("out", [P, 2, TOK]) if out_scratch is not None else None
        landed = [sem(f"landed{b}") for b in range(2)]
        hi = [sem(f"hi{j}") for j in range(BODY)]
        lo = [sem(f"lo{j}") for j in range(BODY)]
        made = [sem(f"made{j}") for j in range(BODY)]
        moved = [sem(f"moved{j}") for j in range(BODY)]
        stored = [sem(f"stored{j}") for j in range(BODY)]
        t_in, t_zero, t_made = sem("t_in"), sem("t_zero"), sem("t_made")
        raw = [T.wraw[:, 2048 * b:2048 * b + 2048].rearrange("p (k n) -> p k n", k=KD) for b in range(2)]
        slot_h = [T.wh[:, 1024 * j:1024 * j + 1024].rearrange("p (k n) -> p k n", k=KD) for j in range(6)]
        slot_l = [T.wl[:, 1024 * j:1024 * j + 1024].rearrange("p (k n) -> p k n", k=KD) for j in range(6)]
        traw = T.wraw[:, 4096:4096 + 1024].rearrange("p (k n) -> p k n", k=KD)
        wk = w.rearrange("(k p) m -> p k m", p=P)
        if out_scratch is not None:
            rows = out_scratch.rearrange("(m p) n -> m p n", p=P)
        with nc.Block() as block:
            @block.sync
            def _(sp):
                def load(i):
                    for b in range(2):
                        sp.wait_ge(lo[2 * b + 1], i)
                        sp.dma_start(raw[b], wk[:, :, bass.ds((2 * i + b) * 256, 256)]).then_inc(landed[b], 16)

                def store(j, i):
                    if out_scratch is not None:
                        sp.wait_ge(moved[j], i + 1)
                        sp.dma_start(rows[bass.ds(BODY * i + j, 1), :, :].rearrange("a p n -> p (a n)"),
                                     out[:, j % 2, :]).then_inc(stored[j], 16)

                load(0)
                with sp.Fori(0, n_iter - 1) as i:
                    load(i + 1)
                    for j in range(BODY):
                        store(j, i)
                if tail is not None:
                    sp.wait_ge(t_zero, 1)
                    sp.dma_start(traw[:, :, 0:4], wk[:, :, tail:tail + 4]).then_inc(t_in, 16)
                    sp.dma_start(traw[:, :, 32:36], wk[:, :, tail + 4:tail + 8]).then_inc(t_in, 16)
                for j in range(BODY):
                    store(j, n_iter - 1)
                if tail is not None:
                    store(0, n_iter)
                if out_scratch is not None:
                    for j in range(BODY):
                        sp.wait_ge(stored[j], 16 * (n_iter + (tail is not None and j == 0)))

            @block.gpsimd
            def _(pool):
                if tail is not None:
                    pool.memset(traw, 0.0).then_inc(t_zero, 1)
                with pool.Fori(0, n_iter) as i:
                    for j in range(BODY):
                        pool.wait_ge(hi[j], i + 1)
                        pool.tensor_tensor(slot_l[j], raw[j // 2][:, :, P * (j % 2):P * (j % 2) + P], slot_h[j],
                                              ALU.subtract).then_inc(lo[j], 1)
                if tail is not None:
                    pool.wait_ge(hi[0], n_iter + 1)
                    pool.tensor_tensor(slot_l[0], traw, slot_h[0],
                                              ALU.subtract).then_inc(lo[0], 1)

            @block.scalar
            def _(act):
                with act.Fori(0, n_iter) as i:
                    for j in range(BODY):
                        act.wait_ge(landed[j // 2], 16 * i + 16)
                        act.wait_ge(made[j], i)
                        act.activation(slot_h[j], raw[j // 2][:, :, P * (j % 2):P * (j % 2) + P],
                                       ACT.Copy).then_inc(hi[j], 1)
                if tail is not None:
                    act.wait_ge(t_in, 32)
                    act.wait_ge(made[0], n_iter)
                    act.activation(slot_h[0], traw, ACT.Copy).then_inc(hi[0], 1)

            @block.tensor
            def _(pe):
                def tile(j, i):
                    pe.wait_ge(lo[j], i + 1)
                    if j >= 2:
                        pe.wait_ge(moved[j - 2], i + 1)
                    else:
                        pe.wait_ge(moved[j + 2], i)
                    for k in range(KD):
                        ins = product(pe, T.ps, j % 2, slot_h[j][:, k, :], slot_l[j][:, k, :],
                                      T.hh[:, k, :], T.hl[:, k, :], k == 0, k == KD - 1)
                    ins.then_inc(made[j], 1)

                with pe.Fori(0, n_iter) as i:
                    for j in range(BODY):
                        tile(j, i)
                if tail is not None:
                    tile(0, n_iter)

            @block.vector
            def _(dve):
                def move(j, i):
                    dve.wait_ge(made[j], i + 1)
                    if out_scratch is None:
                        dst = one(T.acc, BODY * i + j)
                    else:
                        dst = out[:, j % 2, :]
                        if j >= 2:
                            dve.wait_ge(stored[j - 2], 16 * i + 16)
                        else:
                            dve.wait_ge(stored[j + 2], 16 * i)
                    dve.tensor_copy(chunks(dst), region(T.ps, j % 2)).then_inc(moved[j], 1)

                with dve.Fori(0, n_iter) as i:
                    for j in range(BODY):
                        move(j, i)
                if tail is not None:
                    move(0, n_iter)



def stage_ffn(nc, T, name, layer, w_gate, w_up, w_down, w_conv, b_conv, state, out_prompt, out_sample):
    ROWS = 2 * SAMPLES + 4
    with ExitStack() as ctx:
        sb = lambda n, s, d=F32: ctx.enter_context(nc.sbuf_tensor(name + n, s, d))
        sem = lambda n: nc.alloc_semaphore(name + n)
        raw_g, raw_u = (T.wraw[:, 2048 * b:2048 * b + 2048].rearrange("p (k n) -> p k n", k=KD) for b in range(2))
        raw_d = T.wraw[:, 4096:6144]
        raws = (raw_g, raw_u)
        slot_h = [T.wh[:, 1024 * j:1024 * j + 1024].rearrange("p (k n) -> p k n", k=KD) for j in range(4)]
        slot_l = [T.wl[:, 1024 * j:1024 * j + 1024].rearrange("p (k n) -> p k n", k=KD) for j in range(4)]
        down_h, down_l = T.wh[:, 4096:6144], T.wl[:, 4096:6144]
        prm = sb("prm", [P, FT, ROWS])
        last = sb("last", [P, FT, 2 + SAMPLES])
        ah, al = sb("ah", [P, 2, TOK], F32R), sb("al", [P, 2, TOK], F32R)
        gate, conv = sb("gate", [P, 2 + TOK]), sb("conv", [P, TOK])
        rows_in, turned, prm_done = sem("rows_in"), sem("turned"), sem("prm_done")
        in_g, in_u, in_d = sem("in_g"), sem("in_u"), sem("in_d")
        landed = (in_g, in_u)
        hi = [sem(f"hi{j}") for j in range(4)]
        lo = [sem(f"lo{j}") for j in range(4)]
        made = [sem(f"made{j}") for j in range(4)]
        hi_d, lo_d, made_d = sem("hi_d"), sem("lo_d"), sem("made_d")
        gate_in, conved, activated = sem("gate_in"), sem("conved"), sem("activated")
        multiplied, collected, acc_zero = sem("multiplied"), sem("collected"), sem("acc_zero")
        kept, a_ready, dve_own = sem("kept"), sem("a_ready"), sem("dve_own")
        out_done, keep_turned, keep_moved = sem("out_done"), sem("keep_turned"), sem("keep_moved")
        wg, wu = (w.rearrange("(k p) m -> p k m", p=P) for w in (w_gate, w_up))
        wd = w_down.rearrange("(g j p) m -> g p j m", p=P, j=2)
        KEEP = 2 + SAMPLES
        rows = T.wraw[0:ROWS, 0:FF]

        with nc.Block() as block:
            @block.sync
            def _(sp):
                for b in range(SAMPLES):
                    sp.dma_start(rows[2 * b:2 * b + 2, :], state[layer, b]).then_inc(rows_in, 16)
                sp.dma_start(rows[2 * SAMPLES:2 * SAMPLES + 3, :], w_conv).then_inc(rows_in, 16)
                sp.dma_start(rows[2 * SAMPLES + 3:ROWS, :], b_conv).then_inc(rows_in, 16)

            @block.tensor
            def _(pe):
                pe.wait_ge(rows_in, 16 * (SAMPLES + 2))
                for t in range(FT):
                    ins = pe.transpose(T.ps[:, 6, ROWS * t:ROWS * t + ROWS], rows[:, P * t:P * t + P],
                                       T.ident[0:ROWS, 0:ROWS])
                ins.then_inc(turned, 1)

            @block.vector
            def _(dve):
                dve.memset(gate[:, 0:2], 0.0)
                dve.wait_ge(turned, 1)
                dve.tensor_copy(prm[:], T.ps[:, 6, 0:FT * ROWS].rearrange("p (t r) -> p t r", r=ROWS)).then_inc(prm_done, 1)

        with nc.Block() as block:
            @block.sync
            def _(sp):
                def load_gu(g):
                    for b, w in enumerate((wg, wu)):
                        sp.wait_ge(lo[b], g)
                        sp.wait_ge(lo[2 + b], g)
                        sp.dma_start(raws[b], w[:, :, bass.ds(256 * g, 256)]).then_inc(landed[b], 16)

                def load_d(g):
                    sp.wait_ge(lo_d, g)
                    sp.dma_start(raw_d.rearrange("p (j m) -> p j m", j=2),
                                 wd[bass.ds(g, 1), :, :, :].rearrange("a p j m -> p (a j) m")).then_inc(in_d, 16)

                load_gu(0)
                with sp.Fori(0, GROUPS - 1) as g:
                    load_d(g)
                    load_gu(g + 1)
                load_d(GROUPS - 1)

            @block.scalar
            def _(act):
                def split(s, g):
                    act.wait_ge(landed[s % 2], 16 * g + 16)
                    act.wait_ge(made[s], g)
                    act.activation(slot_h[s], raws[s % 2][:, :, P * (s // 2):P * (s // 2) + P],
                                   ACT.Copy).then_inc(hi[s], 1)

                def tile(t, g):
                    act.wait_ge(made[2 * t], g + 1)
                    act.wait_ge(kept, 2 * g + t)
                    act.wait_ge(conved, 2 * g + t)
                    act.activation(chunks(gate[:, 2:2 + TOK]), region(T.ps, 0), ACT.Copy).then_inc(gate_in, 1)

                def gelu(t, g):
                    act.wait_ge(conved, 2 * g + t + 1)
                    act.activation(conv[:], conv[:], ACT.Gelu_apprx_tanh,
                                   bias=prm[:, bass.ds(2 * g + t, 1), ROWS - 1:ROWS].rearrange("p a n -> p (a n)")
                                   ).then_inc(activated, 1)

                def split_down(g):
                    act.wait_ge(in_d, 16 * g + 16)
                    act.wait_ge(made_d, KD * g)
                    act.activation(down_h, raw_d, ACT.Copy).then_inc(hi_d, 1)

                def group(g, more):
                    tile(0, g)
                    if more:
                        split(0, g + 1)
                    gelu(0, g)
                    if more:
                        split(1, g + 1)
                    split_down(g)
                    tile(1, g)
                    if more:
                        split(2, g + 1)
                    gelu(1, g)
                    if more:
                        split(3, g + 1)

                for s in range(4):
                    split(s, 0)
                with act.Fori(0, GROUPS - 1) as g:
                    group(g, True)
                group(GROUPS - 1, False)

            @block.gpsimd
            def _(pool):
                def split(s, g):
                    pool.wait_ge(hi[s], g + 1)
                    pool.tensor_tensor(slot_l[s], raws[s % 2][:, :, P * (s // 2):P * (s // 2) + P], slot_h[s],
                                              ALU.subtract).then_inc(lo[s], 1)

                def keep(t, g):
                    pool.wait_ge(gate_in, 2 * g + t + 1)
                    pool.tensor_copy(last[:, bass.ds(2 * g + t, 1), :].rearrange("p a n -> p (a n)"),
                                     gate[:, PROMPT:2 + TOK]).then_inc(kept, 1)

                def group(g, more):
                    keep(0, g)
                    if more:
                        split(0, g + 1)
                        split(1, g + 1)
                    pool.wait_ge(hi_d, g + 1)
                    pool.tensor_tensor(down_l, raw_d, down_h, ALU.subtract).then_inc(lo_d, 1)
                    keep(1, g)
                    if more:
                        split(2, g + 1)
                        split(3, g + 1)

                pool.memset(T.acc[:], 0.0).then_inc(acc_zero, 1)
                for s in range(4):
                    split(s, 0)
                with pool.Fori(0, GROUPS - 1) as g:
                    group(g, True)
                group(GROUPS - 1, False)

            @block.tensor
            def _(pe):
                def hidden(s, g):
                    pe.wait_ge(lo[s], g + 1)
                    for k in range(KD):
                        ins = product(pe, T.ps, s % 2, slot_h[s][:, k, :], slot_l[s][:, k, :],
                                      T.hh[:, k, :], T.hl[:, k, :], k == 0, k == KD - 1)
                    ins.then_inc(made[s], 1)

                def tile0(g):
                    pe.wait_ge(gate_in, 2 * g)
                    hidden(0, g)
                    pe.wait_ge(multiplied, 2 * g)
                    hidden(1, g)

                def down(g, taken):
                    pe.wait_ge(lo_d, g + 1)
                    pe.wait_ge(a_ready, 2 * g + 2)
                    for m in range(KD):
                        if m >= 2:
                            pe.wait_ge(collected, KD * g + m - 1)
                        for j in range(2):
                            cols = slice(1024 * j + P * m, 1024 * j + P * m + P)
                            ins = product(pe, T.ps, m % 2, down_h[:, cols], down_l[:, cols], ah[:, j, :], al[:, j, :],
                                          j == 0, j == 1)
                        ins.then_inc(made_d, 1)
                        if m == 0:
                            pe.wait_ge(multiplied, taken)

                tile0(0)
                pe.wait_ge(gate_in, 1)
                hidden(2, 0)
                pe.wait_ge(multiplied, 1)
                hidden(3, 0)
                with pe.Fori(1, GROUPS) as g:
                    tile0(g)
                    pe.wait_ge(gate_in, 2 * g + 1)
                    down(g - 1, 2 * g + 1)
                    pe.wait_ge(collected, KD * g - 1)
                    hidden(2, g)
                    pe.wait_ge(collected, KD * g)
                    hidden(3, g)
                pe.wait_ge(gate_in, 2 * GROUPS)
                down(GROUPS - 1, 2 * GROUPS)

            @block.vector
            def _(dve):
                def tap(g, t, r):
                    return prm[:, bass.ds(2 * g + t, 1), r:r + 1].rearrange("p a n -> p (a n)")

                def convolve(steps, t, g):
                    dve.wait_ge(gate_in, 2 * g + t + 1)
                    pv, sv = conv[:, 0:PROMPT], conv[:, PROMPT:TOK]
                    st = [prm[:, bass.ds(2 * g + t, 1), j:2 * SAMPLES:2].rearrange("p a b -> p (a b)") for j in range(2)]
                    first, second, third = (tap(g, t, 2 * SAMPLES + j) for j in range(3))
                    steps.note(dve.tensor_scalar(pv, gate[:, 0:PROMPT], first, None, ALU.mult))
                    steps.done(dve.tensor_scalar(sv, st[0], first, None, ALU.mult))
                    steps.note(dve.scalar_tensor_tensor(out=pv, in0=gate[:, 1:1 + PROMPT], scalar=second, in1=pv,
                                                        op0=ALU.mult, op1=ALU.add))
                    steps.done(dve.scalar_tensor_tensor(out=sv, in0=st[1], scalar=second, in1=sv,
                                                        op0=ALU.mult, op1=ALU.add))
                    dve.scalar_tensor_tensor(out=conv[:], in0=gate[:, 2:2 + TOK], scalar=third, in1=conv[:],
                                             op0=ALU.mult, op1=ALU.add).then_inc(conved, 1)

                def multiply(t, g):
                    dve.wait_ge(activated, 2 * g + t + 1)
                    dve.wait_ge(made[2 * t + 1], g + 1)
                    dve.tensor_tensor(chunks(conv[:]), chunks(conv[:]), region(T.ps, 1), ALU.mult).then_inc(multiplied, 1)

                def split(steps, t, g):
                    dve.wait_ge(multiplied, 2 * g + t + 1)
                    steps.done(dve.tensor_copy(ah[:, t, :], conv[:]))
                    dve.tensor_tensor(al[:, t, :], conv[:], ah[:, t, :], ALU.subtract).then_inc(a_ready, 1)
                    dve.wait_ge(a_ready, 2 * g + t + 1)

                def collect(g):
                    for m in range(KD):
                        dve.wait_ge(made_d, KD * g + m + 1)
                        a = chunks(T.acc[:, m, :])
                        dve.tensor_tensor(a, a, region(T.ps, m % 2), ALU.add).then_inc(collected, 1)
                    dve.wait_ge(collected, KD * g + KD)

                def group(g, with_down):
                    steps = Steps(dve, dve_own, 10 * g)
                    convolve(steps, 0, g)
                    multiply(0, g)
                    if with_down:
                        collect(g - 1)
                    split(steps, 0, g)
                    convolve(steps, 1, g)
                    multiply(1, g)
                    split(steps, 1, g)
                    assert steps.n == 10

                group(0, False)
                dve.wait_ge(acc_zero, 1)
                with dve.Fori(1, GROUPS) as g:
                    group(g, True)
                collect(GROUPS - 1)

        with nc.Block() as block:
            flat = T.ps[0:KEEP, 0:6, :].rearrange("r b n -> r (b n)")
            kept_rows = T.wraw[0:KEEP, 0:FF]

            @block.tensor
            def _(pe):
                for t in range(FT):
                    ins = pe.transpose(flat[:, P * t:P * t + P], last[:, t, :], T.ident)
                ins.then_inc(keep_turned, 1)

            @block.vector
            def _(dve):
                dve.wait_ge(keep_turned, 1)
                dve.tensor_copy(kept_rows, flat[:, 0:FF]).then_inc(keep_moved, 1)

            @block.sync
            def _(sp):
                sp.dma_start(out_sample[layer, :, 0, :], state[layer, :, 1, :]).then_inc(out_done, 16)
                sp.wait_ge(keep_moved, 1)
                sp.dma_start(out_prompt[layer, 0], kept_rows[0:2, :]).then_inc(out_done, 16)
                sp.dma_start(out_sample[layer, :, 1, :], kept_rows[2:KEEP, :]).then_inc(out_done, 16)
                sp.wait_ge(out_done, 48)


def open_trunk(nc, ctx):
    T = Trunk()
    sb = lambda n, s, d=F32: ctx.enter_context(nc.sbuf_tensor(n, s, d))
    T.ps = ctx.enter_context(nc.psum_tensor("ps", [P, 8, 512], F32))
    T.wraw = sb("wraw", [P, 6144])
    T.con, T.onesr, T.eps = sb("con_sb", [P, 512]), sb("onesr", [P, P], F32R), sb("eps", [P, 1])
    T.ident = T.con[:, C_ID:C_ID + P]
    T.one = sb("one", [P, 1])
    T.gain = sb("gain", [P, KD, 8])
    T.acc = sb("acc", [P, KD, TOK])
    return T


class split_weights:

    def __init__(self, nc, T, name):
        self.ctx, self.nc, self.T, self.name = ExitStack(), nc, T, name

    def __enter__(self):
        self.T.wh = self.ctx.enter_context(self.nc.sbuf_tensor(self.name + "wh", [P, 6144], F32R))
        self.T.wl = self.ctx.enter_context(self.nc.sbuf_tensor(self.name + "wl", [P, 6144], F32R))

    def __exit__(self, *exc):
        return self.ctx.__exit__(*exc)


class split_pair:

    def __init__(self, nc, T, name):
        self.ctx, self.nc, self.T, self.name = ExitStack(), nc, T, name

    def __enter__(self):
        self.T.hh = self.ctx.enter_context(self.nc.sbuf_tensor(self.name + "hi", [P, KD, TOK], F32R))
        self.T.hl = self.ctx.enter_context(self.nc.sbuf_tensor(self.name + "lo", [P, KD, TOK], F32R))

    def __exit__(self, *exc):
        return self.ctx.__exit__(*exc)


def over(ap, n):
    return ap.unsqueeze(1).to_broadcast([ap.shape[0], n, ap.shape[-1]])


def per_column(ap, w):
    return ap.unsqueeze(2).to_broadcast([ap.shape[0], ap.shape[1], w])


def stage_split(nc, T, name):
    with ExitStack() as ctx:
        hi, lo = (nc.alloc_semaphore(name + n) for n in ("hi", "lo"))
        with nc.Block() as block:
            @block.scalar
            def _(act):
                for k in range(KD):
                    act.activation(T.hh[:, k, :], T.acc[:, k, :], ACT.Copy).then_inc(hi, 1)

            @block.vector
            def _(dve):
                for k in range(KD):
                    dve.wait_ge(hi, k + 1)
                    dve.tensor_tensor(T.hl[:, k, :], T.acc[:, k, :], T.hh[:, k, :], ALU.subtract).then_inc(lo, 1)


def stage_gmlp(nc, T, proj, v_gain, w_s, b_s, chunk_v):
    G = 4
    with ExitStack() as ctx:
        sb = lambda n, s, d=F32: ctx.enter_context(nc.sbuf_tensor("ga_" + n, s, d))
        sem = lambda n: nc.alloc_semaphore("ga_" + n)
        u, v, rstd = sb("u", [P, G, TOK]), sb("v", [P, G, TOK]), sb("rstd", [P, TOK])
        vt, mixed = sb("vt", [P, 2, G, P]), sb("mixed", [P, 2, G, P])
        wn, wt, bias = sb("wn", [P, G, P]), sb("wt", [P, G, P]), sb("bias", [P, G, P])
        w00, gain, incl = sb("w00", [P, G]), sb("gain", [P, G]), T.con[:, C_INCL:C_INCL + P]
        sm, cv = sb("sm", [P, G, SAMPLES]), sb("cv", [SAMPLES, G * P])
        sq = T.wraw[:, 0:2 * TOK].rearrange("p (a n) -> p a n", a=2)
        sqh = T.wh[:, 0:2 * TOK].rearrange("p (a n) -> p a n", a=2)
        sql = T.wl[:, 0:2 * TOK].rearrange("p (a n) -> p a n", a=2)
        ss = SquareSums(sem, "ss", sq, sqh, sql, T.onesr[:], T.ps, 0)
        v_in, u_in, par_in, out_done = sem("v_in"), sem("u_in"), sem("par_in"), sem("out_done")
        v_act, u_act, rstd_done, act_own = sem("v_act"), sem("u_act"), sem("rstd_done"), sem("act_own")
        normed, w_turned, w_masked = sem("normed"), sem("w_turned"), sem("w_masked")
        turned, vt_moved, mixed_made, mix_moved = sem("turned"), sem("vt_moved"), sem("mixed_made"), sem("mix_moved")
        cv_turned, cv_moved, dve_own = sem("cv_turned"), sem("cv_moved"), sem("dve_own")
        rows = proj.rearrange("(m p) n -> p m n", p=P)
        with nc.Block() as block:
            @block.sync
            def _(sp):
                sp.dma_start(v[:], rows[:, G:2 * G, :]).then_inc(v_in, 16)
                sp.dma_start(u[:], rows[:, 0:G, :]).then_inc(u_in, 16)
                sp.dma_start(wn[:], w_s.rearrange("g t s -> t g s")).then_inc(par_in, 16)
                sp.dma_start(bias[:], b_s.rearrange("g t -> (g t)").partition_broadcast(P)).then_inc(par_in, 16)
                sp.dma_start(w00[:], w_s[:, 0, 0].partition_broadcast(P), allow_slow_non_contiguous=True).then_inc(par_in, 16)
                sp.dma_start(gain[:], v_gain.rearrange("(g p) -> p g", p=P), allow_slow_non_contiguous=True).then_inc(par_in, 16)
                sp.wait_ge(cv_moved, 1)
                sp.dma_start(chunk_v, cv[:]).then_inc(out_done, 16)
                sp.wait_ge(out_done, 16)

            @block.scalar
            def _(act):
                steps = Steps(act, act_own)
                act.wait_ge(v_in, 16)
                for g in range(G):
                    act.activation(v[:, g, :], v[:, g, :], ACT.Gelu_apprx_tanh).then_inc(v_act, 1)
                act.wait_ge(v_act, G)
                act.wait_ge(u_in, 16)
                act.activation(u[:], u[:], ACT.Gelu_apprx_tanh).then_inc(u_act, 1)
                for g in range(G):
                    ss.scalar(act, g, v[:, g, :])
                act.wait_ge(ss.added, G)
                rsqrt_of(act, steps, chunks(rstd[:]), region(T.ps, 0), 1.0 / (G * P), T.eps[:]).then_inc(rstd_done, 1)
                for c in range(NCHUNK):
                    act.wait_ge(turned, c + 1)
                    if c >= 2:
                        act.wait_ge(mixed_made, c - 1)
                    act.activation(vt[:, c % 2], T.ps[:, 6 + c % 2, :].rearrange("p (g n) -> p g n", g=G),
                                   ACT.Copy).then_inc(vt_moved, 1)

            @block.tensor
            def _(pe):
                pe.wait_ge(par_in, 64)
                for g in range(G):
                    ins = pe.transpose(T.ps[:, 3, P * g:P * g + P], wn[:, g, :], T.ident)
                ins.then_inc(w_turned, 1)
                for g in range(G):
                    ss.tensor(pe, g, g == 0, g == G - 1)
                pe.wait_ge(normed, G)
                pe.wait_ge(w_masked, 1)
                for g in range(G):
                    ins = pe.transpose(T.ps[0:SAMPLES, 3, P * g:P * g + P], v[:, g, PROMPT:TOK], T.ident)
                ins.then_inc(cv_turned, 1)

                def turn(c):
                    if c >= 2:
                        pe.wait_ge(vt_moved, c - 1)
                    for g in range(G):
                        ins = pe.transpose(T.ps[:, 6 + c % 2, P * g:P * g + P], v[:, g, P * c:P * c + P], T.ident)
                    ins.then_inc(turned, 1)

                turn(0)
                for c in range(NCHUNK):
                    if c + 1 < NCHUNK:
                        turn(c + 1)
                    pe.wait_ge(vt_moved, c + 1)
                    if c >= 2:
                        pe.wait_ge(mix_moved, c - 1)
                    for g in range(G):
                        ins = pe.matmul(T.ps[:, 4 + c % 2, P * g:P * g + P], vt[:, c % 2, g, :], wt[:, g, :],
                                        start=True, stop=True)
                    ins.then_inc(mixed_made, 1)

            @block.vector
            def _(dve):
                steps = Steps(dve, dve_own)
                dve.wait_ge(w_turned, 1)
                dve.tensor_tensor(wt[:], T.ps[:, 3, :].rearrange("p (g n) -> p g n", g=G), over(incl, G),
                                  ALU.mult).then_inc(w_masked, 1)
                dve.wait_ge(v_act, G)
                for g in range(G):
                    ss.vector(dve, g)
                dve.wait_ge(rstd_done, 1)
                for g in range(G):
                    dve.scalar_tensor_tensor(out=v[:, g, :], in0=v[:, g, :], scalar=gain[:, g:g + 1], in1=rstd[:],
                                             op0=ALU.mult, op1=ALU.mult).then_inc(normed, 1)
                dve.wait_ge(normed, G)
                dve.wait_ge(u_act, 1)
                for g in range(G):
                    steps.note(dve.tensor_scalar(sm[:, g, :], v[:, g, PROMPT:TOK], w00[:, g:g + 1], bias[:, g, 0:1],
                                                 ALU.mult, ALU.add))
                steps.eng.wait_ge(steps.sem, steps.n)
                dve.tensor_tensor(T.acc[:, 0:G, PROMPT:TOK], sm[:], u[:, :, PROMPT:TOK], ALU.mult)
                dve.wait_ge(cv_turned, 1)
                dve.tensor_copy(cv[:], T.ps[0:SAMPLES, 3, :]).then_inc(cv_moved, 1)
                for c in range(NCHUNK):
                    dve.wait_ge(mixed_made, c + 1)
                    if c >= 2:
                        dve.wait_ge(dve_own, steps.n - 1)
                    dve.tensor_tensor(mixed[:, c % 2], T.ps[:, 4 + c % 2, :].rearrange("p (g n) -> p g n", g=G),
                                      bias[:], ALU.add).then_inc(mix_moved, 1)
                    dve.wait_ge(mix_moved, c + 1)
                    steps.note(dve.tensor_tensor(T.acc[:, 0:G, P * c:P * c + P], mixed[:, c % 2],
                                                 u[:, :, P * c:P * c + P], ALU.mult))


def head_norms(nc, T, name, tiles, scale, factor, after=None):
    n = len(tiles)
    with ExitStack() as ctx:
        sb = lambda s_, s, d=F32: ctx.enter_context(nc.sbuf_tensor(name + s_, s, d))
        sem = lambda s_: nc.alloc_semaphore(name + s_)
        rstd = sb("rstd", [P, 2, TOK])
        sq = T.wraw[:, 0:2 * TOK].rearrange("p (a n) -> p a n", a=2)
        sqh = T.wh[:, 0:2 * TOK].rearrange("p (a n) -> p a n", a=2)
        sql = T.wl[:, 0:2 * TOK].rearrange("p (a n) -> p a n", a=2)
        sums = [SquareSums(sem, "ss", sq, sqh, sql, T.onesr[:], T.ps, r) for r in range(1)]
        ss = sums[0]
        rooted, scaled, act_own = sem("rooted"), sem("scaled"), sem("act_own")
        with nc.Block() as block:
            @block.scalar
            def _(act):
                steps = Steps(act, act_own)

                def root(k):
                    act.wait_ge(ss.added, k + 1)
                    if k >= 2:
                        act.wait_ge(scaled, k - 1)
                    rsqrt_of(act, steps, chunks(rstd[:, k % 2, :]), region(T.ps, k % 2), scale, T.eps[:]
                             ).then_inc(rooted, 1)

                for k in range(n):
                    ss.scalar(act, k, tiles[k])
                    if k >= 1:
                        root(k - 1)
                root(n - 1)

            @block.vector
            def _(dve):
                def multiply(k):
                    dve.wait_ge(rooted, k + 1)
                    dve.scalar_tensor_tensor(out=tiles[k], in0=tiles[k], scalar=factor(k), in1=rstd[:, k % 2, :],
                                             op0=ALU.mult, op1=ALU.mult).then_inc(scaled, 1)
                    if after is not None:
                        dve.wait_ge(scaled, k + 1)
                        dve.tensor_tensor(tiles[k], tiles[k], after(k), ALU.mult)

                for k in range(n):
                    ss.vector(dve, k)
                    if k >= 1:
                        multiply(k - 1)
                multiply(n - 1)

            @block.tensor
            def _(pe):
                for k in range(n):
                    if k >= 2:
                        pe.wait_ge(rooted, k - 1)
                    ss.r = k % 2
                    ss.tensor(pe, k, True, True)


def stage_conv_b(nc, T, proj, qkv, gates, w_conv, state, a_log, dt_bias, consts, out_prompt, out_sample):
    M = 3 * HEADS_B
    TAPS = 4
    ROWS = (TAPS - 1) * SAMPLES + TAPS
    KEEP = TAPS - 1 + SAMPLES
    W = M * P
    with ExitStack() as ctx:
        sb = lambda n, s, d=F32: ctx.enter_context(nc.sbuf_tensor("cb_" + n, s, d))
        sem = lambda n: nc.alloc_semaphore("cb_" + n)
        raw = sb("raw", [P, 2, TAPS - 1 + TOK])
        conv = T.wraw[:, 0:2 * TOK].rearrange("p (a n) -> p a n", a=2)
        prm, last = sb("prm", [P, M, ROWS]), sb("last", [P, M, KEEP])
        rows = T.wraw[0:ROWS, 2 * TOK:2 * TOK + W]
        reset = sb("reset", [P, PROMPT])
        x, t1, t2 = (sb(n, [P, TOK]) for n in ("x", "t1", "t2"))
        col = sb("col", [P, 3])
        hr = slice(32, 32 + HEADS_B)
        rows_in, turned, prm_done, gates_in = sem("rows_in"), sem("turned"), sem("prm_done"), sem("gates_in")
        dve_own, act_own, g1, g2 = sem("dve_own"), sem("act_own"), sem("g1"), sem("g2")
        raw_in = [sem("raw_in0"), sem("raw_in1")]
        conved, silued, kept = sem("conved"), sem("silued"), sem("kept")
        k_turned, k_moved, out_done, loop_own = sem("k_turned"), sem("k_moved"), sem("out_done"), sem("loop_own")
        mt = proj.rearrange("(m p) n -> m p n", p=P)
        with nc.Block() as block:
            @block.sync
            def _(sp):
                n = (TAPS - 1) * SAMPLES
                sp.dma_start(rows[0:n, :], state.rearrange("b j c -> (b j) c")).then_inc(rows_in, 16)
                sp.dma_start(rows[n:ROWS, :], w_conv).then_inc(rows_in, 16)
                sp.dma_start(gates[:], mt[24, 0:64, :]).then_inc(gates_in, 16)
                sp.dma_start(col[hr, 0:1], a_log.rearrange("(a b) -> a b", b=1)).then_inc(gates_in, 16)
                sp.dma_start(col[hr, 1:2], dt_bias.rearrange("(a b) -> a b", b=1)).then_inc(gates_in, 16)
                sp.dma_start(reset[:], consts[:, C_RESET:C_RESET + PROMPT]).then_inc(gates_in, 16)

            @block.tensor
            def _(pe):
                pe.wait_ge(rows_in, 32)
                for t in range(M):
                    ins = pe.transpose(T.ps[:, 6, ROWS * t:ROWS * t + ROWS], rows[:, P * t:P * t + P],
                                       T.ident[0:ROWS, 0:ROWS])
                ins.then_inc(turned, 1)

            @block.scalar
            def _(act):
                steps = Steps(act, act_own)
                act.wait_ge(gates_in, 64)
                act.activation(gates[0:HEADS_B, :], gates[0:HEADS_B, :], ACT.Sigmoid)
                act.wait_ge(g1, 1)
                steps.done(act.activation(t1[hr, :], t1[hr, :], ACT.Exp, scale=-1.0))
                steps.note(act.activation(t1[hr, :], t1[hr, :], ACT.Ln, bias=T.one[hr, :]))
                act.activation(col[hr, 2:3], col[hr, 0:1], ACT.Exp).then_inc(g2, 1)
                act.wait_ge(act_own, steps.n)

            @block.vector
            def _(dve):
                steps = Steps(dve, dve_own)
                dve.memset(raw[:, :, 0:TAPS - 1], 0.0)
                dve.wait_ge(turned, 1)
                dve.tensor_copy(prm[:], T.ps[:, 6, 0:M * ROWS].rearrange("p (t r) -> p t r", r=ROWS))
                dve.wait_ge(gates_in, 64)
                steps.done(dve.tensor_scalar(x[hr, :], gates[hr, :], col[hr, 1:2], None, ALU.add))
                steps.done(dve.tensor_scalar(t1[hr, :], x[hr, :], -1.0, None, ALU.mult))
                dve.tensor_tensor(t1[hr, :], t1[hr, :], x[hr, :], ALU.max).then_inc(g1, 1)
                dve.wait_ge(g2, 1)
                dve.wait_ge(act_own, 2)
                steps.done(dve.scalar_tensor_tensor(out=t2[hr, :], in0=x[hr, :], scalar=0.0, in1=t1[hr, :],
                                                    op0=ALU.max, op1=ALU.add))
                steps.done(dve.tensor_scalar(gates[hr, :], t2[hr, :], col[hr, 2:3], -1.0, ALU.mult, ALU.mult))
                steps.done(dve.tensor_tensor_scan(x[hr, 0:PROMPT], reset[hr, :], gates[hr, 0:PROMPT], 0.0,
                                                  ALU.mult, ALU.add))
                dve.tensor_copy(gates[hr, 0:PROMPT], x[hr, 0:PROMPT])

        with nc.Block() as block:
            @block.sync
            def _(sp):
                with sp.Fori(0, M // 2) as i:
                    for r in range(2):
                        sp.wait_ge(kept, 2 * i)
                        sp.wait_ge(conved, 2 * i)
                        sp.dma_start(raw[:, r, TAPS - 1:], mt[bass.ds(8 + 2 * i + r, 1), :, :].rearrange("a p n -> p (a n)")
                                     ).then_inc(raw_in[r], 16)

            @block.gpsimd
            def _(pool):
                with pool.Fori(0, M // 2) as i:
                    for r in range(2):
                        pool.wait_ge(raw_in[r], 16 * i + 16)
                        pool.tensor_copy(last[:, bass.ds(2 * i + r, 1), :].rearrange("p a n -> p (a n)"),
                                         raw[:, r, PROMPT:TAPS - 1 + TOK]).then_inc(kept, 1)

            @block.vector
            def _(dve):
                with dve.Fori(0, M // 2) as i:
                    steps = Steps(dve, loop_own, 12 * i)
                    for r in range(2):
                        m = 2 * i + r
                        tap = [prm[:, bass.ds(m, 1), ROWS - TAPS + j:ROWS - TAPS + j + 1].rearrange("p a n -> p (a n)")
                               for j in range(TAPS)]
                        st = [prm[:, bass.ds(m, 1), j:ROWS - TAPS:TAPS - 1].rearrange("p a b -> p (a b)")
                              for j in range(TAPS - 1)]
                        dve.wait_ge(raw_in[r], 16 * i + 16)
                        dve.wait_ge(silued, 2 * i)
                        pv, sv = conv[:, r, 0:PROMPT], conv[:, r, PROMPT:TOK]
                        steps.note(dve.tensor_scalar(pv, raw[:, r, 0:PROMPT], tap[0], None, ALU.mult))
                        steps.done(dve.tensor_scalar(sv, st[0], tap[0], None, ALU.mult))
                        for j in range(1, TAPS - 1):
                            steps.note(dve.scalar_tensor_tensor(out=pv, in0=raw[:, r, j:j + PROMPT], scalar=tap[j],
                                                                in1=pv, op0=ALU.mult, op1=ALU.add))
                            steps.done(dve.scalar_tensor_tensor(out=sv, in0=st[j], scalar=tap[j], in1=sv,
                                                                op0=ALU.mult, op1=ALU.add))
                        dve.scalar_tensor_tensor(out=conv[:, r, :], in0=raw[:, r, TAPS - 1:], scalar=tap[TAPS - 1],
                                                 in1=conv[:, r, :], op0=ALU.mult, op1=ALU.add).then_inc(conved, 1)
                    assert steps.n == 12

            @block.scalar
            def _(act):
                with act.Fori(0, M // 2) as i:
                    for r in range(2):
                        act.wait_ge(conved, 2 * i + r + 1)
                        act.activation(one(qkv, 2 * i + r), conv[:, r, :], ACT.Silu).then_inc(silued, 1)

        with nc.Block() as block:
            flat = T.ps[0:KEEP, 0:3, :].rearrange("r b n -> r (b n)")
            kept_rows = T.wraw[0:KEEP, 0:W]

            @block.tensor
            def _(pe):
                for t in range(M):
                    ins = pe.transpose(flat[:, P * t:P * t + P], last[:, t, :], T.ident)
                ins.then_inc(k_turned, 1)

            @block.vector
            def _(dve):
                dve.wait_ge(k_turned, 1)
                dve.tensor_copy(kept_rows, flat[:, 0:W]).then_inc(k_moved, 1)

            @block.sync
            def _(sp):
                sp.dma_start(out_sample[:, 0:TAPS - 2, :], state[:, 1:TAPS - 1, :]).then_inc(out_done, 16)
                sp.wait_ge(k_moved, 1)
                sp.dma_start(out_prompt[0], kept_rows[0:TAPS - 1, :]).then_inc(out_done, 16)
                sp.dma_start(out_sample[:, TAPS - 2, :], kept_rows[TAPS - 1:KEEP, :]).then_inc(out_done, 16)
                sp.wait_ge(out_done, 48)


def stage_delta(nc, T, qkv, gates, consts, state_out):
    H = HEADS_B
    LV = 7
    UP = 2 * LV - 3
    with ExitStack() as ctx:
        sb = lambda n, s, d=F32: ctx.enter_context(nc.sbuf_tensor("gd_" + n, s, d))
        sem = lambda n: nc.alloc_semaphore("gd_" + n)
        both = lambda n: [sem(n + "0"), sem(n + "1")]
        masks, sel, cap = sb("masks", [P, LV, P]), sb("sel", [64, 8, P]), sb("cap", [P, P])
        tiles, rows = sb("tiles", [P, 2, 3 * H, P]), sb("rows", [64, 2, P])
        col, eg_col, beg, wend = (sb(n, [P, 2, w]) for n, w in (("col", 64), ("eg_col", H), ("beg", H), ("wend", H)))
        names = "eg dm pt lt qe t tt p1 w2 u kbe vb kw first".split()
        eg, dm, pt, lt, qe, t, tt, p1, w2, u, kbe, vb, kw, first = (sb(n, [P, 2, H, P]) for n in names)
        state = sb("state", [P, H, P])
        am = T.wraw[:].rearrange("p (x l h n) -> p x l h n", x=2, l=LV - 1, h=H)
        bank = [[T.ps[:, 4 * x + n, :].rearrange("p (h n) -> p h n", h=H) for n in range(4)] for x in range(2)]
        heads = range(H)
        K = lambda x, h: tiles[:, x, H + h, :]
        Q = lambda x, h: tiles[:, x, h, :]
        V = lambda x, h: tiles[:, x, 2 * H + h, :]
        con_in, cap_done, out_done = sem("con_in"), sem("cap_done"), sem("out_done")
        staged, spread, v_turned, k_turned = both("staged"), both("spread"), both("v_turned"), both("k_turned")
        col_copied, diffed, decayed, beg_done = both("col_copied"), both("diffed"), both("decayed"), both("beg_done")
        beta_used, kk_made, kq_made, lt_done, pt_done = (both(n) for n in "beta_used kk_made kq_made lt_done pt_done".split())
        masked, qe_done, scaled, tt_first, t_turned = (both(n) for n in "masked qe_done scaled tt_first t_turned".split())
        t_first, p1_made, p1_moved, merged, updated = (both(n) for n in "t_first p1_made p1_moved merged updated".split())
        w2_made, w2_moved, u_made, u_moved, o_made, o_moved, s_made, s_updated = (
            both(n) for n in "w2_made w2_moved u_made u_moved o_made o_moved s_made s_updated".split())

        def run_pairs(eng, body):
            with eng.Fori(0, NCHUNK // 2 - 1) as i:
                body(i, True)
            body(NCHUNK // 2 - 1, False)

        with nc.Block() as block:
            @block.sync
            def _(sp):
                sp.dma_start(masks[:], consts[:, C_LEVEL:C_LEVEL + LV * P].rearrange("p (l n) -> p l n", l=LV)
                             ).then_inc(con_in, 16)
                sp.dma_start(sel[:], consts[0:64, C_SEL:C_SEL + 8 * P].rearrange("p (l n) -> p l n", l=8)
                             ).then_inc(con_in, 16)

            @block.vector
            def _(dve):
                dve.memset(state[:], 0.0)
                dve.tensor_scalar(cap[:], T.con[:, C_INCL:C_INCL + P], -MASKED, MASKED, ALU.mult, ALU.add
                                  ).then_inc(cap_done, 1)
                dve.wait_ge(con_in, 32)

        with nc.Block() as block:
            @block.tensor
            def _(pe):
                def spread_gates(x, i):
                    pe.wait_ge(staged[x], 2 * i + 2)
                    pe.wait_ge(o_moved[x], i)
                    pe.wait_ge(u_moved[x], i)
                    pe.wait_ge(w2_moved[x], i)
                    pe.wait_ge(s_updated[x], H * i)
                    for n in range(8):
                        pe.matmul(bank[x][n // H][:, n % H, :], sel[:, n, :], rows[:, x, :], start=True, stop=True)
                    pe.transpose(T.ps[:, 4 * x + 2, 0:64], rows[:, x, :], T.ident[0:64, 0:64]).then_inc(spread[x], 1)
                    for h in heads:
                        ins = pe.transpose(bank[x][3][:, h, :], K(x, h), T.ident)
                    ins.then_inc(k_turned[x], 1)

                def products(x, i):
                    pe.wait_ge(col_copied[x], i + 1)
                    for h in heads:
                        ins = pe.transpose(bank[x][2][:, h, :], V(x, h), T.ident)
                    ins.then_inc(v_turned[x], 1)
                    pe.wait_ge(decayed[x], 4 * i + 4)
                    for h in heads:
                        ins = pe.matmul(bank[x][1][:, h, :], K(x, h), K(x, h), start=True, stop=True)
                    ins.then_inc(kk_made[x], 1)
                    pe.wait_ge(beta_used[x], i + 1)
                    for h in heads:
                        ins = pe.matmul(bank[x][0][:, h, :], K(x, h), Q(x, h), start=True, stop=True)
                    ins.then_inc(kq_made[x], 1)

                def turn_first(x, i):
                    pe.wait_ge(tt_first[x], i + 1)
                    for h in heads:
                        ins = pe.transpose(bank[x][1][:, h, :], tt[:, x, h, :], T.ident)
                    ins.then_inc(t_turned[x], 1)

                def off_block(x, i, l):
                    if l == 1:
                        pe.wait_ge(t_first[x], i + 1)
                    else:
                        pe.wait_ge(updated[x], UP * i + 2 * (l - 1))
                    pe.wait_ge(masked[x], LV * i + l + 1)
                    for h in heads:
                        ins = pe.matmul(bank[x][1][:, h, :], am[:, x, l - 1, h, :], t[:, x, h, :], start=True, stop=True)
                    ins.then_inc(p1_made[x], 1)

                def merge(x, i, l):
                    pe.wait_ge(p1_moved[x], (LV - 1) * i + l)
                    if l == 1:
                        pe.wait_ge(pt_done[x], i + 1)
                        pe.wait_ge(scaled[x], 3 * i + 3)
                    if l < LV - 1:
                        for h in heads:
                            ins = pe.matmul(bank[x][0][:, h, :], tt[:, x, h, :], p1[:, x, h, :], start=True, stop=True)
                        ins.then_inc(merged[x], 1)
                    for h in heads:
                        ins = pe.matmul(bank[x][2][:, h, :], p1[:, x, h, :], tt[:, x, h, :], start=True, stop=True)
                    ins.then_inc(merged[x], 1)

                def keys(x, i):
                    pe.wait_ge(updated[x], UP * i + UP)
                    for h in heads:
                        ins = pe.matmul(bank[x][3][:, h, :], kbe[:, x, h, :], tt[:, x, h, :], start=True, stop=True)
                    ins.then_inc(w2_made[x], 1)

                def recur(x, i):
                    pe.wait_ge(w2_moved[x], i + 1)
                    pe.wait_ge(s_updated[1 - x], H * i + (H if x else 0))
                    for h in heads:
                        pe.matmul(bank[x][1][:, h, :], tt[:, x, h, :], vb[:, x, h, :], start=True, stop=False)
                        ins = pe.matmul(bank[x][1][:, h, :], w2[:, x, h, :], state[:, h, :], start=False, stop=True)
                    ins.then_inc(u_made[x], 1)
                    pe.wait_ge(u_moved[x], i + 1)
                    for h in heads:
                        ins = pe.matmul(bank[x][2][:, h, :], kw[:, x, h, :], u[:, x, h, :], start=True, stop=True)
                    ins.then_inc(s_made[x], 1)
                    pe.wait_ge(qe_done[x], i + 1)
                    for h in heads:
                        pe.matmul(bank[x][0][:, h, :], state[:, h, :], qe[:, x, h, :], start=True, stop=False)
                        ins = pe.matmul(bank[x][0][:, h, :], u[:, x, h, :], pt[:, x, h, :], start=False, stop=True)
                    ins.then_inc(o_made[x], 1)

                def pair(i, more):
                    for f in (spread_gates, products, turn_first):
                        for x in range(2):
                            f(x, i)
                    for l in range(1, LV):
                        for f in (off_block, merge):
                            for x in range(2):
                                f(x, i, l)
                    for x in range(2):
                        keys(x, i)
                    for x in range(2):
                        recur(x, i)

                run_pairs(pe, pair)

            @block.vector
            def _(dve):
                def differences(x, i):
                    dve.wait_ge(spread[x], i + 1)
                    dve.tensor_copy(col[:, x, :], T.ps[:, 4 * x + 2, 0:64]).then_inc(col_copied[x], 1)
                    dve.wait_ge(col_copied[x], i + 1)
                    for h in heads:
                        dve.scalar_tensor_tensor(out=dm[:, x, h, :], in0=bank[x][1][:, h, :], scalar=col[:, x, 32 + h:33 + h],
                                                 in1=cap[:], op0=ALU.subtract, op1=ALU.min)
                    dve.tensor_tensor(wend[:, x, :], bank[x][1][:, :, P - 1], col[:, x, 32:32 + H], ALU.subtract
                                      ).then_inc(diffed[x], 1)

                def scores(x, i):
                    dve.wait_ge(decayed[x], 4 * i + 4)
                    dve.tensor_tensor(beg[:, x, :], col[:, x, 0:H], eg_col[:, x, :], ALU.mult).then_inc(beg_done[x], 1)
                    dve.tensor_tensor(lt[:, x], dm[:, x], bank[x][0], ALU.mult).then_inc(beta_used[x], 1)
                    dve.wait_ge(beta_used[x], i + 1)
                    dve.wait_ge(kk_made[x], i + 1)
                    dve.tensor_tensor(lt[:, x], lt[:, x], bank[x][1], ALU.mult).then_inc(lt_done[x], 1)
                    dve.wait_ge(kq_made[x], i + 1)
                    dve.tensor_tensor(pt[:, x], dm[:, x], bank[x][0], ALU.mult).then_inc(pt_done[x], 1)

                def first_tt(x, i):
                    dve.wait_ge(masked[x], LV * i + 1)
                    dve.tensor_tensor(tt[:, x], over(T.ident, H), first[:, x], ALU.subtract).then_inc(tt_first[x], 1)

                def first_t(x, i):
                    dve.wait_ge(t_turned[x], i + 1)
                    dve.tensor_copy(t[:, x], bank[x][1]).then_inc(t_first[x], 1)

                def update(x, i, l):
                    if l < LV - 1:
                        dve.wait_ge(merged[x], UP * i + 2 * l - 1)
                        if l == 1:
                            dve.wait_ge(t_first[x], i + 1)
                        dve.tensor_tensor(t[:, x], t[:, x], bank[x][0], ALU.subtract).then_inc(updated[x], 1)
                        dve.wait_ge(merged[x], UP * i + 2 * l)
                    else:
                        dve.wait_ge(merged[x], UP * i + UP)
                    dve.tensor_tensor(tt[:, x], tt[:, x], bank[x][2], ALU.subtract).then_inc(updated[x], 1)
                    dve.wait_ge(updated[x], UP * i + min(2 * l, UP))

                def recur(x, i):
                    dve.wait_ge(u_made[x], i + 1)
                    dve.tensor_copy(u[:, x], bank[x][1]).then_inc(u_moved[x], 1)
                    dve.wait_ge(s_made[x], i + 1)
                    dve.wait_ge(o_made[x], i + 1)
                    for h in heads:
                        dve.scalar_tensor_tensor(out=state[:, h, :], in0=state[:, h, :], scalar=eg[:, x, h, P - 1:P],
                                                 in1=bank[x][2][:, h, :], op0=ALU.mult, op1=ALU.add
                                                 ).then_inc(s_updated[x], 1)
                    dve.wait_ge(s_updated[x], H * i + H)

                def pair(i, more):
                    for f in (differences, scores, first_tt, first_t):
                        for x in range(2):
                            f(x, i)
                    for l in range(1, LV):
                        for x in range(2):
                            update(x, i, l)
                    for x in range(2):
                        recur(x, i)

                run_pairs(dve, pair)

            @block.scalar
            def _(act):
                def decay(x, i):
                    act.wait_ge(diffed[x], i + 1)
                    act.activation(eg_col[:, x, :], col[:, x, 32:32 + H], ACT.Exp).then_inc(decayed[x], 1)
                    act.activation(dm[:, x], dm[:, x], ACT.Exp).then_inc(decayed[x], 1)
                    act.activation(wend[:, x, :], wend[:, x, :], ACT.Exp).then_inc(decayed[x], 1)
                    act.activation(eg[:, x], bank[x][1], ACT.Exp).then_inc(decayed[x], 1)

                def scale(x, i):
                    act.wait_ge(k_turned[x], i + 1)
                    act.wait_ge(v_turned[x], i + 1)
                    act.wait_ge(beg_done[x], i + 1)
                    act.wait_ge(decayed[x], 4 * i + 4)
                    for dst, src, factor in ((vb, 2, col), (kbe, 3, beg), (kw, 3, wend)):
                        for h in heads:
                            ins = act.activation(dst[:, x, h, :], bank[x][src][:, h, :], ACT.Copy,
                                                 scale=factor[:, x, h:h + 1])
                        ins.then_inc(scaled[x], 1)

                def move_p1(x, i, l):
                    act.wait_ge(p1_made[x], (LV - 1) * i + l)
                    act.activation(p1[:, x], bank[x][1], ACT.Copy).then_inc(p1_moved[x], 1)

                def pair(i, more):
                    for f in (decay, scale):
                        for x in range(2):
                            f(x, i)
                    for l in range(1, LV):
                        for x in range(2):
                            move_p1(x, i, l)
                    for x in range(2):
                        act.wait_ge(w2_made[x], i + 1)
                        act.activation(w2[:, x], bank[x][3], ACT.Copy, scale=-1.0).then_inc(w2_moved[x], 1)
                    for x in range(2):
                        act.wait_ge(o_made[x], i + 1)
                        act.activation(T.acc[:, H:2 * H, bass.ds(2 * P * i + P * x, P)], bank[x][0], ACT.Copy
                                       ).then_inc(o_moved[x], 1)

                run_pairs(act, pair)

            @block.gpsimd
            def _(pool):
                def stage(x, i):
                    cols = bass.ds(2 * P * i + P * x, P)
                    pool.tensor_copy(tiles[:, x], qkv[:, :, cols]).then_inc(staged[x], 1)
                    pool.tensor_copy(rows[:, x, :], gates[:, cols]).then_inc(staged[x], 1)

                def pair(i, more):
                    for l in range(LV):
                        for x in range(2):
                            if l == 0:
                                pool.wait_ge(lt_done[x], i + 1)
                            dst = first[:, x] if l == 0 else am[:, x, l - 1]
                            pool.tensor_tensor(dst, lt[:, x], over(masks[:, l, :], H), ALU.mult).then_inc(masked[x], 1)
                    for x in range(2):
                        pool.wait_ge(decayed[x], 4 * i + 4)
                        pool.tensor_tensor(qe[:, x], tiles[:, x, 0:H, :], eg[:, x], ALU.mult).then_inc(qe_done[x], 1)
                    if more:
                        for x in range(2):
                            pool.wait_ge(kq_made[x], i + 1)
                            pool.wait_ge(qe_done[x], i + 1)
                            stage(x, i + 1)

                for x in range(2):
                    stage(x, 0)
                run_pairs(pool, pair)

            @block.sync
            def _(sp):
                sp.wait_ge(s_updated[1], H * (NCHUNK // 2))
                sp.dma_start(state_out.rearrange("h d e -> d h e"), state[:]).then_inc(out_done, 16)
                sp.wait_ge(out_done, 16)


def stage_delta_sample(nc, T, qkv, gates, consts, state_in, state_out):
    H, B = HEADS_B, SAMPLES
    J = H * B
    with ExitStack() as ctx:
        sb = lambda n, s, d=F32: ctx.enter_context(nc.sbuf_tensor("gs_" + n, s, d))
        sem = lambda n: nc.alloc_semaphore("gs_" + n)
        sel, st, kq = sb("sel", [64, 8, P]), sb("st", [P, J, P]), sb("kq", [P, J, 2])
        beta, a, qk, prod, u, o, vs, srows = (sb(n, [P, J]) for n in "beta a qk prod u o vs srows".split())
        kt, ut = sb("kt", [J, P]), sb("ut", [J, P])
        ud = T.wraw[0:J, 0:J * P].rearrange("p (j n) -> p j n", j=J)
        con_in, st_in, staged, spread = sem("con_in"), sem("st_in"), sem("staged"), sem("spread")
        a_done, sums_made, steps_s, u_done = sem("a_done"), sem("sums_made"), sem("steps"), sem("u_done")
        turned, ud_done, outer, st_new, out_done = sem("turned"), sem("ud_done"), sem("outer"), sem("st_new"), sem("out_done")
        with nc.Block() as block:
            @block.sync
            def _(sp):
                sp.dma_start(sel[:], consts[0:64, C_SEL:C_SEL + 8 * P].rearrange("p (l n) -> p l n", l=8)
                             ).then_inc(con_in, 16)
                for h in range(H):
                    sp.dma_start(st[:, B * h:B * h + B, :], state_in[:, h].rearrange("b d e -> d b e")).then_inc(st_in, 16)
                sp.wait_ge(st_new, J)
                for h in range(H):
                    sp.dma_start(state_out[:, h].rearrange("b d e -> d b e"), st[:, B * h:B * h + B, :]).then_inc(out_done, 16)
                sp.wait_ge(out_done, 16 * H)

            @block.tensor
            def _(pe):
                pe.wait_ge(con_in, 16)
                for n in range(8):
                    ins = pe.matmul(T.ps[:, 1, B * n:B * n + B], sel[:, n, :], gates[:, PROMPT:TOK], start=True, stop=True)
                ins.then_inc(spread, 1)
                pe.wait_ge(staged, 4)
                pe.wait_ge(st_in, 16 * H)
                for j in range(J):
                    pe.matmul(T.ps[:, 0, 2 * j:2 * j + 2], st[:, j, :], kq[:, j, :], start=True, stop=True)
                pe.matmul(T.ps[:, 2, 0:J], T.con[:, C_ONE:C_ONE + P], prod[:], start=True, stop=True).then_inc(sums_made, 1)
                pe.wait_ge(u_done, 1)
                pe.transpose(T.ps[0:J, 3, 0:P], srows[:], T.ident)
                pe.transpose(T.ps[0:J, 3, P:2 * P], u[:], T.ident).then_inc(turned, 1)
                for half in range(2):
                    pe.wait_ge(ud_done, 2)
                    pe.wait_ge(st_new, 16 * half)
                    for n in range(4):
                        j = 16 * half + 4 * n
                        pe.matmul(T.ps[:, 4 + n, :], kt[:], ud[:, j:j + 4, :].rearrange("p j n -> p (j n)"),
                                  start=True, stop=True).then_inc(outer, 1)

            @block.scalar
            def _(act):
                act.wait_ge(spread, 1)
                act.activation(a[:], T.ps[:, 1, J:2 * J], ACT.Exp).then_inc(a_done, 1)

            @block.vector
            def _(dve):
                steps = Steps(dve, steps_s)
                sample = lambda n: qkv[:, H * n:H * n + H, PROMPT:TOK]
                grid = lambda x: x.rearrange("p (h b) -> p h b", h=H)
                dve.tensor_copy(kq[:, :, 0].rearrange("p (h b) -> p h b", h=H), sample(1)).then_inc(staged, 1)
                dve.tensor_copy(kq[:, :, 1].rearrange("p (h b) -> p h b", h=H), sample(0)).then_inc(staged, 1)
                dve.tensor_tensor(grid(prod[:]), sample(0), sample(1), ALU.mult).then_inc(staged, 1)
                dve.tensor_copy(grid(srows[:]), sample(1)).then_inc(staged, 1)
                steps.note(dve.tensor_copy(grid(vs[:]), sample(2)))
                dve.wait_ge(spread, 1)
                dve.wait_ge(a_done, 1)
                steps.done(dve.tensor_copy(beta[:], T.ps[:, 1, 0:J]))
                dve.wait_ge(sums_made, 1)
                kqs = T.ps[:, 0, 0:2 * J].rearrange("p (j c) -> p c j", c=2)
                steps.done(dve.tensor_tensor(u[:], a[:], kqs[:, 0, :], ALU.mult))
                steps.done(dve.tensor_tensor(u[:], vs[:], u[:], ALU.subtract))
                steps.done(dve.tensor_tensor(u[:], u[:], beta[:], ALU.mult))
                u_val = steps.note(dve.tensor_tensor(o[:], a[:], kqs[:, 1, :], ALU.mult))
                dve.tensor_tensor(qk[:], u[:], T.ps[:, 2, 0:J], ALU.mult).then_inc(u_done, 1)
                dve.wait_ge(u_done, 1)
                dve.wait_ge(steps_s, u_val)
                dve.tensor_tensor(T.acc[:, H:2 * H, PROMPT:TOK], grid(o[:]), grid(qk[:]), ALU.add)
                dve.wait_ge(turned, 1)
                dve.tensor_copy(kt[:], T.ps[0:J, 3, 0:P]).then_inc(ud_done, 1)
                steps.done(dve.tensor_copy(ut[:], T.ps[0:J, 3, P:2 * P]))
                dve.tensor_tensor(ud, over(ut[:], J), per_column(T.ident[0:J, 0:J], P), ALU.mult).then_inc(ud_done, 1)
                for half in range(2):
                    for n in range(16):
                        j = 16 * half + n
                        dve.wait_ge(outer, 4 * half + n // 4 + 1)
                        dve.scalar_tensor_tensor(out=st[:, j, :], in0=st[:, j, :], scalar=a[:, j:j + 1],
                                                 in1=T.ps[:, 4 + n // 4, P * (n % 4):P * (n % 4) + P],
                                                 op0=ALU.mult, op1=ALU.add).then_inc(st_new, 1)


def stage_gate_z(nc, T, proj, g_out):
    H = HEADS_B
    with ExitStack() as ctx:
        z = ctx.enter_context(nc.sbuf_tensor("gz_z", [P, H, TOK], F32))
        gain = ctx.enter_context(nc.sbuf_tensor("gz_gain", [P, 1], F32))
        z_in, zs = (nc.alloc_semaphore("gz_" + n) for n in ("z_in", "zs"))
        with nc.Block() as block:
            @block.sync
            def _(sp):
                sp.dma_start(z[:], proj.rearrange("(m p) n -> p m n", p=P)[:, 20:24, :]).then_inc(z_in, 16)
                sp.dma_start(gain[:], g_out.rearrange("(a b) -> a b", b=1)).then_inc(z_in, 16)

            @block.scalar
            def _(act):
                act.wait_ge(z_in, 32)
                act.activation(z[:], z[:], ACT.Silu).then_inc(zs, 1)
        head_norms(nc, T, "gz", [T.acc[:, H + h, :] for h in range(H)], 1.0 / P, lambda k: gain[:], lambda k: z[:, k, :])


def mixer_even(nc, T, proj, ins, outs, consts):
    with split_weights(nc, T, "gmlp"):
        stage_gmlp(nc, T, proj, ins["a_v_norm"][0], ins["a_w_s"][0], ins["a_b_s"][0],
                   outs["chunk_v"][0].rearrange("b s c -> (b s) c"))
    with ExitStack() as ctx:
        qkv = ctx.enter_context(nc.sbuf_tensor("qkv", [P, 3 * HEADS_B, TOK], F32))
        gates = ctx.enter_context(nc.sbuf_tensor("gates", [64, TOK], F32))
        stage_conv_b(nc, T, proj, qkv, gates, ins["b_conv_w"][0], ins["state_gdn_conv"][0], ins["b_a_log"][0],
                     ins["b_dt_bias"][0], consts, outs["gdn_conv_prompt"][0], outs["gdn_conv_sample"][0])
        with split_weights(nc, T, "qk_norm"):
            head_norms(nc, T, "qk", [qkv[:, m, :] for m in range(2 * HEADS_B)], 1.0,
                       lambda k: float(P) ** -0.5 if k < HEADS_B else 1.0)
        stage_delta(nc, T, qkv, gates, consts, outs["gdn_state_prompt"][0, 0])
        stage_delta_sample(nc, T, qkv, gates, consts, ins["state_gdn"][0], outs["gdn_state_sample"][0])
    with split_weights(nc, T, "gate_z"):
        stage_gate_z(nc, T, proj, ins["b_out_norm"][0])


def stage_lambda(nc, T, nlam, subln_cols, subln_rows, c_lambda, c_subln):
    with ExitStack() as ctx:
        sem = lambda n: nc.alloc_semaphore("lm_" + n)
        lq = ctx.enter_context(nc.sbuf_tensor("lm_lq", [P, 4, 64], F32))
        pr = ctx.enter_context(nc.sbuf_tensor("lm_pr", [P, 2, 64], F32))
        sm = ctx.enter_context(nc.sbuf_tensor("lm_sm", [P, 2], F32))
        par_in, own, exped = sem("par_in"), sem("own"), sem("exped")
        with nc.Block() as block:
            @block.sync
            def _(sp):
                sp.dma_start(lq[:], c_lambda.rearrange("a d -> (a d)").partition_broadcast(P)).then_inc(par_in, 16)
                sp.dma_start(subln_rows, c_subln.partition_broadcast(P)).then_inc(par_in, 16)
                sp.dma_start(subln_cols, c_subln.rearrange("(a b) -> a b", b=1)).then_inc(par_in, 16)

            @block.vector
            def _(dve):
                steps = Steps(dve, own)
                dve.wait_ge(par_in, 48)
                steps.note(dve.tensor_scalar(subln_rows, subln_rows, 1.0 - LAM_INIT, None, ALU.mult))
                steps.note(dve.tensor_scalar(subln_cols, subln_cols, 1.0 - LAM_INIT, None, ALU.mult))
                steps.done(dve.tensor_tensor(pr[:], lq[:, 0:4:2, :], lq[:, 1:4:2, :], ALU.mult))
                steps.note(dve.tensor_reduce(sm[:], pr[:], AX_X, ALU.add))
                dve.wait_ge(exped, 1)
                dve.scalar_tensor_tensor(out=nlam, in0=sm[:, 1:2], scalar=-LAM_INIT, in1=sm[:, 0:1], op0=ALU.add,
                                         op1=ALU.subtract)

            @block.scalar
            def _(act):
                act.wait_ge(own, 4)
                act.activation(sm[:], sm[:], ACT.Exp).then_inc(exped, 1)


def stage_attention(nc, T, proj, consts, nlam, subln_rows, k_out, v_out):
    H, NQ = HEADS_C, NCHUNK
    spans = [(i + 1) * P for i in range(NQ)]
    parts = [1 if s <= 512 else 2 for s in spans]
    LEAD = 4

    def ahead(h, p, i, d, more):
        n = i + d
        if n < 0 or (n >= NQ and not more):
            return None
        return (h, p, n) if n < NQ else (h + 1, 1 - p, n - NQ)

    def run_heads(eng, start, head):
        start()
        with eng.Fori(0, H // 2 - 1) as j:
            head(2 * j, 0, True)
            head(2 * j + 1, 1, True)
        head(H - 2, 0, True)
        head(H - 1, 1, False)

    with ExitStack() as ctx:
        sb = lambda n, s, d=F32: ctx.enter_context(nc.sbuf_tensor("at_" + n, s, d))
        sem = lambda n: nc.alloc_semaphore("at_" + n)
        qin, kin, vin = (sb(n, [P, PROMPT]) for n in ("qin", "kin", "vin"))
        split = lambda p, n: (T.wh, T.wl)[p][:, n * PROMPT:(n + 1) * PROMPT]
        kh, kl = [split(p, 0) for p in range(2)], [split(p, 1) for p in range(2)]
        qh = [[split(p, 2 + c) for c in range(2)] for p in range(2)]
        ql = [[split(p, 4 + c) for c in range(2)] for p in range(2)]
        vt, kt = sb("vt", [P, 2, NQ, P]), sb("kt", [P, NQ, P])
        dist = sb("dist", [P, PROMPT])
        bias = T.wraw[:, 0:2 * PROMPT].rearrange("p (r n) -> p r n", r=2)
        w = T.wraw[:, 2 * PROMPT:4 * PROMPT].rearrange("p (r n) -> p r n", r=2)
        wt = T.wraw[:, 4 * PROMPT:6 * PROMPT].rearrange("p (r t e) -> p r t e", r=2, e=P)
        slope, half = sb("slope", [P, H]), sb("half", [P, 2])
        s = sb("s", [P, 4, 2, PROMPT])
        o, junk = sb("o", [P, 2, NQ, P]), sb("junk", [P, P])
        mx, nmx, sm, rc = (sb(n, [P, 4, 2]) for n in ("mx", "nmx", "sm", "rc"))
        ms = sb("ms", [P, 2, NQ])
        con_in, half_done, seen = sem("con_in"), sem("half_done"), sem("seen")
        q_in, k_in, v_in = sem("q_in"), sem("k_in"), sem("v_in")
        q_hi, q_lo, k_hi, k_lo, bias_done = sem("q_hi"), sem("q_lo"), sem("k_hi"), sem("k_lo"), sem("bias_done")
        kv_turned, kv_taken, o_turned, o_taken = sem("kv_turned"), sem("kv_taken"), sem("o_turned"), sem("o_taken")
        v_stored, k_stored = sem("v_stored"), sem("k_stored")
        scored, maxed, negated, exped = sem("scored"), sem("maxed"), sem("negated"), sem("exped")
        inverted, coefs, w_first, weighted = sem("inverted"), sem("coefs"), sem("w_first"), sem("weighted")
        w_turned, wt_moved, av_made, o_moved, squared = (sem(n) for n in "w_turned wt_moved av_made o_moved squared".split())
        logged, rooted, normed = sem("logged"), sem("rooted"), sem("normed")
        mt = proj.rearrange("(m p) n -> m p n", p=P)
        k_rows = k_out.rearrange("(t p) (h e) -> h p t e", p=P, e=P)
        v_rows = v_out.rearrange("(t p) (h e) -> h p t e", p=P, e=P)
        scores = lambda c, i: T.ps[:, 2 * c:2 * c + parts[i], 0:spans[i] // parts[i]]
        av = T.ps[:, 6, 0:P]
        fold = lambda ap, i: ap[:, 0:spans[i]].rearrange("p (a n) -> p a n", a=parts[i])

        with nc.Block() as block:
            @block.sync
            def _(sp):
                sp.dma_start(dist[:], consts[:, C_DIST:C_DIST + PROMPT]).then_inc(con_in, 16)
                sp.dma_start(slope[:], consts[:, C_SLOPE:C_SLOPE + H]).then_inc(con_in, 16)
                sp.dma_start(half[:], consts[:, C_HALF:C_HALF + 2]).then_inc(con_in, 16)

            @block.vector
            def _(dve):
                dve.wait_ge(con_in, 48)
                dve.tensor_scalar(half[:], half[:], 64.0 ** -0.5, None, ALU.mult).then_inc(half_done, 1)

        with nc.Block() as block:
            @block.sync
            def _(sp):
                def load(h):
                    sp.wait_ge(q_lo, 2 * h)
                    sp.dma_start(qin[:], mt[bass.ds(h, 1), :, 0:PROMPT].rearrange("a p n -> p (a n)")).then_inc(q_in, 16)
                    sp.wait_ge(kv_turned, 4 * h)
                    sp.wait_ge(k_lo, h)
                    sp.dma_start(kin[:], mt[bass.ds(h + H, 1), :, 0:PROMPT].rearrange("a p n -> p (a n)")).then_inc(k_in, 16)
                    sp.dma_start(vin[:], mt[bass.ds(h + 2 * H, 1), :, 0:PROMPT].rearrange("a p n -> p (a n)")).then_inc(v_in, 16)

                def store(h, p):
                    sp.wait_ge(kv_taken, 4 * h + 2)
                    sp.dma_start(v_rows[bass.ds(h, 1), :, :, :].rearrange("a p t e -> p (a t) e"), vt[:, p]).then_inc(v_stored, 16)
                    sp.wait_ge(kv_taken, 4 * h + 4)
                    sp.dma_start(k_rows[bass.ds(h, 1), :, :, :].rearrange("a p t e -> p (a t) e"), kt[:]).then_inc(k_stored, 16)

                def head(h, p, more):
                    store(h, p)
                    if more:
                        load(h + 1)

                run_heads(sp, lambda: load(0), head)
                sp.wait_ge(v_stored, 16 * H)
                sp.wait_ge(k_stored, 16 * H)

            @block.tensor
            def _(pe):
                def turn_kv(h, n, outputs_before):
                    pe.wait_ge((v_in, v_in, k_in, k_in)[n], 16 * h + 16)
                    pe.wait_ge(kv_taken, 4 * h + n)
                    if outputs_before is not None:
                        pe.wait_ge(o_taken, outputs_before)
                    src = (vin, kin)[n // 2]
                    for j in range(4):
                        t = 4 * (n % 2) + j
                        ins = pe.transpose(T.ps[:, 7, P * j:P * j + P], src[:, P * t:P * t + P], T.ident)
                    ins.then_inc(kv_turned, 1)

                def turn_output(h, p, n, kv_before):
                    pe.wait_ge(normed, NQ * h + 4 * n + 4)
                    pe.wait_ge(o_taken, 2 * h + n)
                    pe.wait_ge(kv_taken, kv_before)
                    for j in range(4):
                        ins = pe.transpose(T.ps[:, 7, P * j:P * j + P], o[:, p, 4 * n + j, :], T.ident)
                    ins.then_inc(o_turned, 1)

                def score(h, p, i):
                    if i == 0:
                        pe.wait_ge(q_lo, 2 * h + 2)
                        pe.wait_ge(k_lo, h + 1)
                    pe.wait_ge(maxed, 2 * NQ * h + 2 * i)
                    width = spans[i] // parts[i]
                    for c in range(2):
                        for part in range(parts[i]):
                            cols = slice(part * width, (part + 1) * width)
                            for n, (a, b) in enumerate(((qh[p][c], kh[p]), (qh[p][c], kl[p]), (ql[p][c], kh[p]))):
                                ins = pe.matmul(T.ps[:, 2 * c + part, 0:width], a[:, P * i:P * i + P], b[:, cols],
                                                start=n == 0, stop=n == 2)
                        ins.then_inc(scored, 1)

                def turn_weights(h, p, i):
                    pe.wait_ge(weighted, NQ * h + i + 1)
                    pe.wait_ge(wt_moved, NQ * h + i)
                    for t in range(i + 1):
                        ins = pe.transpose(T.ps[:, 4 + t // 4, P * (t % 4):P * (t % 4) + P],
                                           w[:, i % 2, P * t:P * t + P], T.ident)
                    ins.then_inc(w_turned, 1)

                def times_values(h, p, i):
                    pe.wait_ge(wt_moved, NQ * h + i + 1)
                    pe.wait_ge(o_moved, NQ * h + i)
                    if i == 0:
                        pe.wait_ge(kv_taken, 4 * h + 2)
                    for t in range(i + 1):
                        ins = pe.matmul(av, wt[:, i % 2, t, :], vt[:, p, t, :], start=t == 0, stop=t == i)
                    ins.then_inc(av_made, 1)

                def step(h, p, i, more):
                    if i >= 0:
                        times_values(h, p, i)
                    for f, d in ((turn_weights, 1), (score, LEAD)):
                        tile = ahead(h, p, i, d, more)
                        if tile is not None:
                            f(*tile)

                def head(h, p, more):
                    for i in range(NQ):
                        step(h, p, i, more)
                        n = {0: 0, 1: 1, 4: 2, 5: 3}.get(i)
                        if more and n is not None:
                            turn_kv(h + 1, n, 2 * h if p == 0 or n >= 2 else 2 * (h - 1))
                        if p == 1 and i in (2, 3):
                            turn_output(h - 1, 0, i - 2, 4 * (h + 1) + (2 if more else 0))
                    if p == 1:
                        for n in range(2):
                            turn_output(h, 1, n, 4 * (h + 1) + (4 if more else 0))

                def start():
                    for n in range(4):
                        turn_kv(0, n, None)
                    for i in range(-LEAD, 0):
                        step(0, 0, i, True)

                run_heads(pe, start, head)

            @block.scalar
            def _(act):
                def split_q(h, p):
                    act.wait_ge(q_in, 16 * h + 16)
                    for c in range(2):
                        act.activation(qh[p][c], qin[:], ACT.Copy, scale=half[:, c:c + 1]).then_inc(q_hi, 1)

                def split_k(h, p):
                    act.wait_ge(k_in, 16 * h + 16)
                    act.activation(kh[p], kin[:], ACT.Copy).then_inc(k_hi, 1)

                def make_bias(h, p):
                    act.activation(bias[:, p, :], dist[:], ACT.Copy, scale=slope[:, bass.ds(h, 1)]).then_inc(bias_done, 1)

                def take_kv(h, p, n):
                    act.wait_ge(kv_turned, 4 * h + n + 1)
                    dst = (vt[:, p], kt)[n // 2]
                    act.activation(dst[:, 4 * (n % 2):4 * (n % 2) + 4, :], T.ps[:, 7, :].rearrange("p (t e) -> p t e", t=4),
                                   ACT.Copy).then_inc(kv_taken, 1)

                def exponentials(h, p, i):
                    act.wait_ge(negated, NQ * h + i + 1)
                    for c in range(2):
                        x = s[:, i % 4, c, 0:spans[i]]
                        act.activation(x, x, ACT.Exp, bias=nmx[:, i % 4, c:c + 1],
                                       accum_out=sm[:, i % 4, c:c + 1]).then_inc(exped, 1)

                def square(h, p, i):
                    act.wait_ge(o_moved, NQ * h + i + 1)
                    act.wait_ge(squared, NQ * h + i)
                    if i == 0:
                        act.wait_ge(normed, NQ * h if p == 0 else NQ * (h - 1))
                    act.activation(junk[:], o[:, p, i, :], ACT.Square, accum_out=ms[:, p, i:i + 1]).then_inc(squared, 1)

                def take_weights(h, p, i):
                    act.wait_ge(w_turned, NQ * h + i + 1)
                    act.wait_ge(av_made, NQ * h + max(i - 1, 0))
                    for b in range(i // 4 + 1):
                        n = min(4, i + 1 - 4 * b)
                        ins = act.activation(wt[:, i % 2, 4 * b:4 * b + n, :],
                                             T.ps[:, 4 + b, 0:P * n].rearrange("p (t e) -> p t e", t=n), ACT.Copy)
                    ins.then_inc(wt_moved, 1)

                def step(h, p, i, more):
                    tile = ahead(h, p, i, 2, more)
                    if tile is not None:
                        exponentials(*tile)
                    tile = ahead(h, p, i, 1, more)
                    if tile is not None:
                        take_weights(*tile)
                    if i >= 0:
                        square(h, p, i)

                def root(h, p):
                    act.wait_ge(squared, NQ * h + NQ)
                    act.activation(ms[:, p, :], ms[:, p, :], ACT.Ln, scale=1.0 / P, bias=T.eps[:]).then_inc(logged, 1)
                    act.wait_ge(logged, h + 1)
                    act.activation(ms[:, p, :], ms[:, p, :], ACT.Exp, scale=-0.5).then_inc(rooted, 1)

                def take_output(h, n):
                    act.wait_ge(o_turned, 2 * h + n + 1)
                    act.activation(T.acc[:, bass.ds(h, 1), 512 * n:512 * n + 512].rearrange("p a n -> p (a n)"),
                                   T.ps[:, 7, :], ACT.Copy).then_inc(o_taken, 1)

                def head(h, p, more):
                    for i in range(NQ):
                        step(h, p, i, more)
                        if more and i == 0:
                            act.wait_ge(v_stored, 16 * h)
                            act.wait_ge(scored, 2 * NQ * h)
                            split_q(h + 1, 1 - p)
                        if p == 1 and i == 0:
                            root(h - 1, 0)
                        if more and i == 1:
                            split_k(h + 1, 1 - p)
                        if more and i == 2:
                            act.wait_ge(maxed, 2 * NQ * h)
                            make_bias(h + 1, 1 - p)
                        n = {0: 0, 1: 1, 4: 2, 5: 3}.get(i)
                        if more and n is not None:
                            if n == 2:
                                act.wait_ge(k_stored, 16 * h + 16)
                            take_kv(h + 1, 1 - p, n)
                        if p == 1 and i in (2, 3):
                            take_output(h - 1, i - 2)
                    if p == 1:
                        root(h, 1)
                        for n in range(2):
                            take_output(h, n)

                def start():
                    split_q(0, 0)
                    split_k(0, 0)
                    make_bias(0, 0)
                    for n in range(4):
                        take_kv(0, 0, n)
                    for i in range(-LEAD, 0):
                        step(0, 0, i, True)

                run_heads(act, start, head)

            @block.vector
            def _(dve):
                def split_q(h, p):
                    for c in range(2):
                        dve.wait_ge(q_hi, 2 * h + c + 1)
                        dve.scalar_tensor_tensor(out=ql[p][c], in0=qin[:], scalar=half[:, c:c + 1], in1=qh[p][c],
                                                 op0=ALU.mult, op1=ALU.subtract).then_inc(q_lo, 1)

                def weigh(h, p, i):
                    dve.wait_ge(w_first, NQ * h + i + 1)
                    x = w[:, i % 2, 0:spans[i]]
                    dve.scalar_tensor_tensor(out=x, in0=s[:, i % 4, 1, 0:spans[i]], scalar=rc[:, i % 4, 1:2], in1=x,
                                             op0=ALU.mult, op1=ALU.add).then_inc(weighted, 1)

                def maxima(h, p, i):
                    if i == 0:
                        dve.wait_ge(bias_done, h + 1)
                    for c in range(2):
                        dve.wait_ge(scored, 2 * NQ * h + 2 * i + c + 1)
                        dve.sem_inc(seen, 1)
                        dve.tensor_tensor_reduce(fold(s[:, i % 4, c, :], i), scores(c, i),
                                                 fold(bias[:, p, PROMPT - spans[i]:], i), 1.0,
                                                 -3e38, ALU.add, ALU.max, mx[:, i % 4, c:c + 1]).then_inc(maxed, 1)
                    dve.wait_ge(maxed, 2 * NQ * h + 2 * i + 2)
                    dve.tensor_scalar(nmx[:, i % 4, :], mx[:, i % 4, :], -1.0, None, ALU.mult).then_inc(negated, 1)

                def coefficients(h, p, i):
                    dve.wait_ge(exped, 2 * NQ * h + 2 * i + 2)
                    dve.reciprocal(rc[:, i % 4, :], sm[:, i % 4, :]).then_inc(inverted, 1)
                    dve.wait_ge(inverted, NQ * h + i + 1)
                    dve.tensor_scalar(rc[:, i % 4, 1:2], rc[:, i % 4, 1:2], nlam, None, ALU.mult).then_inc(coefs, 1)

                def take_output(h, p, i):
                    dve.wait_ge(av_made, NQ * h + i + 1)
                    if i == 0:
                        dve.wait_ge(o_turned, 2 * h if p == 0 else 2 * (h - 1))
                    dve.tensor_copy(o[:, p, i, :], av).then_inc(o_moved, 1)

                def norm(h, p):
                    dve.wait_ge(rooted, h + 1)
                    dve.wait_ge(o_moved, NQ * h + NQ)
                    for i in range(NQ):
                        dve.scalar_tensor_tensor(out=o[:, p, i, :], in0=o[:, p, i, :], scalar=ms[:, p, i:i + 1],
                                                 in1=subln_rows, op0=ALU.mult, op1=ALU.mult).then_inc(normed, 1)

                def step(h, p, i, more):
                    for f, d in ((weigh, 1), (maxima, 3), (coefficients, 2)):
                        tile = ahead(h, p, i, d, more)
                        if tile is not None:
                            f(*tile)
                    if i >= 0:
                        take_output(h, p, i)

                def head(h, p, more):
                    for i in range(NQ):
                        step(h, p, i, more)
                        if more and i == 1:
                            split_q(h + 1, 1 - p)
                        if p == 1 and i == 1:
                            norm(h - 1, 0)
                    if p == 1:
                        norm(h, 1)

                def start():
                    split_q(0, 0)
                    for i in range(-LEAD, 0):
                        step(0, 0, i, True)

                run_heads(dve, start, head)

            @block.gpsimd
            def _(pool):
                def split_k(h, p):
                    pool.wait_ge(k_hi, h + 1)
                    pool.tensor_tensor(kl[p], kin[:], kh[p], ALU.subtract).then_inc(k_lo, 1)

                def first(h, p, i):
                    pool.wait_ge(coefs, NQ * h + i + 1)
                    pool.wait_ge(w_turned, NQ * h + (i - 1 if i else 0))
                    pool.tensor_tensor(w[:, i % 2, 0:spans[i]], s[:, i % 4, 0, 0:spans[i]],
                                       rc[:, i % 4, 0:1].to_broadcast([P, spans[i]]), ALU.mult).then_inc(w_first, 1)

                def head(h, p, more):
                    for i in range(NQ):
                        tile = ahead(h, p, i, 2, more)
                        if tile is not None:
                            first(*tile)
                        if more and i == 2:
                            split_k(h + 1, 1 - p)

                def start():
                    split_k(0, 0)
                    for i in range(2):
                        first(0, 0, i)

                run_heads(pool, start, head)


def stage_attention_sample(nc, T, proj, consts, nlam, subln_cols, cache_k, cache_v, page_table, k_out, v_out):
    H, B = HEADS_C, SAMPLES
    J = H * B
    N_POOL = cache_k.shape[0]
    with ExitStack() as ctx:
        sb = lambda n, s, d=F32: ctx.enter_context(nc.sbuf_tensor("as_" + n, s, d))
        sem = lambda n: nc.alloc_semaphore("as_" + n)
        xs = sb("xs", [P, 3 * H, B])
        xrows, qrow, qm = sb("xrows", [B, 3 * D]), sb("qrow", [B, D]), sb("qm", [B, D])
        table = sb("table", [1, B * PAGES], I32)
        page, prod, qb = sb("page", [P, 2, PAGES, D]), sb("prod", [P, PAGES, D]), sb("qb", [P, 2, D])
        sc, scp = sb("sc", [P, PAGES, B, 2 * H]), sb("scp", [P, PAGES, P])
        sbias, half, pair = sb("sbias", [P, PAST + 1]), sb("half", [P, 2]), sb("pair", [P, J])
        s, pn, pq = sb("s", [P, PAST + 1]), sb("pn", [P, 2, J]), sb("pq", [P, J])
        mx, sm, wcol = sb("mx", [P, 2]), sb("sm", [P, 2]), sb("wcol", [P, P])
        wk, wb, av, sq, rs = sb("wk", [P, PAGES, J]), sb("wb", [P, SAMPLES, PAGES, H]), sb("av", [P, H, B]), sb("sq", [P, J]), sb("rs", [P, J])
        x_in, con_in, r_turned, r_moved, out_done = (sem(n) for n in "x_in con_in r_turned r_moved out_done".split())
        qm_done, qb_made, qb_moved, reduced, reduced_v = (sem(n) for n in "qm_done qb_made qb_moved reduced reduced_v".split())
        page_in, multiplied, multiplied_v, v_in, o_made, o_moved = (
            [sem(n + "0"), sem(n + "1")] for n in "page_in multiplied multiplied_v v_in o_made o_moved".split())
        own, t_made, s_moved, exped, p_turned, wc_done, wn_made = (sem(n) for n in "own t_made s_moved exped p_turned wc_done wn_made".split())
        wb_done, own2, ss_made, rooted, act_own = (sem(n) for n in "wb_done own2 ss_made rooted act_own".split())
        ptab = sem("ptab")

        def load_page(sp, cache, dst, i, signal):
            for j in range(PAGES):
                n = sp.value_load(table[0:1, bass.ds(PAGES * i + j, 1)], min_val=0, max_val=N_POOL - 1)
                sp.dma_start(dst[:, j, :], cache[bass.ds(n, 1), :, :].rearrange("a p n -> p (a n)")).then_inc(signal, 16)

        with nc.Block() as block:
            @block.sync
            def _(sp):
                sp.dma_start(xs[:], proj.rearrange("(m p) n -> p m n", p=P)[:, 0:3 * H, PROMPT:TOK]).then_inc(x_in, 16)
                sp.dma_start(table[:], page_table.rearrange("b j -> (b j)").unsqueeze(0)).then_inc(ptab, 16)
                sp.dma_start(sbias[:], consts[:, C_SBIAS:C_SBIAS + PAST + 1]).then_inc(con_in, 16)
                sp.dma_start(half[:], consts[:, C_HALF:C_HALF + 2]).then_inc(con_in, 16)
                sp.dma_start(pair[:], consts[:, C_PAIR:C_PAIR + J]).then_inc(con_in, 16)
                sp.wait_ge(r_moved, 1)
                sp.dma_start(k_out, xrows[:, D:2 * D]).then_inc(out_done, 16)
                sp.dma_start(v_out, xrows[:, 2 * D:3 * D]).then_inc(out_done, 16)
                sp.wait_ge(out_done, 32)
                sp.wait_ge(ptab, 16)

            @block.tensor
            def _(pe):
                pe.wait_ge(x_in, 16)
                flat = T.ps[0:B, 0:6, :].rearrange("r b n -> r (b n)")
                for m in range(3 * H):
                    ins = pe.transpose(flat[:, P * m:P * m + P], xs[:, m, :], T.ident)
                ins.then_inc(r_turned, 1)

            @block.vector
            def _(dve):
                dve.wait_ge(r_turned, 1)
                dve.tensor_copy(xrows[:], T.ps[0:B, 0:6, :].rearrange("r b n -> r (b n)")).then_inc(r_moved, 1)
                dve.wait_ge(r_moved, 1)
                dve.tensor_scalar(qrow[:], xrows[:, 0:D], 64.0 ** -0.5, None, ALU.mult)
                dve.wait_ge(con_in, 48)

        with nc.Block() as block:
            @block.sync
            def _(sp):
                with sp.Fori(0, B // 2) as i:
                    for r in range(2):
                        sp.wait_ge(multiplied[r], i)
                        sp.wait_ge(multiplied_v[r], i)
                        load_page(sp, cache_k, page[:, r], 2 * i + r, page_in[r])

            @block.vector
            def _(dve):
                def mask(b):
                    dve.tensor_scalar(qm[:], qrow[:], T.ident[0:B, bass.ds(b, 1)], None, ALU.mult).then_inc(qm_done, 1)

                def add_up(j, b):
                    return dve.tensor_reduce(sc[:, j, bass.ds(b, 1), :].rearrange("p a m -> p (a m)"),
                                             prod[:, j, :].rearrange("p (m d) -> p m d", d=64), AX_X, ALU.add)

                dve.tensor_scalar(qm[:], qrow[:], T.ident[0:B, 0:1], None, ALU.mult).then_inc(qm_done, 1)
                with dve.Fori(0, B // 2) as i:
                    for r in range(2):
                        b = 2 * i + r
                        dve.wait_ge(qb_made, b + 1)
                        mask(b + 1)
                        dve.wait_ge(qb_moved, b + 1)
                        dve.wait_ge(page_in[r], 16 * PAGES * i + 16 * PAGES)
                        dve.wait_ge(reduced_v, b)
                        dve.tensor_tensor(prod[:, 1, :], page[:, r, 1, :], qb[:, r, :], ALU.mult).then_inc(multiplied_v[r], 1)
                        dve.wait_ge(multiplied_v[r], i + 1)
                        add_up(1, b).then_inc(reduced_v, 1)
                        dve.wait_ge(multiplied[r], i + 1)
                        add_up(0, b).then_inc(reduced, 1)

            @block.tensor
            def _(pe):
                with pe.Fori(0, B) as b:
                    pe.wait_ge(qm_done, b + 1)
                    pe.wait_ge(qb_moved, b)
                    for n in range(2):
                        ins = pe.matmul(T.ps[:, n, :], T.con[0:B, C_ONE:C_ONE + P], qm[:, 512 * n:512 * n + 512],
                                        start=True, stop=True)
                    ins.then_inc(qb_made, 1)

            @block.scalar
            def _(act):
                with act.Fori(0, B // 2) as i:
                    for r in range(2):
                        act.wait_ge(qb_made, 2 * i + r + 1)
                        act.wait_ge(multiplied[r], i)
                        act.wait_ge(multiplied_v[r], i)
                        act.activation(qb[:, r, :], T.ps[:, 0:2, :].rearrange("p a n -> p (a n)"), ACT.Copy
                                       ).then_inc(qb_moved, 1)

            @block.gpsimd
            def _(pool):
                with pool.Fori(0, B // 2) as i:
                    for r in range(2):
                        pool.wait_ge(page_in[r], 16 * PAGES * i + 16 * PAGES)
                        pool.wait_ge(qb_moved, 2 * i + r + 1)
                        pool.wait_ge(reduced, 2 * i + r)
                        pool.tensor_tensor(prod[:, 0, :], page[:, r, 0, :], qb[:, r, :], ALU.mult).then_inc(multiplied[r], 1)

        with nc.Block() as block:
            @block.vector
            def _(dve):
                steps = Steps(dve, own)
                q, k = xs[:, 0:H, :], xs[:, H:2 * H, :]
                for j in range(PAGES):
                    steps.note(dve.tensor_copy(scp[:, j, :].rearrange("p (c h b) -> p c h b", c=2, h=H),
                                               sc[:, j].rearrange("p b (h c) -> p c h b", c=2)))
                steps.done(dve.scalar_tensor_tensor(out=pq[:].rearrange("p (h b) -> p h b", h=H), in0=q,
                                                    scalar=64.0 ** -0.5, in1=k, op0=ALU.mult, op1=ALU.mult))
                for c in range(2):
                    steps.note(dve.tensor_scalar(pn[:, c, :], pq[:], half[:, c:c + 1], None, ALU.mult))
                dve.wait_ge(t_made, 1)
                steps.done(dve.tensor_tensor_reduce(s[:], T.ps[:, 0, 0:PAST + 1], sbias[:], 1.0, -3e38, ALU.add, ALU.max,
                                                    mx[:, 0:1]))
                dve.tensor_scalar(mx[:, 1:2], mx[:, 0:1], -1.0, None, ALU.mult).then_inc(s_moved, 1)
                dve.wait_ge(exped, 1)
                steps.done(dve.reciprocal(sm[:, 1:2], sm[:, 0:1]))
                steps.done(dve.tensor_scalar(sm[64:P, 1:2], sm[64:P, 1:2], nlam[64:P, :], None, ALU.mult))
                steps.done(dve.tensor_scalar(s[:], s[:], sm[:, 1:2], None, ALU.mult))
                dve.tensor_copy(wcol[:], s[:, PAST:PAST + 1].to_broadcast([P, P])).then_inc(wc_done, 1)
                dve.wait_ge(p_turned, 1)
                x = T.ps[:, 1, 0:PAGES * P].rearrange("p (j c n) -> p j c n", j=PAGES, c=2)
                steps.done(dve.tensor_copy(wk[:], x[:, :, 0, :]))
                dve.tensor_tensor(wk[:], wk[:], x[:, :, 1, :], ALU.add)

            @block.scalar
            def _(act):
                act.wait_ge(s_moved, 1)
                act.activation(s[:], s[:], ACT.Exp, bias=mx[:, 1:2], accum_out=sm[:, 0:1]).then_inc(exped, 1)

            @block.tensor
            def _(pe):
                pe.wait_ge(own, 5)
                for j in range(PAGES):
                    pe.transpose(T.ps[:, 0, P * j:P * j + P], scp[:, j, :], T.ident)
                pe.matmul(T.ps[:, 0, PAST:PAST + 1], pn[:].rearrange("p c n -> p (c n)"), T.con[:, C_ONE:C_ONE + 1],
                          start=True, stop=True).then_inc(t_made, 1)
                pe.wait_ge(wc_done, 1)
                for j in range(PAGES):
                    ins = pe.transpose(T.ps[:, 1, P * j:P * j + P], s[:, P * j:P * j + P], T.ident)
                ins.then_inc(p_turned, 1)
                pe.matmul(T.ps[:, 2, 0:J], wcol[:], pair[:], start=True, stop=True).then_inc(wn_made, 1)

        with nc.Block() as block:
            @block.sync
            def _(sp):
                with sp.Fori(0, B // 2) as i:
                    for r in range(2):
                        sp.wait_ge(o_made[r], i)
                        load_page(sp, cache_v, page[:, r], 2 * i + r, v_in[r])

            @block.vector
            def _(dve):
                dve.tensor_copy(wb[:], wk[:].rearrange("p j (h b) -> p b j h", b=B)).then_inc(wb_done, 1)
                with dve.Fori(0, B // 2) as i:
                    for r in range(2):
                        dve.wait_ge(o_made[r], i + 1)
                        dve.tensor_copy(av[:, :, bass.ds(2 * i + r, 1)].rearrange("p h a -> p (h a)"),
                                        T.ps[:, 3 + r, 0:H]).then_inc(o_moved[r], 1)

            @block.tensor
            def _(pe):
                pe.wait_ge(wb_done, 1)
                with pe.Fori(0, B // 2) as i:
                    for r in range(2):
                        b = 2 * i + r
                        pe.wait_ge(v_in[r], 16 * PAGES * i + 16 * PAGES)
                        pe.wait_ge(o_moved[r], i)
                        for h in range(H):
                            for j in range(PAGES):
                                ins = pe.matmul(T.ps[:, 3 + r, h:h + 1], page[:, r, j, P * h:P * h + P],
                                                wb[:, bass.ds(b, 1), j, h:h + 1].rearrange("p a n -> p (a n)"),
                                                start=j == 0, stop=j == PAGES - 1)
                        ins.then_inc(o_made[r], 1)

        with nc.Block() as block:
            @block.vector
            def _(dve):
                steps = Steps(dve, own2)
                a = av[:].rearrange("p h b -> p (h b)")
                v = xs[:, 2 * H:3 * H, :].rearrange("p h b -> p (h b)")
                steps.done(dve.tensor_tensor(sq[:], v, T.ps[:, 2, 0:J], ALU.mult))
                steps.done(dve.tensor_tensor(a, a, sq[:], ALU.add))
                steps.done(dve.tensor_tensor(sq[:], a, a, ALU.mult))
                dve.wait_ge(rooted, 1)
                steps.done(dve.tensor_tensor(sq[:], a, rs[:], ALU.mult))
                dve.tensor_scalar(T.acc[:, :, PROMPT:TOK], sq[:].rearrange("p (h b) -> p h b", h=H), subln_cols, None,
                                  ALU.mult)

            @block.tensor
            def _(pe):
                pe.wait_ge(own2, 3)
                pe.matmul(T.ps[:, 4, 0:J], T.con[:, C_ONE:C_ONE + P], sq[:], start=True, stop=True).then_inc(ss_made, 1)

            @block.scalar
            def _(act):
                steps = Steps(act, act_own)
                act.wait_ge(ss_made, 1)
                rsqrt_of(act, steps, rs[:], T.ps[:, 4, 0:J], 1.0 / P, T.eps[:]).then_inc(rooted, 1)


def mixer_odd(nc, T, proj, ins, outs, consts):
    with ExitStack() as ctx:
        nlam = ctx.enter_context(nc.sbuf_tensor("nlam", [P, 1], F32))
        cols = ctx.enter_context(nc.sbuf_tensor("subln_cols", [P, 1], F32))
        rows = ctx.enter_context(nc.sbuf_tensor("subln_rows", [P, P], F32))
        stage_lambda(nc, T, nlam[:], cols[:], rows[:], ins["c_lambda"][0], ins["c_subln"][0])
        with split_weights(nc, T, "scores"):
            stage_attention(nc, T, proj, consts, nlam[:], rows[:],
                            outs["k_prompt"][0, 0].rearrange("t h c d -> t (h c d)"),
                            outs["v_prompt"][0, 0].rearrange("t h d -> t (h d)"))
        stage_attention_sample(nc, T, proj, consts, nlam[:], cols[:],
                               ins["cache_k"][0].rearrange("n t h c d -> n t (h c d)"),
                               ins["cache_v"][0].rearrange("n t h d -> n t (h d)"), ins["page_table"],
                               outs["k_sample"][0, :, 0].rearrange("b h c d -> b (h c d)"),
                               outs["v_sample"][0, :, 0].rearrange("b h d -> b (h d)"))


def stage_output(nc, T, y_prompt, y_sample):
    with ExitStack() as ctx:
        sb = lambda n, s, d=F32: ctx.enter_context(nc.sbuf_tensor("out_" + n, s, d))
        sem = lambda n: nc.alloc_semaphore("out_" + n)
        y, ys = sb("y", [P, 2, D]), sb("ys", [SAMPLES, D])
        turned, moved, stored, s_stored = sem("turned"), sem("moved"), [sem("stored0"), sem("stored1")], sem("s_stored")
        dst = y_prompt.rearrange("b (t p) d -> (b t) p d", p=P)
        with nc.Block() as block:
            @block.tensor
            def _(pe):
                for t in range(NCHUNK):
                    if t >= 2:
                        pe.wait_ge(moved, t - 1)
                    for k in range(KD):
                        ins = pe.transpose(T.ps[:, 2 * (t % 2) + k // 4, P * (k % 4):P * (k % 4) + P],
                                           T.acc[:, k, P * t:P * t + P], T.ident)
                    ins.then_inc(turned, 1)
                for k in range(KD):
                    ins = pe.transpose(T.ps[0:SAMPLES, 4 + k // 4, P * (k % 4):P * (k % 4) + P],
                                       T.acc[:, k, PROMPT:TOK], T.ident)
                ins.then_inc(turned, 1)

            @block.vector
            def _(dve):
                for t in range(NCHUNK):
                    dve.wait_ge(turned, t + 1)
                    if t >= 2:
                        dve.wait_ge(stored[t % 2], 16 * (t // 2))
                    dve.tensor_copy(y[:, t % 2, :], T.ps[:, 2 * (t % 2):2 * (t % 2) + 2, :].rearrange("p b n -> p (b n)")
                                    ).then_inc(moved, 1)
                dve.wait_ge(turned, NCHUNK + 1)
                dve.tensor_copy(ys[:], T.ps[0:SAMPLES, 4:6, :].rearrange("p b n -> p (b n)")).then_inc(moved, 1)

            @block.sync
            def _(sp):
                for t in range(NCHUNK):
                    sp.wait_ge(moved, t + 1)
                    sp.dma_start(dst[t], y[:, t % 2, :]).then_inc(stored[t % 2], 16)
                sp.wait_ge(moved, NCHUNK + 1)
                sp.dma_start(y_sample.rearrange("b s d -> (b s) d"), ys[:]).then_inc(s_stored, 16)
                for r in range(2):
                    sp.wait_ge(stored[r], 16 * NCHUNK // 2)
                sp.wait_ge(s_stored, 16)


def trunk_step(nc, ins, outs, consts):
    x_t = nc.dram_tensor("x_scratch", [D, TOK], F32, kind="Internal").ap()
    proj0 = nc.dram_tensor("proj_even", [25 * P, TOK], F32, kind="Internal").ap()
    proj1 = nc.dram_tensor("proj_odd", [24 * P, TOK], F32, kind="Internal").ap()
    with ExitStack() as ctx:
        T = open_trunk(nc, ctx)
        with nc.cleanup_on_exit():
            stage_load_x(nc, T, ins["x_prompt"], ins["x_sample"],
                         [ins[n] for n in ("norm_mix_pre", "norm_mix_post", "norm_ffn_pre", "norm_ffn_post")], consts)
        for layer in range(2):
            with nc.cleanup_on_exit():
                with split_weights(nc, T, f"in{layer}"), split_pair(nc, T, f"mix_in{layer}"):
                    if layer == 0:
                        stage_norm(nc, T, "n0", None, 0, x_t)
                        stage_project(nc, T, "pe", ins["w_in_even"][0], 24, proj0, tail=24 * P)
                    else:
                        stage_norm(nc, T, "n3", 6, 1, x_t)
                        stage_project(nc, T, "po", ins["w_in_odd"][0], 24, proj1)
            with nc.cleanup_on_exit():
                if layer == 0:
                    mixer_even(nc, T, proj0, ins, outs, consts)
                else:
                    mixer_odd(nc, T, proj1, ins, outs, consts)
            with nc.cleanup_on_exit(), split_weights(nc, T, f"rest{layer}"):
                with split_pair(nc, T, f"mix_out{layer}"):
                    stage_split(nc, T, f"sp{layer}")
                    stage_project(nc, T, f"out{layer}", ins["w_out_even" if layer == 0 else "w_out_odd"][0], 8)
                with split_pair(nc, T, f"ffn_in{layer}"):
                    stage_norm(nc, T, f"nf{layer}", 2 + layer, 4 + layer, x_t)
                    stage_ffn(nc, T, f"ffn{layer}", layer, ins["w_ffn_gate"][layer], ins["w_ffn_up"][layer],
                              ins["w_ffn_down"][layer], ins["w_ffn_conv"][layer], ins["b_ffn_conv"][layer:layer + 1],
                              ins["state_ffn_conv"], outs["ffn_conv_prompt"], outs["ffn_conv_sample"])
        with split_weights(nc, T, "last"):
            stage_norm(nc, T, "n6", 7, None, x_t, want_h=False)
        stage_output(nc, T, outs["y_prompt"], outs["y_sample"])


_INS = ["x_prompt", "x_sample", "cache_k", "cache_v", "page_table", "state_gdn", "state_gdn_conv", "state_ffn_conv",
        "norm_mix_pre", "norm_mix_post", "norm_ffn_pre", "norm_ffn_post", "w_in_even", "a_v_norm", "a_w_s", "a_b_s",
        "b_conv_w", "b_a_log", "b_dt_bias", "b_out_norm", "w_out_even", "w_in_odd", "c_lambda", "c_subln",
        "w_out_odd", "w_ffn_gate", "w_ffn_up", "w_ffn_conv", "b_ffn_conv", "w_ffn_down"]
_OUTS = [("y_prompt", (1, PROMPT, D)), ("y_sample", (SAMPLES, 1, D)),
         ("gdn_state_prompt", (1, 1, HEADS_B, P, P)), ("gdn_state_sample", (1, SAMPLES, HEADS_B, P, P)),
         ("gdn_conv_prompt", (1, 1, 3, 12 * P)), ("gdn_conv_sample", (1, SAMPLES, 3, 12 * P)),
         ("chunk_v", (1, SAMPLES, 1, 4 * P)),
         ("k_prompt", (1, 1, PROMPT, HEADS_C, 2, 64)), ("v_prompt", (1, 1, PROMPT, HEADS_C, P)),
         ("k_sample", (1, SAMPLES, 1, HEADS_C, 2, 64)), ("v_sample", (1, SAMPLES, 1, HEADS_C, P)),
         ("ffn_conv_prompt", (2, 1, 2, FF)), ("ffn_conv_sample", (2, SAMPLES, 2, FF))]


def kernel(**inputs):
    import concourse.bacc as _bacc
    from concourse.bass_utils import run_bass_kernel_spmd as _run

    nc = _bacc.Bacc("TRN2", target_bir_lowering=False, num_devices=1)
    arrays, ins, outs = {}, {}, {}
    for name in _INS:
        a = np.ascontiguousarray(inputs[name])
        arrays[f"in_{name}"] = a
        ins[name] = nc.dram_tensor(f"in_{name}", a.shape, mybir.dt.from_np(a.dtype), kind="ExternalInput").ap()
    arrays["in_constants"] = shape_constants()
    consts = nc.dram_tensor("in_constants", [P, C_END], F32, kind="ExternalInput").ap()
    for name, shape in _OUTS:
        outs[name] = nc.dram_tensor(f"out_{name}", shape, F32, kind="ExternalOutput").ap()
    trunk_step(nc, ins, outs, consts)
    r = _run(nc, [arrays], core_ids=[0])
    return tuple(r.results[0][f"out_{name}"] for name, _ in _OUTS)
```

```python
import math
from contextlib import ExitStack

import numpy as np

import concourse.bass as bass
from concourse import mybir

ALU = mybir.AluOpType
ACT = mybir.ActivationFunctionType
F32 = mybir.dt.float32
F32R = mybir.dt.float32r
I32 = mybir.dt.int32
AX_X = mybir.AxisListType.X

P = 128
D = 1024
KD = D // P
PROMPT = 1024
SAMPLES = 8
TOK = PROMPT + SAMPLES
CH = TOK // 3
NCHUNK = PROMPT // P
FF = 2816
FT = FF // P
GROUPS = FT // 2
HEADS_B = 4
HEADS_C = 8
EPS = 1e-6
MASKED = -1e30
PAGES = 2
PAST = PAGES * P
LAM_INIT = 0.8 - 0.6 * math.exp(-0.3)

C_ID, C_INCL, C_STRICT, C_ONE = 0, 128, 256, 384
C_LEVEL = 512
C_SEL = C_LEVEL + 7 * 128
C_RESET = C_SEL + 8 * 128
C_DIST = C_RESET + PROMPT
C_SLOPE = C_DIST + PROMPT
C_SBIAS = C_SLOPE + HEADS_C
C_PAIR = C_SBIAS + PAST + 1
C_HALF = C_PAIR + 64
C_END = C_HALF + 2


def shape_constants():
    c = np.zeros((P, C_END), np.float32)
    i = np.arange(P)
    c[:, C_ID:C_ID + P] = np.eye(P)
    c[:, C_INCL:C_INCL + P] = i[:, None] <= i[None, :]
    c[:, C_STRICT:C_STRICT + P] = i[:, None] < i[None, :]
    c[:, C_ONE:C_ONE + P] = 1.0
    for n, s in enumerate((1, 2, 4, 8, 16, 32, 64)):
        col, row = i[:, None] // s, i[None, :] // s
        c[:, C_LEVEL + n * P:C_LEVEL + (n + 1) * P] = (row % 2 == 1) & (col == row - 1)
    for n in range(8):
        c[n if n < 4 else 32 + n - 4, C_SEL + n * P:C_SEL + (n + 1) * P] = 1.0
    c[:, C_RESET:C_RESET + PROMPT] = np.arange(PROMPT) % P != 0
    dist = (np.arange(PROMPT) - (PROMPT - P))[None, :] - i[:, None]
    c[:, C_DIST:C_DIST + PROMPT] = np.where(dist <= 0, dist, MASKED)
    slopes = np.exp2(-8.0 * np.arange(1, HEADS_C + 1, dtype=np.float32) / HEADS_C).astype(np.float32)
    c[:, C_SLOPE:C_SLOPE + HEADS_C] = slopes
    head = (i // SAMPLES) % HEADS_C
    c[:, C_SBIAS:C_SBIAS + PAST + 1] = slopes[head][:, None] * (np.arange(PAST + 1) - PAST)[None, :]
    c[:, C_PAIR:C_PAIR + 64] = (i % 64)[:, None] == np.arange(64)[None, :]
    c[:64, C_HALF] = 1.0
    c[64:, C_HALF + 1] = 1.0
    return c


class Steps:

    def __init__(self, eng, sem, base=0):
        self.eng, self.sem, self.base, self.n = eng, sem, base, 0

    def note(self, ins):
        ins.then_inc(self.sem, 1)
        self.n += 1
        return self.base + self.n

    def done(self, ins):
        self.eng.wait_ge(self.sem, self.note(ins))


class Trunk:
    pass


def one(t, i):
    if isinstance(i, int):
        return t[:, i, :]
    return t[:, bass.ds(i, 1), :].rearrange("p a w -> p (a w)")


def region(ps, r):
    return ps[:, 3 * r:3 * r + 3, 0:CH]


def chunks(ap):
    return ap.rearrange("p (c n) -> p c n", c=3)


def product(pe, ps, r, wh, wl, hh, hl, first, last):
    for n, (w, h) in enumerate(((wh, hh), (wh, hl), (wl, hh))):
        for c in range(3):
            ins = pe.matmul(ps[:, 3 * r + c, 0:CH], w, h[:, c * CH:(c + 1) * CH],
                            start=first and n == 0, stop=last and n == 2)
    return ins


def ones_times(pe, T, r, src, first=True, last=True):
    for c in range(3):
        ins = pe.matmul(T.ps[:, 3 * r + c, 0:CH], T.con[:, C_ONE:C_ONE + P], src[:, c * CH:(c + 1) * CH],
                        start=first, stop=last)
    return ins


def rsqrt_of(act, steps, out, sums, scale, eps_col):
    steps.done(act.activation(out, sums, ACT.Ln, scale=scale, bias=eps_col))
    return act.activation(out, out, ACT.Exp, scale=-0.5)


class TileSquares:

    def __init__(self, sem, T, bufs):
        self.T, self.bufs = T, bufs
        self.squared, self.summed = [sem("squared0"), sem("squared1")], [sem("summed0"), sem("summed1")]

    def scalar(self, act, m, n, r):
        act.wait_ge(self.summed[r], n)
        act.activation(self.bufs[r], one(self.T.acc, m), ACT.Square).then_inc(self.squared[r], 1)

    def gpsimd(self, pool, n, r, own):
        pool.wait_ge(self.squared[r], n + 1)
        own()
        pool.tensor_tensor(self.T.sqsum[:], self.T.sqsum[:], self.bufs[r], ALU.add).then_inc(self.summed[r], 1)


def stage_load_x(nc, T, x_prompt, x_sample, gains, consts):
    with ExitStack() as ctx:
        sb = lambda n, s, d=F32: ctx.enter_context(nc.sbuf_tensor("ld_" + n, s, d))
        sem = lambda n: nc.alloc_semaphore("ld_" + n)
        xin, xs, grow = sb("xin", [P, 2, D]), sb("xs", [SAMPLES, D]), sb("grow", [8, D])
        const_in, small_in, landed = sem("const_in"), sem("small_in"), [sem("landed0"), sem("landed1")]
        turned, moved = [sem("turned0"), sem("turned1")], [sem("moved0"), sem("moved1")]
        small_turned, prepared = sem("small_turned"), sem("prepared")
        src = x_prompt.rearrange("b (t p) d -> (b t) p d", p=P)
        with nc.Block() as block:
            @block.sync
            def _(sp):
                sp.dma_start(T.con[:], consts[:, 0:512]).then_inc(const_in, 16)
                with sp.Fori(0, NCHUNK // 2) as i:
                    for r in range(2):
                        sp.wait_ge(turned[r], i)
                        sp.dma_start(xin[:, r, :], src[bass.ds(2 * i + r, 1), :, :].rearrange("a p d -> p (a d)")
                                     ).then_inc(landed[r], 16)
                sp.dma_start(xs[:], x_sample.rearrange("b s d -> (b s) d")).then_inc(small_in, 16)
                for n, g in enumerate(gains):
                    sp.dma_start(grow[2 * n:2 * n + 2, :], g).then_inc(small_in, 16)

            @block.tensor
            def _(pe):
                pe.wait_ge(const_in, 16)
                with pe.Fori(0, NCHUNK // 2) as i:
                    for r in range(2):
                        pe.wait_ge(landed[r], 16 * i + 16)
                        pe.wait_ge(moved[r], i)
                        for k in range(KD):
                            ins = pe.transpose(T.ps[:, 2 * r + k // 4, P * (k % 4):P * (k % 4) + P],
                                               xin[:, r, P * k:P * k + P], T.ident)
                        ins.then_inc(turned[r], 1)
                pe.wait_ge(small_in, 16 * (1 + len(gains)))
                for k in range(KD):
                    pe.transpose(T.ps[:, 6, 8 * k:8 * k + 8], xs[:, P * k:P * k + P], T.ident[0:8, 0:8])
                for k in range(KD):
                    ins = pe.transpose(T.ps[:, 7, 8 * k:8 * k + 8], grow[:, P * k:P * k + P], T.ident[0:8, 0:8])
                ins.then_inc(small_turned, 1)

            @block.vector
            def _(dve):
                with dve.Fori(0, NCHUNK // 2) as i:
                    for r in range(2):
                        dve.wait_ge(turned[r], i + 1)
                        dve.tensor_copy(T.acc[:, :, bass.ds((2 * i + r) * P, P)],
                                        T.ps[:, 2 * r:2 * r + 2, :].rearrange("p b (k n) -> p (b k) n", n=P)
                                        ).then_inc(moved[r], 1)
                dve.wait_ge(small_turned, 1)
                dve.tensor_copy(T.acc[:, :, PROMPT:TOK], T.ps[:, 6, 0:64].rearrange("p (k n) -> p k n", n=8))
                dve.tensor_copy(T.gain[:], T.ps[:, 7, 0:64].rearrange("p (k n) -> p k n", n=8))
                dve.wait_ge(const_in, 16)
                dve.memset(T.one[:], 1.0)
                dve.memset(T.eps[:], EPS).then_inc(prepared, 1)


class StageInput:

    def __init__(self, nc, T, name, gain_row=None):
        sem = lambda n: nc.alloc_semaphore(name + n)
        self.T, self.gain_row, self.bufs = T, gain_row, None
        self.scaled, self.hi_done = sem("scaled"), sem("hi_done")
        self.lo_done = [sem("lo_done0"), sem("lo_done1")]

    def source(self, k):
        return self.T.acc[:, k, :] if self.gain_row is None else self.bufs[k % 2]

    def scalar(self, act, k):
        if self.gain_row is not None:
            act.wait_ge(self.scaled, k + 1)
        act.activation(self.T.hh[:, k, :], self.source(k), ACT.Copy).then_inc(self.hi_done, 1)

    def lo_half(self, eng, k):
        eng.wait_ge(self.hi_done, k + 1)
        eng.tensor_tensor(self.T.hl[:, k, :], self.source(k), self.T.hh[:, k, :], ALU.subtract
                          ).then_inc(self.lo_done[k % 2], 1)

    def scale(self, dve, k):
        if k >= 2:
            dve.wait_ge(self.lo_done[k % 2], k // 2)
        dve.scalar_tensor_tensor(out=self.bufs[k % 2], in0=self.T.acc[:, k, :],
                                 scalar=self.T.gain[:, k, self.gain_row:self.gain_row + 1], in1=self.T.sqsum[:],
                                 op0=ALU.mult, op1=ALU.mult).then_inc(self.scaled, 1)

    def vector(self, dve):
        if self.gain_row is None:
            for k in range(KD):
                self.lo_half(dve, k)
        else:
            self.scale(dve, 0)
            for k in range(1, KD, 2):
                self.scale(dve, k)
                if k + 1 < KD:
                    self.scale(dve, k + 1)
                self.lo_half(dve, k)

    def gpsimd(self, pool):
        for k in range(0, KD if self.gain_row is not None else 0, 2):
            self.lo_half(pool, k)

    def ready(self, pe, k):
        pe.wait_ge(self.lo_done[k % 2], k // 2 + 1)


def stage_norm(nc, T, name, post_row, x_scratch, feed=None):
    with ExitStack() as ctx:
        sb = lambda n, s, d=F32: ctx.enter_context(nc.sbuf_tensor(name + n, s, d))
        sem = lambda n: nc.alloc_semaphore(name + n)
        post, want_h = post_row is not None, feed is not None
        sq, xold, rstd = sb("sq", [P, 2, TOK]), sb("xold", [P, 2, TOK]), sb("rstd", [P, TOK])
        root1, act_own = sem("root1"), sem("act_own")
        summed1, squared, summed2 = sem("summed1"), sem("squared"), sem("summed2")
        x_in = [sem("x_in0"), sem("x_in1")]
        x_new, x_out, dve_own = sem("x_new"), sem("x_out"), sem("dve_own")
        xs = x_scratch.rearrange("(k p) n -> k p n", p=P)
        with nc.Block() as block:
            @block.sync
            def _(sp):
                for k in range(KD if post else 0):
                    if k >= 2:
                        sp.wait_ge(x_new, k - 1)
                    sp.dma_start(xold[:, k % 2, :], xs[k]).then_inc(x_in[k % 2], 16)
                    if k == 1 and want_h:
                        feed.first_sync(sp)
                if want_h:
                    if not post:
                        feed.first_sync(sp)
                    for k in range(KD):
                        if post:
                            sp.wait_ge(x_new, k + 1)
                        sp.dma_start(xs[k], T.acc[:, k, :]).then_inc(x_out, 16)
                    sp.wait_ge(x_out, 16 * KD)

            @block.scalar
            def _(act):
                steps = Steps(act, act_own)
                if post:
                    act.wait_ge(summed1, 1)
                    rsqrt_of(act, steps, chunks(rstd[:]), region(T.ps, 0), 1.0 / D, T.eps[:]).then_inc(root1, 1)
                if not want_h:
                    return
                for k in range(KD):
                    if k >= KD - feed.SLOTS:
                        feed.hi_half(act, k - (KD - feed.SLOTS), 0)
                    if post:
                        act.wait_ge(x_new, k + 1)
                    if k >= 2:
                        act.wait_ge(summed2, k - 1)
                    act.activation(sq[:, k % 2, :], T.acc[:, k, :], ACT.Square).then_inc(squared, 1)
                act.wait_ge(summed2, KD)
                rsqrt_of(act, steps, chunks(T.sqsum[:]), region(T.ps, 1), 1.0 / D, T.eps[:])

            @block.vector
            def _(dve):
                steps = Steps(dve, dve_own)

                if post:
                    dve.wait_ge(root1, 1)
                    for k in range(KD):
                        steps.done(dve.tensor_tensor(T.acc[:, k, :], T.acc[:, k, :], rstd[:], ALU.mult))
                        dve.wait_ge(x_in[k % 2], 16 * (k // 2 + 1))
                        dve.scalar_tensor_tensor(out=T.acc[:, k, :], in0=T.acc[:, k, :],
                                                 scalar=T.gain[:, k, post_row:post_row + 1],
                                                 in1=xold[:, k % 2, :], op0=ALU.mult, op1=ALU.add).then_inc(x_new, 1)

            @block.gpsimd
            def _(pool):
                if want_h:
                    feed.first_gpsimd(pool)

            @block.tensor
            def _(pe):
                if post:
                    ones_times(pe, T, 0, T.sqsum[:]).then_inc(summed1, 1)
                for k in range(KD if want_h else 0):
                    pe.wait_ge(squared, k + 1)
                    ones_times(pe, T, 1, sq[:, k % 2, :], k == 0, k == KD - 1).then_inc(summed2, 1)


class WeightFeed:
    SLOTS = 4

    def __init__(self, nc, T, name, matrices, column, buf, half):
        sem = lambda n: nc.alloc_semaphore(name + n)
        self.landed = [sem(f"landed{b}") for b in range(2)]
        self.hi, self.lo, self.made = ([sem(f"{n}{j}") for j in range(self.SLOTS)] for n in ("hi", "lo", "made"))
        self.raw = [T.wraw[:, 2048 * b:2048 * b + 2048].rearrange("p (k n) -> p k n", k=KD) for b in range(2)]
        self.slot_h, self.slot_l = ([t[:, 1024 * j:1024 * j + 1024].rearrange("p (k n) -> p k n", k=KD)
                                     for j in range(self.SLOTS)] for t in (T.wh, T.wl))
        self.w = [m.rearrange("(k p) m -> p k m", p=P) for m in matrices]
        self.column, self.buf, self.half = column, buf, half
        self.users = [[j for j in range(self.SLOTS) if buf(j) == b] for b in range(2)]

    def source(self, j):
        return self.raw[self.buf(j)][:, :, P * self.half(j):P * self.half(j) + P]

    def load(self, sp, i):
        for b in range(2):
            for j in self.users[b]:
                sp.wait_ge(self.lo[j], i)
            sp.dma_start(self.raw[b], self.w[b][:, :, bass.ds(self.column(b, i), 256)]).then_inc(self.landed[b], 16)

    def hi_half(self, act, j, i):
        act.wait_ge(self.landed[self.buf(j)], 16 * i + 16)
        act.wait_ge(self.made[j], i)
        act.activation(self.slot_h[j], self.source(j), ACT.Copy).then_inc(self.hi[j], 1)

    def lo_half(self, pool, j, i):
        pool.wait_ge(self.hi[j], i + 1)
        pool.tensor_tensor(self.slot_l[j], self.source(j), self.slot_h[j], ALU.subtract).then_inc(self.lo[j], 1)

    def first_sync(self, sp):
        self.load(sp, 0)

    def first_scalar(self, act):
        for j in range(self.SLOTS):
            self.hi_half(act, j, 0)

    def first_gpsimd(self, pool):
        for j in range(self.SLOTS):
            self.lo_half(pool, j, 0)


def projection_feed(nc, T, name, w):
    return WeightFeed(nc, T, name, (w, w), lambda b, i: (2 * i + b) * 256, lambda j: j // 2, lambda j: j % 2)


class QkvConv:
    TAPS, ROWS, KEEP = 4, 3 * SAMPLES + 4, 3 + SAMPLES
    FIRST, LAST = 2, 5

    def __init__(self, w_conv, state, out_prompt, out_sample):
        self.w_conv, self.state, self.out_prompt, self.out_sample = w_conv, state, out_prompt, out_sample


def stage_project(nc, T, name, source, feed, m_tiles, out_scratch=None, tail=None, conv=None):
    BODY = 4
    n_iter = m_tiles // BODY
    c0, c1 = (conv.FIRST, conv.LAST) if conv is not None else (n_iter, n_iter)
    PAD = 3
    with ExitStack() as ctx:
        sb = lambda n, s, d=F32: ctx.enter_context(nc.sbuf_tensor(name + n, s, d))
        sem = lambda n: nc.alloc_semaphore(name + n)
        out = sb("out", [P, 2, PAD + TOK])
        squares = TileSquares(sem, T, [out[:, r, PAD:] for r in range(2)]) if out_scratch is None else None
        source.bufs = [out[:, r, PAD:] for r in range(2)]
        fed = source.gain_row is not None
        sqsum_own = sem("sqsum_own")
        landed, hi, lo, made = feed.landed, feed.hi, feed.lo, feed.made
        raw, slot_h, slot_l = feed.raw, feed.slot_h, feed.slot_l
        moved = [sem(f"moved{j}") for j in range(BODY)]
        stored = [sem(f"stored{j}") for j in range(BODY)]
        t_in, t_zero = sem("t_in"), sem("t_zero")
        traw = T.wraw[:, 4096:4096 + 1024].rearrange("p (k n) -> p k n", k=KD)
        if out_scratch is not None:
            rows = out_scratch.rearrange("(m p) n -> m p n", p=P)
        if conv is not None:
            M, ROWS, KEEP, TAPS = 3 * HEADS_B, conv.ROWS, conv.KEEP, conv.TAPS
            cv = sb("cv", [P, 2, TOK])
            prm, last = sb("prm", [P, M, ROWS]), sb("last", [P, M, KEEP])
            small_rows = cv[0:ROWS, :, :].rearrange("p a n -> p (a n)")[:, 0:M * P]
            kept_rows = T.wraw[0:KEEP, 0:M * P]
            rows_in, turned, conv_own = sem("rows_in"), sem("turned"), sem("conv_own")
            conved, silued, kept = sem("conved"), sem("silued"), sem("kept")
            k_turned, k_moved, k_out = sem("k_turned"), sem("k_moved"), sem("k_out")
            flat = T.ps[0:KEEP, 3:6, :].rearrange("r b n -> r (b n)")

        def iterations(eng, body, lag):
            for a, b in ((0, c0), (c0, c1), (c1, n_iter)):
                b = min(b, n_iter - lag)
                if b > a:
                    with eng.Fori(a + lag, b + lag) as i:
                        body(i, conv is not None and a == c0, conv is not None and a == c1)

        with nc.Block() as block:
            @block.sync
            def _(sp):
                def store(j, i, convolved):
                    if out_scratch is not None:
                        if convolved:
                            sp.wait_ge(silued, BODY * (i - c0) + j + 1)
                            src = cv[:, j % 2, :]
                        else:
                            sp.wait_ge(moved[j], i + 1)
                            src = out[:, j % 2, PAD:]
                        sp.dma_start(rows[bass.ds(BODY * i + j, 1), :, :].rearrange("a p n -> p (a n)"), src
                                     ).then_inc(stored[j], 16)

                def iteration(i, convolved, after):
                    feed.load(sp, i)
                    for j in range(BODY):
                        store(j, i - 1, convolved)

                if not fed:
                    feed.first_sync(sp)
                if conv is not None:
                    n = (TAPS - 1) * SAMPLES
                    sp.dma_start(small_rows[0:n, :], conv.state.rearrange("b j c -> (b j) c")).then_inc(rows_in, 16)
                    sp.dma_start(small_rows[n:ROWS, :], conv.w_conv).then_inc(rows_in, 16)
                iterations(sp, iteration, 1)
                if tail is not None:
                    sp.wait_ge(t_zero, 1)
                    sp.dma_start(traw[:, :, 0:4], feed.w[0][:, :, tail:tail + 4]).then_inc(t_in, 16)
                    sp.dma_start(traw[:, :, 32:36], feed.w[0][:, :, tail + 4:tail + 8]).then_inc(t_in, 16)
                for j in range(BODY):
                    store(j, n_iter - 1, False)
                if tail is not None:
                    store(0, n_iter, False)
                if conv is not None:
                    sp.dma_start(conv.out_sample[:, 0:TAPS - 2, :], conv.state[:, 1:TAPS - 1, :]).then_inc(k_out, 16)
                    sp.wait_ge(k_moved, 1)
                    sp.dma_start(conv.out_prompt[0], kept_rows[0:TAPS - 1, :]).then_inc(k_out, 16)
                    sp.dma_start(conv.out_sample[:, TAPS - 2, :], kept_rows[TAPS - 1:KEEP, :]).then_inc(k_out, 16)
                    sp.wait_ge(k_out, 48)
                if out_scratch is not None:
                    for j in range(BODY):
                        sp.wait_ge(stored[j], 16 * (n_iter + (tail is not None and j == 0)))

            @block.gpsimd
            def _(pool):
                def add(j, i):
                    squares.gpsimd(pool, 2 * i + j // 2, j % 2, lambda: pool.wait_ge(sqsum_own, BODY * i + j + 1))
                    pool.wait_ge(squares.summed[j % 2], 2 * i + j // 2 + 1)
                    pool.sem_inc(sqsum_own, 1)

                def keep(j, i):
                    pool.wait_ge(moved[j], i + 1)
                    pool.tensor_copy(last[:, bass.ds(BODY * (i - c0) + j, 1), :].rearrange("p a n -> p (a n)"),
                                     out[:, j % 2, PROMPT:PAD + TOK]).then_inc(kept, 1)

                def iteration(i, convolved, after):
                    for j in range(BODY):
                        feed.lo_half(pool, j, i)
                        if squares is not None:
                            add(j, i - 1)
                        if convolved:
                            keep(j, i - 1)

                if not fed:
                    feed.first_gpsimd(pool)
                source.gpsimd(pool)
                if tail is not None:
                    pool.memset(traw, 0.0).then_inc(t_zero, 1)
                if squares is not None:
                    pool.memset(T.sqsum[:], 0.0).then_inc(sqsum_own, 1)
                iterations(pool, iteration, 1)
                if squares is not None:
                    for j in range(BODY):
                        add(j, n_iter - 1)
                if tail is not None:
                    pool.wait_ge(hi[0], n_iter + 1)
                    pool.tensor_tensor(slot_l[0], traw, slot_h[0], ALU.subtract).then_inc(lo[0], 1)

            @block.scalar
            def _(act):
                def square(j, i):
                    act.wait_ge(moved[j], i + 1)
                    squares.scalar(act, BODY * i + j, 2 * i + j // 2, j % 2)

                def iteration(i, convolved, after):
                    for j in range(BODY):
                        feed.hi_half(act, j, i)
                        if squares is not None:
                            square(j, i - 1)
                        if convolved:
                            act.wait_ge(conved, BODY * (i - 1 - c0) + j + 1)
                            act.activation(cv[:, j % 2, :], cv[:, j % 2, :], ACT.Silu).then_inc(silued, 1)

                for k in range(KD):
                    source.scalar(act, k)
                    if not fed and k >= KD - feed.SLOTS:
                        feed.hi_half(act, k - (KD - feed.SLOTS), 0)
                iterations(act, iteration, 1)
                if squares is not None:
                    for j in range(BODY):
                        square(j, n_iter - 1)
                if tail is not None:
                    act.wait_ge(t_in, 32)
                    act.wait_ge(made[0], n_iter)
                    act.activation(slot_h[0], traw, ACT.Copy).then_inc(hi[0], 1)

            @block.tensor
            def _(pe):
                def tile(j, i):
                    pe.wait_ge(lo[j], i + 1)
                    if j >= 2:
                        pe.wait_ge(moved[j - 2], i + 1)
                    else:
                        pe.wait_ge(moved[j + 2], i)
                    for k in range(KD):
                        if j == 0:
                            source.ready(pe, k)
                        ins = product(pe, T.ps, j % 2, slot_h[j][:, k, :], slot_l[j][:, k, :],
                                      T.hh[:, k, :], T.hl[:, k, :], k == 0, k == KD - 1)
                    ins.then_inc(made[j], 1)

                if conv is not None:
                    pe.wait_ge(rows_in, 32)
                    for t in range(M):
                        ins = pe.transpose(T.ps[:, 6, ROWS * t:ROWS * t + ROWS], small_rows[:, P * t:P * t + P],
                                           T.ident[0:ROWS, 0:ROWS])
                    ins.then_inc(turned, 1)
                with pe.Fori(0, n_iter) as i:
                    for j in range(BODY):
                        tile(j, i)
                if tail is not None:
                    tile(0, n_iter)
                if conv is not None:
                    pe.wait_ge(kept, M)
                    pe.wait_ge(moved[3], n_iter)
                    for t in range(M):
                        ins = pe.transpose(flat[:, P * t:P * t + P], last[:, t, :], T.ident)
                    ins.then_inc(k_turned, 1)

            @block.vector
            def _(dve):
                def move(j, i):
                    dve.wait_ge(made[j], i + 1)
                    if out_scratch is None:
                        dst = one(T.acc, BODY * i + j)
                    else:
                        dst = out[:, j % 2, PAD:]
                        if j >= 2:
                            dve.wait_ge(stored[j - 2], 16 * i + 16)
                        else:
                            dve.wait_ge(stored[j + 2], 16 * i)
                    dve.tensor_copy(chunks(dst), region(T.ps, j % 2)).then_inc(moved[j], 1)

                def convolve(steps, j, i):
                    m = BODY * (i - c0) + j
                    tap = [prm[:, bass.ds(m, 1), ROWS - TAPS + n:ROWS - TAPS + n + 1].rearrange("p a n -> p (a n)")
                           for n in range(TAPS)]
                    st = [prm[:, bass.ds(m, 1), n:ROWS - TAPS:TAPS - 1].rearrange("p a b -> p (a b)")
                          for n in range(TAPS - 1)]
                    pv, sv = cv[:, j % 2, 0:PROMPT], cv[:, j % 2, PROMPT:TOK]
                    dve.wait_ge(moved[j], i + 1)
                    steps.note(dve.tensor_scalar(pv, out[:, j % 2, 0:PROMPT], tap[0], None, ALU.mult))
                    steps.done(dve.tensor_scalar(sv, st[0], tap[0], None, ALU.mult))
                    for n in range(1, TAPS - 1):
                        steps.note(dve.scalar_tensor_tensor(out=pv, in0=out[:, j % 2, n:n + PROMPT], scalar=tap[n],
                                                            in1=pv, op0=ALU.mult, op1=ALU.add))
                        steps.done(dve.scalar_tensor_tensor(out=sv, in0=st[n], scalar=tap[n], in1=sv,
                                                            op0=ALU.mult, op1=ALU.add))
                    dve.scalar_tensor_tensor(out=cv[:, j % 2, :], in0=out[:, j % 2, PAD:], scalar=tap[TAPS - 1],
                                             in1=cv[:, j % 2, :], op0=ALU.mult, op1=ALU.add).then_inc(conved, 1)

                def iteration(i, convolving, after):
                    steps = Steps(dve, conv_own, 24 * (i - c0)) if convolving else None
                    for j in range(BODY):
                        if convolving:
                            dve.wait_ge(kept, BODY * (i - c0) + max(j - 1, 0))
                        elif after:
                            dve.wait_ge(kept, M)
                        move(j, i)
                        if convolving:
                            convolve(steps, j, i)

                source.vector(dve)
                dve.wait_ge(source.lo_done[0], KD // 2)
                if conv is not None:
                    dve.memset(out[:, :, 0:PAD], 0.0)
                    dve.wait_ge(turned, 1)
                    dve.tensor_copy(prm[:], T.ps[:, 6, 0:M * ROWS].rearrange("p (t r) -> p t r", r=ROWS))
                iterations(dve, iteration, 0)
                if tail is not None:
                    move(0, n_iter)
                if conv is not None:
                    dve.wait_ge(k_turned, 1)
                    dve.tensor_copy(kept_rows, flat[:, 0:M * P]).then_inc(k_moved, 1)


def ffn_feed(nc, T, name, w_gate, w_up):
    return WeightFeed(nc, T, name, (w_gate, w_up), lambda b, g: 256 * g, lambda j: j % 2, lambda j: j // 2)


def stage_ffn(nc, T, name, source, feed, layer, w_down, w_conv, b_conv, state, out_prompt, out_sample):
    ROWS = 2 * SAMPLES + 4
    with ExitStack() as ctx:
        sb = lambda n, s, d=F32: ctx.enter_context(nc.sbuf_tensor(name + n, s, d))
        sem = lambda n: nc.alloc_semaphore(name + n)
        raw_d = T.wraw[:, 4096:6144]
        slot_h, slot_l, lo, made = feed.slot_h, feed.slot_l, feed.lo, feed.made
        down_h, down_l = T.wh[:, 4096:6144], T.wl[:, 4096:6144]
        prm = sb("prm", [P, FT, ROWS])
        last = sb("last", [P, FT, 2 + SAMPLES])
        ah, al = sb("ah", [P, 2, TOK], F32R), sb("al", [P, 2, TOK], F32R)
        gate, conv = sb("gate", [P, 2 + TOK]), sb("conv", [P, TOK])
        rows_in, turned, prm_done = sem("rows_in"), sem("turned"), sem("prm_done")
        in_d = sem("in_d")
        hi_d, lo_d, made_d = sem("hi_d"), sem("lo_d"), sem("made_d")
        gate_in, conved, activated = sem("gate_in"), sem("conved"), sem("activated")
        multiplied, collected, acc_zero = sem("multiplied"), sem("collected"), sem("acc_zero")
        kept, a_ready, dve_own = sem("kept"), sem("a_ready"), sem("dve_own")
        out_done, keep_turned, keep_moved = sem("out_done"), sem("keep_turned"), sem("keep_moved")
        squares, sqsum_own = TileSquares(sem, T, [gate[:, 2:2 + TOK], conv[:]]), sem("sqsum_own")
        wd = w_down.rearrange("(g j p) m -> g p j m", p=P, j=2)
        KEEP = 2 + SAMPLES
        flat, kept_rows = T.ps[0:KEEP, 0:6, :].rearrange("r b n -> r (b n)"), T.wraw[0:KEEP, 0:FF]
        source.bufs = [gate[:, 2:2 + TOK], conv[:]]
        rows = ((slice(0, 2048), raw_d[0:ROWS, :]), (slice(2048, FF), sb("more_rows", [ROWS, FF - 2048])[:]))

        with nc.Block() as block:
            @block.sync
            def _(sp):
                def load_d(g):
                    sp.wait_ge(lo_d, g)
                    sp.dma_start(raw_d.rearrange("p (j m) -> p j m", j=2),
                                 wd[bass.ds(g, 1), :, :, :].rearrange("a p j m -> p (a j) m")).then_inc(in_d, 16)

                for cols, dst in rows:
                    for first, src in ((0, state[layer].rearrange("b j c -> (b j) c")), (2 * SAMPLES, w_conv),
                                       (2 * SAMPLES + 3, b_conv)):
                        sp.dma_start(dst[first:first + src.shape[0], :], src[:, cols]).then_inc(rows_in, 16)
                sp.dma_start(out_sample[layer, :, 0, :], state[layer, :, 1, :]).then_inc(out_done, 16)
                sp.wait_ge(turned, 1)
                with sp.Fori(0, GROUPS - 1) as g:
                    load_d(g)
                    feed.load(sp, g + 1)
                load_d(GROUPS - 1)
                sp.wait_ge(keep_moved, 1)
                sp.dma_start(out_prompt[layer, 0], kept_rows[0:2, :]).then_inc(out_done, 16)
                sp.dma_start(out_sample[layer, :, 1, :], kept_rows[2:KEEP, :]).then_inc(out_done, 16)
                sp.wait_ge(out_done, 48)

            @block.scalar
            def _(act):
                def split(s, g):
                    feed.hi_half(act, s, g)

                def tile(t, g):
                    act.wait_ge(made[2 * t], g + 1)
                    act.wait_ge(kept, 2 * g + t)
                    act.wait_ge(conved, 2 * g + t)
                    act.activation(chunks(gate[:, 2:2 + TOK]), region(T.ps, 0), ACT.Copy).then_inc(gate_in, 1)

                def gelu(t, g):
                    act.wait_ge(conved, 2 * g + t + 1)
                    act.activation(conv[:], conv[:], ACT.Gelu_apprx_tanh,
                                   bias=prm[:, bass.ds(2 * g + t, 1), ROWS - 1:ROWS].rearrange("p a n -> p (a n)")
                                   ).then_inc(activated, 1)

                def split_down(g):
                    act.wait_ge(in_d, 16 * g + 16)
                    act.wait_ge(made_d, KD * g)
                    act.activation(down_h, raw_d, ACT.Copy).then_inc(hi_d, 1)

                def group(g, more):
                    tile(0, g)
                    if more:
                        split(0, g + 1)
                    gelu(0, g)
                    if more:
                        split(1, g + 1)
                    split_down(g)
                    tile(1, g)
                    if more:
                        split(2, g + 1)
                    gelu(1, g)
                    if more:
                        split(3, g + 1)

                for k in range(KD):
                    source.scalar(act, k)
                with act.Fori(0, GROUPS - 1) as g:
                    group(g, True)
                group(GROUPS - 1, False)
                act.wait_ge(kept, 2 * GROUPS)
                act.wait_ge(a_ready, 2 * GROUPS)
                for m in range(KD):
                    act.wait_ge(collected, KD * (GROUPS - 1) + m + 1)
                    squares.scalar(act, m, m // 2, m % 2)

            @block.gpsimd
            def _(pool):
                def split(s, g):
                    feed.lo_half(pool, s, g)

                def keep(t, g):
                    pool.wait_ge(gate_in, 2 * g + t + 1)
                    pool.tensor_copy(last[:, bass.ds(2 * g + t, 1), :].rearrange("p a n -> p (a n)"),
                                     gate[:, PROMPT:2 + TOK]).then_inc(kept, 1)

                def group(g, more):
                    keep(0, g)
                    if more:
                        split(0, g + 1)
                        split(1, g + 1)
                    pool.wait_ge(hi_d, g + 1)
                    pool.tensor_tensor(down_l, raw_d, down_h, ALU.subtract).then_inc(lo_d, 1)
                    keep(1, g)
                    if more:
                        split(2, g + 1)
                        split(3, g + 1)

                source.gpsimd(pool)
                pool.wait_ge(source.scaled, KD)
                pool.memset(T.acc[:], 0.0).then_inc(acc_zero, 1)
                with pool.Fori(0, GROUPS - 1) as g:
                    group(g, True)
                group(GROUPS - 1, False)
                pool.memset(T.sqsum[:], 0.0).then_inc(sqsum_own, 1)
                for m in range(KD):
                    squares.gpsimd(pool, m // 2, m % 2, lambda: pool.wait_ge(
                        *((squares.summed[(m - 1) % 2], (m + 1) // 2) if m else (sqsum_own, 1))))

            @block.tensor
            def _(pe):
                def hidden(s, g):
                    pe.wait_ge(lo[s], g + 1)
                    for k in range(KD):
                        if s == 0 and isinstance(g, int) and g == 0:
                            source.ready(pe, k)
                        ins = product(pe, T.ps, s % 2, slot_h[s][:, k, :], slot_l[s][:, k, :],
                                      T.hh[:, k, :], T.hl[:, k, :], k == 0, k == KD - 1)
                    ins.then_inc(made[s], 1)

                def tile0(g):
                    pe.wait_ge(gate_in, 2 * g)
                    hidden(0, g)
                    pe.wait_ge(multiplied, 2 * g)
                    hidden(1, g)

                def down(g, taken):
                    pe.wait_ge(lo_d, g + 1)
                    pe.wait_ge(a_ready, 2 * g + 2)
                    for m in range(KD):
                        if m >= 2:
                            pe.wait_ge(collected, KD * g + m - 1)
                        for j in range(2):
                            cols = slice(1024 * j + P * m, 1024 * j + P * m + P)
                            ins = product(pe, T.ps, m % 2, down_h[:, cols], down_l[:, cols], ah[:, j, :], al[:, j, :],
                                          j == 0, j == 1)
                        ins.then_inc(made_d, 1)
                        if m == 0:
                            pe.wait_ge(multiplied, taken)

                pe.wait_ge(rows_in, 16 * 6)
                for t in range(FT):
                    ins = pe.transpose(T.ps[:, 6, ROWS * t:ROWS * t + ROWS],
                                       rows[t // 16][1][:, P * (t % 16):P * (t % 16) + P], T.ident[0:ROWS, 0:ROWS])
                ins.then_inc(turned, 1)
                tile0(0)
                pe.wait_ge(gate_in, 1)
                hidden(2, 0)
                pe.wait_ge(multiplied, 1)
                hidden(3, 0)
                with pe.Fori(1, GROUPS) as g:
                    tile0(g)
                    pe.wait_ge(gate_in, 2 * g + 1)
                    down(g - 1, 2 * g + 1)
                    pe.wait_ge(collected, KD * g - 1)
                    hidden(2, g)
                    pe.wait_ge(collected, KD * g)
                    hidden(3, g)
                pe.wait_ge(gate_in, 2 * GROUPS)
                down(GROUPS - 1, 2 * GROUPS)
                pe.wait_ge(collected, KD * GROUPS)
                pe.wait_ge(kept, 2 * GROUPS)
                for t in range(FT):
                    ins = pe.transpose(flat[:, P * t:P * t + P], last[:, t, :], T.ident)
                ins.then_inc(keep_turned, 1)

            @block.vector
            def _(dve):
                def tap(g, t, r):
                    return prm[:, bass.ds(2 * g + t, 1), r:r + 1].rearrange("p a n -> p (a n)")

                def convolve(steps, t, g):
                    dve.wait_ge(gate_in, 2 * g + t + 1)
                    pv, sv = conv[:, 0:PROMPT], conv[:, PROMPT:TOK]
                    st = [prm[:, bass.ds(2 * g + t, 1), j:2 * SAMPLES:2].rearrange("p a b -> p (a b)") for j in range(2)]
                    first, second, third = (tap(g, t, 2 * SAMPLES + j) for j in range(3))
                    steps.note(dve.tensor_scalar(pv, gate[:, 0:PROMPT], first, None, ALU.mult))
                    steps.done(dve.tensor_scalar(sv, st[0], first, None, ALU.mult))
                    steps.note(dve.scalar_tensor_tensor(out=pv, in0=gate[:, 1:1 + PROMPT], scalar=second, in1=pv,
                                                        op0=ALU.mult, op1=ALU.add))
                    steps.done(dve.scalar_tensor_tensor(out=sv, in0=st[1], scalar=second, in1=sv,
                                                        op0=ALU.mult, op1=ALU.add))
                    dve.scalar_tensor_tensor(out=conv[:], in0=gate[:, 2:2 + TOK], scalar=third, in1=conv[:],
                                             op0=ALU.mult, op1=ALU.add).then_inc(conved, 1)

                def multiply(t, g):
                    dve.wait_ge(activated, 2 * g + t + 1)
                    dve.wait_ge(made[2 * t + 1], g + 1)
                    dve.tensor_tensor(chunks(conv[:]), chunks(conv[:]), region(T.ps, 1), ALU.mult).then_inc(multiplied, 1)

                def split(steps, t, g):
                    dve.wait_ge(multiplied, 2 * g + t + 1)
                    steps.done(dve.tensor_copy(ah[:, t, :], conv[:]))
                    dve.tensor_tensor(al[:, t, :], conv[:], ah[:, t, :], ALU.subtract).then_inc(a_ready, 1)
                    dve.wait_ge(a_ready, 2 * g + t + 1)

                def collect(g):
                    for m in range(KD):
                        dve.wait_ge(made_d, KD * g + m + 1)
                        a = chunks(T.acc[:, m, :])
                        dve.tensor_tensor(a, a, region(T.ps, m % 2), ALU.add).then_inc(collected, 1)
                    dve.wait_ge(collected, KD * g + KD)

                def group(g, with_down):
                    steps = Steps(dve, dve_own, 10 * g)
                    convolve(steps, 0, g)
                    multiply(0, g)
                    if with_down:
                        collect(g - 1)
                    split(steps, 0, g)
                    convolve(steps, 1, g)
                    multiply(1, g)
                    split(steps, 1, g)
                    assert steps.n == 10

                source.vector(dve)
                dve.wait_ge(source.lo_done[0], KD // 2)
                dve.memset(gate[:, 0:2], 0.0)
                dve.wait_ge(turned, 1)
                dve.tensor_copy(prm[:], T.ps[:, 6, 0:FT * ROWS].rearrange("p (t r) -> p t r", r=ROWS)).then_inc(prm_done, 1)
                dve.wait_ge(prm_done, 1)
                group(0, False)
                dve.wait_ge(acc_zero, 1)
                with dve.Fori(1, GROUPS) as g:
                    group(g, True)
                collect(GROUPS - 1)
                dve.wait_ge(keep_turned, 1)
                dve.tensor_copy(kept_rows, flat[:, 0:FF]).then_inc(keep_moved, 1)


def open_trunk(nc, ctx):
    T = Trunk()
    sb = lambda n, s, d=F32: ctx.enter_context(nc.sbuf_tensor(n, s, d))
    T.ps = ctx.enter_context(nc.psum_tensor("ps", [P, 8, 512], F32))
    T.wraw = sb("wraw", [P, 6144])
    T.con, T.eps = sb("con_sb", [P, 512]), sb("eps", [P, 1])
    T.ident = T.con[:, C_ID:C_ID + P]
    T.one = sb("one", [P, 1])
    T.gain = sb("gain", [P, KD, 8])
    T.acc = sb("acc", [P, KD, TOK])
    T.sqsum = sb("sqsum", [P, TOK])
    return T


class split_weights:

    def __init__(self, nc, T, name):
        self.ctx, self.nc, self.T, self.name = ExitStack(), nc, T, name

    def __enter__(self):
        self.T.wh = self.ctx.enter_context(self.nc.sbuf_tensor(self.name + "wh", [P, 6144], F32R))
        self.T.wl = self.ctx.enter_context(self.nc.sbuf_tensor(self.name + "wl", [P, 6144], F32R))

    def __exit__(self, *exc):
        return self.ctx.__exit__(*exc)


class split_pair:

    def __init__(self, nc, T, name):
        self.ctx, self.nc, self.T, self.name = ExitStack(), nc, T, name

    def __enter__(self):
        self.T.hh = self.ctx.enter_context(self.nc.sbuf_tensor(self.name + "hi", [P, KD, TOK], F32R))
        self.T.hl = self.ctx.enter_context(self.nc.sbuf_tensor(self.name + "lo", [P, KD, TOK], F32R))

    def __exit__(self, *exc):
        return self.ctx.__exit__(*exc)


def over(ap, n):
    return ap.unsqueeze(1).to_broadcast([ap.shape[0], n, ap.shape[-1]])


def per_column(ap, w):
    return ap.unsqueeze(2).to_broadcast([ap.shape[0], ap.shape[1], w])


def stage_gmlp(nc, T, proj, qkv, v_gain, w_s, b_s, chunk_v):
    G = 4
    with ExitStack() as ctx:
        sb = lambda n, s, d=F32: ctx.enter_context(nc.sbuf_tensor("ga_" + n, s, d))
        sem = lambda n: nc.alloc_semaphore("ga_" + n)
        u, v, rstd = sb("u", [P, G, TOK]), sb("v", [P, G, TOK]), sb("rstd", [P, TOK])
        vt, mixed = sb("vt", [P, 2, G, P]), sb("mixed", [P, 2, G, P])
        wn, wt, bias = sb("wn", [P, G, P]), sb("wt", [P, G, P]), sb("bias", [P, G, P])
        w00, gain, incl = sb("w00", [P, G]), sb("gain", [P, G]), T.con[:, C_INCL:C_INCL + P]
        sm, cv = sb("sm", [P, G, SAMPLES]), sb("cv", [SAMPLES, G * P])
        sq = T.wraw[:, 0:G * TOK].rearrange("p (a n) -> p a n", a=G)
        squared, summed, qkv_in = sem("squared"), sem("summed"), sem("qkv_in")
        v_in, u_in, par_in, out_done = sem("v_in"), sem("u_in"), sem("par_in"), sem("out_done")
        v_act, u_act, rstd_done, act_own = sem("v_act"), sem("u_act"), sem("rstd_done"), sem("act_own")
        normed, w_turned, w_masked = sem("normed"), sem("w_turned"), sem("w_masked")
        turned, vt_moved, mixed_made, mix_moved = sem("turned"), sem("vt_moved"), sem("mixed_made"), sem("mix_moved")
        cv_turned, cv_moved, dve_own = sem("cv_turned"), sem("cv_moved"), sem("dve_own")
        rows = proj.rearrange("(m p) n -> p m n", p=P)
        with nc.Block() as block:
            @block.sync
            def _(sp):
                sp.dma_start(v[:], rows[:, G:2 * G, :]).then_inc(v_in, 16)
                sp.dma_start(u[:], rows[:, 0:G, :]).then_inc(u_in, 16)
                sp.dma_start(wn[:], w_s.rearrange("g t s -> t g s")).then_inc(par_in, 16)
                sp.dma_start(bias[:], b_s.rearrange("g t -> (g t)").partition_broadcast(P)).then_inc(par_in, 16)
                sp.dma_start(w00[:], w_s[:, 0, 0].partition_broadcast(P), allow_slow_non_contiguous=True).then_inc(par_in, 16)
                sp.dma_start(gain[:], v_gain.rearrange("(g p) -> p g", p=P), allow_slow_non_contiguous=True).then_inc(par_in, 16)
                sp.dma_start(qkv[:], rows[:, 2 * G:5 * G, :]).then_inc(qkv_in, 16)
                sp.wait_ge(qkv_in, 16)
                sp.wait_ge(cv_moved, 1)
                sp.dma_start(chunk_v, cv[:]).then_inc(out_done, 16)
                sp.wait_ge(out_done, 16)

            @block.scalar
            def _(act):
                steps = Steps(act, act_own)
                act.wait_ge(v_in, 16)
                for g in range(G):
                    act.activation(v[:, g, :], v[:, g, :], ACT.Gelu_apprx_tanh).then_inc(v_act, 1)
                act.wait_ge(v_act, G)
                act.wait_ge(u_in, 16)
                act.activation(u[:], u[:], ACT.Gelu_apprx_tanh).then_inc(u_act, 1)
                for g in range(G):
                    act.activation(sq[:, g, :], v[:, g, :], ACT.Square).then_inc(squared, 1)
                act.wait_ge(summed, G)
                rsqrt_of(act, steps, chunks(rstd[:]), region(T.ps, 0), 1.0 / (G * P), T.eps[:]).then_inc(rstd_done, 1)
                for c in range(NCHUNK):
                    act.wait_ge(turned, c + 1)
                    if c >= 2:
                        act.wait_ge(mixed_made, c - 1)
                    act.activation(vt[:, c % 2], T.ps[:, 6 + c % 2, :].rearrange("p (g n) -> p g n", g=G),
                                   ACT.Copy).then_inc(vt_moved, 1)

            @block.tensor
            def _(pe):
                pe.wait_ge(par_in, 64)
                for g in range(G):
                    ins = pe.transpose(T.ps[:, 3, P * g:P * g + P], wn[:, g, :], T.ident)
                ins.then_inc(w_turned, 1)
                for g in range(G):
                    pe.wait_ge(squared, g + 1)
                    ones_times(pe, T, 0, sq[:, g, :], g == 0, g == G - 1).then_inc(summed, 1)
                pe.wait_ge(normed, G)
                pe.wait_ge(w_masked, 1)
                for g in range(G):
                    ins = pe.transpose(T.ps[0:SAMPLES, 3, P * g:P * g + P], v[:, g, PROMPT:TOK], T.ident)
                ins.then_inc(cv_turned, 1)

                def turn(c):
                    if c >= 2:
                        pe.wait_ge(vt_moved, c - 1)
                    for g in range(G):
                        ins = pe.transpose(T.ps[:, 6 + c % 2, P * g:P * g + P], v[:, g, P * c:P * c + P], T.ident)
                    ins.then_inc(turned, 1)

                turn(0)
                for c in range(NCHUNK):
                    if c + 1 < NCHUNK:
                        turn(c + 1)
                    pe.wait_ge(vt_moved, c + 1)
                    if c >= 2:
                        pe.wait_ge(mix_moved, c - 1)
                    for g in range(G):
                        ins = pe.matmul(T.ps[:, 4 + c % 2, P * g:P * g + P], vt[:, c % 2, g, :], wt[:, g, :],
                                        start=True, stop=True)
                    ins.then_inc(mixed_made, 1)

            @block.vector
            def _(dve):
                steps = Steps(dve, dve_own)
                dve.wait_ge(w_turned, 1)
                dve.tensor_tensor(wt[:], T.ps[:, 3, :].rearrange("p (g n) -> p g n", g=G), over(incl, G),
                                  ALU.mult).then_inc(w_masked, 1)
                dve.wait_ge(rstd_done, 1)
                for g in range(G):
                    dve.scalar_tensor_tensor(out=v[:, g, :], in0=v[:, g, :], scalar=gain[:, g:g + 1], in1=rstd[:],
                                             op0=ALU.mult, op1=ALU.mult).then_inc(normed, 1)
                dve.wait_ge(normed, G)
                dve.wait_ge(u_act, 1)
                for g in range(G):
                    steps.note(dve.tensor_scalar(sm[:, g, :], v[:, g, PROMPT:TOK], w00[:, g:g + 1], bias[:, g, 0:1],
                                                 ALU.mult, ALU.add))
                steps.eng.wait_ge(steps.sem, steps.n)
                dve.tensor_tensor(T.acc[:, 0:G, PROMPT:TOK], sm[:], u[:, :, PROMPT:TOK], ALU.mult)
                dve.wait_ge(cv_turned, 1)
                dve.tensor_copy(cv[:], T.ps[0:SAMPLES, 3, :]).then_inc(cv_moved, 1)
                for c in range(NCHUNK):
                    dve.wait_ge(mixed_made, c + 1)
                    if c >= 2:
                        dve.wait_ge(dve_own, steps.n - 1)
                    dve.tensor_tensor(mixed[:, c % 2], T.ps[:, 4 + c % 2, :].rearrange("p (g n) -> p g n", g=G),
                                      bias[:], ALU.add).then_inc(mix_moved, 1)
                    dve.wait_ge(mix_moved, c + 1)
                    steps.note(dve.tensor_tensor(T.acc[:, 0:G, P * c:P * c + P], mixed[:, c % 2],
                                                 u[:, :, P * c:P * c + P], ALU.mult))


def head_norms(nc, T, name, tiles, scale, factor, after=None):
    n = len(tiles)
    with ExitStack() as ctx:
        sb = lambda s_, s, d=F32: ctx.enter_context(nc.sbuf_tensor(name + s_, s, d))
        sem = lambda s_: nc.alloc_semaphore(name + s_)
        rstd = sb("rstd", [P, 4, TOK])
        sq = T.wraw[:, 0:4 * TOK].rearrange("p (a n) -> p a n", a=4)
        squared, summed, logged, rooted, scaled = (sem(s_) for s_ in "squared summed logged rooted scaled".split())
        with nc.Block() as block:
            @block.scalar
            def _(act):
                for k in range(0, n, 2):
                    for j in (k, k + 1):
                        act.wait_ge(summed, j + 1)
                        if j >= 4:
                            act.wait_ge(scaled, j - 3)
                        act.activation(chunks(rstd[:, j % 4, :]), region(T.ps, j % 2), ACT.Ln, scale=scale, bias=T.eps[:]
                                       ).then_inc(logged, 1)
                    for j in (k, k + 1):
                        act.wait_ge(logged, j + 1)
                        act.activation(rstd[:, j % 4, :], rstd[:, j % 4, :], ACT.Exp, scale=-0.5).then_inc(rooted, 1)

            @block.vector
            def _(dve):
                def square(k):
                    if k >= 4:
                        dve.wait_ge(summed, k - 3)
                    dve.tensor_tensor(sq[:, k % 4, :], tiles[k], tiles[k], ALU.mult).then_inc(squared, 1)

                for k in range(min(4, n)):
                    square(k)
                for k in range(n):
                    if k + 4 < n:
                        square(k + 4)
                    dve.wait_ge(rooted, k + 1)
                    dve.wait_ge(squared, k + 1)
                    dve.scalar_tensor_tensor(out=tiles[k], in0=tiles[k], scalar=factor(k), in1=rstd[:, k % 4, :],
                                             op0=ALU.mult, op1=ALU.mult).then_inc(scaled, 1)
                    if after is not None:
                        dve.wait_ge(scaled, k + 1)
                        dve.tensor_tensor(tiles[k], tiles[k], after(k), ALU.mult)

            @block.tensor
            def _(pe):
                for k in range(n):
                    pe.wait_ge(squared, k + 1)
                    if k >= 2:
                        pe.wait_ge(logged, k - 1)
                    ones_times(pe, T, k % 2, sq[:, k % 4, :]).then_inc(summed, 1)


def stage_gates(nc, T, proj, gates, a_log, dt_bias, consts):
    with ExitStack() as ctx:
        sb = lambda n, s, d=F32: ctx.enter_context(nc.sbuf_tensor("cb_" + n, s, d))
        sem = lambda n: nc.alloc_semaphore("cb_" + n)
        reset = sb("reset", [P, PROMPT])
        x, t1, t2 = (sb(n, [P, TOK]) for n in ("x", "t1", "t2"))
        col = sb("col", [P, 3])
        hr = slice(32, 32 + HEADS_B)
        gates_in, dve_own, act_own, g1, g2 = sem("gates_in"), sem("dve_own"), sem("act_own"), sem("g1"), sem("g2")
        with nc.Block() as block:
            @block.sync
            def _(sp):
                sp.dma_start(gates[:], proj.rearrange("(m p) n -> m p n", p=P)[24, 0:64, :]).then_inc(gates_in, 16)
                sp.dma_start(col[hr, 0:1], a_log.rearrange("(a b) -> a b", b=1)).then_inc(gates_in, 16)
                sp.dma_start(col[hr, 1:2], dt_bias.rearrange("(a b) -> a b", b=1)).then_inc(gates_in, 16)
                sp.dma_start(reset[:], consts[:, C_RESET:C_RESET + PROMPT]).then_inc(gates_in, 16)

            @block.scalar
            def _(act):
                steps = Steps(act, act_own)
                act.wait_ge(gates_in, 64)
                act.activation(gates[0:HEADS_B, :], gates[0:HEADS_B, :], ACT.Sigmoid)
                act.wait_ge(g1, 1)
                steps.done(act.activation(t1[hr, :], t1[hr, :], ACT.Exp, scale=-1.0))
                steps.note(act.activation(t1[hr, :], t1[hr, :], ACT.Ln, bias=T.one[hr, :]))
                act.activation(col[hr, 2:3], col[hr, 0:1], ACT.Exp).then_inc(g2, 1)
                act.wait_ge(act_own, steps.n)

            @block.vector
            def _(dve):
                steps = Steps(dve, dve_own)
                dve.wait_ge(gates_in, 64)
                steps.done(dve.tensor_scalar(x[hr, :], gates[hr, :], col[hr, 1:2], None, ALU.add))
                steps.done(dve.tensor_scalar(t1[hr, :], x[hr, :], -1.0, None, ALU.mult))
                dve.tensor_tensor(t1[hr, :], t1[hr, :], x[hr, :], ALU.max).then_inc(g1, 1)
                dve.wait_ge(g2, 1)
                dve.wait_ge(act_own, 2)
                steps.done(dve.scalar_tensor_tensor(out=t2[hr, :], in0=x[hr, :], scalar=0.0, in1=t1[hr, :],
                                                    op0=ALU.max, op1=ALU.add))
                steps.done(dve.tensor_scalar(gates[hr, :], t2[hr, :], col[hr, 2:3], -1.0, ALU.mult, ALU.mult))
                steps.done(dve.tensor_tensor_scan(x[hr, 0:PROMPT], reset[hr, :], gates[hr, 0:PROMPT], 0.0,
                                                  ALU.mult, ALU.add))
                dve.tensor_copy(gates[hr, 0:PROMPT], x[hr, 0:PROMPT])


def stage_delta(nc, T, qkv, gates, consts, state_out):
    H = HEADS_B
    LV = 7
    UP = 2 * LV - 3
    with ExitStack() as ctx:
        sb = lambda n, s, d=F32: ctx.enter_context(nc.sbuf_tensor("gd_" + n, s, d))
        sem = lambda n: nc.alloc_semaphore("gd_" + n)
        both = lambda n: [sem(n + "0"), sem(n + "1")]
        masks, sel, cap = sb("masks", [P, LV, P]), sb("sel", [64, 8, P]), sb("cap", [P, P])
        tiles, rows = sb("tiles", [P, 2, 3 * H, P]), sb("rows", [64, 2, P])
        col, eg_col, beg, wend = (sb(n, [P, 2, w]) for n, w in (("col", 64), ("eg_col", H), ("beg", H), ("wend", H)))
        names = "eg dm pt lt qe t tt p1 w2 u kbe vb kw first".split()
        eg, dm, pt, lt, qe, t, tt, p1, w2, u, kbe, vb, kw, first = (sb(n, [P, 2, H, P]) for n in names)
        state = sb("state", [P, H, P])
        am = T.wraw[:].rearrange("p (x l h n) -> p x l h n", x=2, l=LV - 1, h=H)
        bank = [[T.ps[:, 4 * x + n, :].rearrange("p (h n) -> p h n", h=H) for n in range(4)] for x in range(2)]
        heads = range(H)
        K = lambda x, h: tiles[:, x, H + h, :]
        Q = lambda x, h: tiles[:, x, h, :]
        V = lambda x, h: tiles[:, x, 2 * H + h, :]
        con_in, cap_done, out_done = sem("con_in"), sem("cap_done"), sem("out_done")
        staged, spread, v_turned, k_turned = both("staged"), both("spread"), both("v_turned"), both("k_turned")
        col_copied, diffed, decayed, beg_done = both("col_copied"), both("diffed"), both("decayed"), both("beg_done")
        beta_used, kk_made, kq_made, lt_done, pt_done = (both(n) for n in "beta_used kk_made kq_made lt_done pt_done".split())
        masked, qe_done, scaled, tt_first, t_turned = (both(n) for n in "masked qe_done scaled tt_first t_turned".split())
        t_first, p1_made, p1_moved, merged, updated = (both(n) for n in "t_first p1_made p1_moved merged updated".split())
        w2_made, w2_moved, u_made, u_moved, o_made, o_moved, s_made, s_updated = (
            both(n) for n in "w2_made w2_moved u_made u_moved o_made o_moved s_made s_updated".split())

        def run_pairs(eng, body):
            with eng.Fori(0, NCHUNK // 2 - 1) as i:
                body(i, True)
            body(NCHUNK // 2 - 1, False)

        with nc.Block() as block:
            @block.sync
            def _(sp):
                sp.dma_start(masks[:], consts[:, C_LEVEL:C_LEVEL + LV * P].rearrange("p (l n) -> p l n", l=LV)
                             ).then_inc(con_in, 16)
                sp.dma_start(sel[:], consts[0:64, C_SEL:C_SEL + 8 * P].rearrange("p (l n) -> p l n", l=8)
                             ).then_inc(con_in, 16)

            @block.vector
            def _(dve):
                dve.memset(state[:], 0.0)
                dve.tensor_scalar(cap[:], T.con[:, C_INCL:C_INCL + P], -MASKED, MASKED, ALU.mult, ALU.add
                                  ).then_inc(cap_done, 1)
                dve.wait_ge(con_in, 32)

        with nc.Block() as block:
            @block.tensor
            def _(pe):
                def spread_gates(x, i):
                    pe.wait_ge(staged[x], 2 * i + 2)
                    pe.wait_ge(o_moved[x], i)
                    pe.wait_ge(u_moved[x], i)
                    pe.wait_ge(w2_moved[x], i)
                    pe.wait_ge(s_updated[x], H * i)
                    for n in range(8):
                        pe.matmul(bank[x][n // H][:, n % H, :], sel[:, n, :], rows[:, x, :], start=True, stop=True)
                    pe.transpose(T.ps[:, 4 * x + 2, 0:64], rows[:, x, :], T.ident[0:64, 0:64]).then_inc(spread[x], 1)
                    for h in heads:
                        ins = pe.transpose(bank[x][3][:, h, :], K(x, h), T.ident)
                    ins.then_inc(k_turned[x], 1)

                def products(x, i):
                    pe.wait_ge(col_copied[x], i + 1)
                    for h in heads:
                        ins = pe.transpose(bank[x][2][:, h, :], V(x, h), T.ident)
                    ins.then_inc(v_turned[x], 1)
                    pe.wait_ge(decayed[x], 4 * i + 4)
                    for h in heads:
                        ins = pe.matmul(bank[x][1][:, h, :], K(x, h), K(x, h), start=True, stop=True)
                    ins.then_inc(kk_made[x], 1)
                    pe.wait_ge(beta_used[x], i + 1)
                    for h in heads:
                        ins = pe.matmul(bank[x][0][:, h, :], K(x, h), Q(x, h), start=True, stop=True)
                    ins.then_inc(kq_made[x], 1)

                def turn_first(x, i):
                    pe.wait_ge(tt_first[x], i + 1)
                    for h in heads:
                        ins = pe.transpose(bank[x][1][:, h, :], tt[:, x, h, :], T.ident)
                    ins.then_inc(t_turned[x], 1)

                def off_block(x, i, l):
                    if l == 1:
                        pe.wait_ge(t_first[x], i + 1)
                    else:
                        pe.wait_ge(updated[x], UP * i + 2 * (l - 1))
                    pe.wait_ge(masked[x], LV * i + l + 1)
                    for h in heads:
                        ins = pe.matmul(bank[x][1][:, h, :], am[:, x, l - 1, h, :], t[:, x, h, :], start=True, stop=True)
                    ins.then_inc(p1_made[x], 1)

                def merge(x, i, l):
                    pe.wait_ge(p1_moved[x], (LV - 1) * i + l)
                    if l == 1:
                        pe.wait_ge(pt_done[x], i + 1)
                        pe.wait_ge(scaled[x], 3 * i + 3)
                    if l < LV - 1:
                        for h in heads:
                            ins = pe.matmul(bank[x][0][:, h, :], tt[:, x, h, :], p1[:, x, h, :], start=True, stop=True)
                        ins.then_inc(merged[x], 1)
                    for h in heads:
                        ins = pe.matmul(bank[x][2][:, h, :], p1[:, x, h, :], tt[:, x, h, :], start=True, stop=True)
                    ins.then_inc(merged[x], 1)

                def keys(x, i):
                    pe.wait_ge(updated[x], UP * i + UP)
                    for h in heads:
                        ins = pe.matmul(bank[x][3][:, h, :], kbe[:, x, h, :], tt[:, x, h, :], start=True, stop=True)
                    ins.then_inc(w2_made[x], 1)

                def recur(x, i):
                    pe.wait_ge(w2_moved[x], i + 1)
                    pe.wait_ge(s_updated[1 - x], H * i + (H if x else 0))
                    for h in heads:
                        pe.matmul(bank[x][1][:, h, :], tt[:, x, h, :], vb[:, x, h, :], start=True, stop=False)
                        ins = pe.matmul(bank[x][1][:, h, :], w2[:, x, h, :], state[:, h, :], start=False, stop=True)
                    ins.then_inc(u_made[x], 1)
                    pe.wait_ge(u_moved[x], i + 1)
                    for h in heads:
                        ins = pe.matmul(bank[x][2][:, h, :], kw[:, x, h, :], u[:, x, h, :], start=True, stop=True)
                    ins.then_inc(s_made[x], 1)
                    pe.wait_ge(qe_done[x], i + 1)
                    for h in heads:
                        pe.matmul(bank[x][0][:, h, :], state[:, h, :], qe[:, x, h, :], start=True, stop=False)
                        ins = pe.matmul(bank[x][0][:, h, :], u[:, x, h, :], pt[:, x, h, :], start=False, stop=True)
                    ins.then_inc(o_made[x], 1)

                def pair(i, more):
                    for f in (spread_gates, products, turn_first):
                        for x in range(2):
                            f(x, i)
                    for l in range(1, LV):
                        for f in (off_block, merge):
                            for x in range(2):
                                f(x, i, l)
                    for x in range(2):
                        keys(x, i)
                    for x in range(2):
                        recur(x, i)

                run_pairs(pe, pair)

            @block.vector
            def _(dve):
                def differences(x, i):
                    dve.wait_ge(spread[x], i + 1)
                    dve.tensor_copy(col[:, x, :], T.ps[:, 4 * x + 2, 0:64]).then_inc(col_copied[x], 1)
                    dve.wait_ge(col_copied[x], i + 1)
                    for h in heads:
                        dve.scalar_tensor_tensor(out=dm[:, x, h, :], in0=bank[x][1][:, h, :], scalar=col[:, x, 32 + h:33 + h],
                                                 in1=cap[:], op0=ALU.subtract, op1=ALU.min)
                    dve.tensor_tensor(wend[:, x, :], bank[x][1][:, :, P - 1], col[:, x, 32:32 + H], ALU.subtract
                                      ).then_inc(diffed[x], 1)

                def scores(x, i):
                    dve.wait_ge(decayed[x], 4 * i + 4)
                    dve.tensor_tensor(beg[:, x, :], col[:, x, 0:H], eg_col[:, x, :], ALU.mult).then_inc(beg_done[x], 1)
                    dve.tensor_tensor(lt[:, x], dm[:, x], bank[x][0], ALU.mult).then_inc(beta_used[x], 1)
                    dve.wait_ge(beta_used[x], i + 1)
                    dve.wait_ge(kk_made[x], i + 1)
                    dve.tensor_tensor(lt[:, x], lt[:, x], bank[x][1], ALU.mult).then_inc(lt_done[x], 1)
                    dve.wait_ge(kq_made[x], i + 1)
                    dve.tensor_tensor(pt[:, x], dm[:, x], bank[x][0], ALU.mult).then_inc(pt_done[x], 1)

                def first_tt(x, i):
                    dve.wait_ge(masked[x], LV * i + 1)
                    dve.tensor_tensor(tt[:, x], over(T.ident, H), first[:, x], ALU.subtract).then_inc(tt_first[x], 1)

                def first_t(x, i):
                    dve.wait_ge(t_turned[x], i + 1)
                    dve.tensor_copy(t[:, x], bank[x][1]).then_inc(t_first[x], 1)

                def update(x, i, l):
                    if l < LV - 1:
                        dve.wait_ge(merged[x], UP * i + 2 * l - 1)
                        if l == 1:
                            dve.wait_ge(t_first[x], i + 1)
                        dve.tensor_tensor(t[:, x], t[:, x], bank[x][0], ALU.subtract).then_inc(updated[x], 1)
                        dve.wait_ge(merged[x], UP * i + 2 * l)
                    else:
                        dve.wait_ge(merged[x], UP * i + UP)
                    dve.tensor_tensor(tt[:, x], tt[:, x], bank[x][2], ALU.subtract).then_inc(updated[x], 1)
                    dve.wait_ge(updated[x], UP * i + min(2 * l, UP))

                def recur(x, i):
                    dve.wait_ge(u_made[x], i + 1)
                    dve.tensor_copy(u[:, x], bank[x][1]).then_inc(u_moved[x], 1)
                    dve.wait_ge(s_made[x], i + 1)
                    dve.wait_ge(o_made[x], i + 1)
                    for h in heads:
                        dve.scalar_tensor_tensor(out=state[:, h, :], in0=state[:, h, :], scalar=eg[:, x, h, P - 1:P],
                                                 in1=bank[x][2][:, h, :], op0=ALU.mult, op1=ALU.add
                                                 ).then_inc(s_updated[x], 1)
                    dve.wait_ge(s_updated[x], H * i + H)

                def pair(i, more):
                    for f in (differences, scores, first_tt, first_t):
                        for x in range(2):
                            f(x, i)
                    for l in range(1, LV):
                        for x in range(2):
                            update(x, i, l)
                    for x in range(2):
                        recur(x, i)

                run_pairs(dve, pair)

            @block.scalar
            def _(act):
                def decay(x, i):
                    act.wait_ge(diffed[x], i + 1)
                    act.activation(eg_col[:, x, :], col[:, x, 32:32 + H], ACT.Exp).then_inc(decayed[x], 1)
                    act.activation(dm[:, x], dm[:, x], ACT.Exp).then_inc(decayed[x], 1)
                    act.activation(wend[:, x, :], wend[:, x, :], ACT.Exp).then_inc(decayed[x], 1)
                    act.activation(eg[:, x], bank[x][1], ACT.Exp).then_inc(decayed[x], 1)

                def scale(x, i):
                    act.wait_ge(k_turned[x], i + 1)
                    act.wait_ge(v_turned[x], i + 1)
                    act.wait_ge(beg_done[x], i + 1)
                    act.wait_ge(decayed[x], 4 * i + 4)
                    for dst, src, factor in ((vb, 2, col), (kbe, 3, beg), (kw, 3, wend)):
                        for h in heads:
                            ins = act.activation(dst[:, x, h, :], bank[x][src][:, h, :], ACT.Copy,
                                                 scale=factor[:, x, h:h + 1])
                        ins.then_inc(scaled[x], 1)

                def move_p1(x, i, l):
                    act.wait_ge(p1_made[x], (LV - 1) * i + l)
                    act.activation(p1[:, x], bank[x][1], ACT.Copy).then_inc(p1_moved[x], 1)

                def pair(i, more):
                    for f in (decay, scale):
                        for x in range(2):
                            f(x, i)
                    for l in range(1, LV):
                        for x in range(2):
                            move_p1(x, i, l)
                    for x in range(2):
                        act.wait_ge(w2_made[x], i + 1)
                        act.activation(w2[:, x], bank[x][3], ACT.Copy, scale=-1.0).then_inc(w2_moved[x], 1)
                    for x in range(2):
                        act.wait_ge(o_made[x], i + 1)
                        act.activation(T.acc[:, H:2 * H, bass.ds(2 * P * i + P * x, P)], bank[x][0], ACT.Copy
                                       ).then_inc(o_moved[x], 1)

                run_pairs(act, pair)

            @block.gpsimd
            def _(pool):
                def stage(x, i):
                    cols = bass.ds(2 * P * i + P * x, P)
                    pool.tensor_copy(tiles[:, x], qkv[:, :, cols]).then_inc(staged[x], 1)
                    pool.tensor_copy(rows[:, x, :], gates[:, cols]).then_inc(staged[x], 1)

                def pair(i, more):
                    for l in range(LV):
                        for x in range(2):
                            if l == 0:
                                pool.wait_ge(lt_done[x], i + 1)
                            dst = first[:, x] if l == 0 else am[:, x, l - 1]
                            pool.tensor_tensor(dst, lt[:, x], over(masks[:, l, :], H), ALU.mult).then_inc(masked[x], 1)
                    for x in range(2):
                        pool.wait_ge(decayed[x], 4 * i + 4)
                        pool.tensor_tensor(qe[:, x], tiles[:, x, 0:H, :], eg[:, x], ALU.mult).then_inc(qe_done[x], 1)
                    if more:
                        for x in range(2):
                            pool.wait_ge(kq_made[x], i + 1)
                            pool.wait_ge(qe_done[x], i + 1)
                            stage(x, i + 1)

                for x in range(2):
                    stage(x, 0)
                run_pairs(pool, pair)

            @block.sync
            def _(sp):
                sp.wait_ge(s_updated[1], H * (NCHUNK // 2))
                sp.dma_start(state_out.rearrange("h d e -> d h e"), state[:]).then_inc(out_done, 16)
                sp.wait_ge(out_done, 16)


def stage_delta_sample(nc, T, qkv, gates, consts, state_in, state_out):
    H, B = HEADS_B, SAMPLES
    J = H * B
    with ExitStack() as ctx:
        sb = lambda n, s, d=F32: ctx.enter_context(nc.sbuf_tensor("gs_" + n, s, d))
        sem = lambda n: nc.alloc_semaphore("gs_" + n)
        sel, st, kq = sb("sel", [64, 8, P]), sb("st", [P, J, P]), sb("kq", [P, J, 2])
        beta, a, qk, prod, u, o, vs, srows = (sb(n, [P, J]) for n in "beta a qk prod u o vs srows".split())
        kt, ut = sb("kt", [J, P]), sb("ut", [J, P])
        ud = T.wraw[0:J, 0:J * P].rearrange("p (j n) -> p j n", j=J)
        con_in, st_in, staged, spread = sem("con_in"), sem("st_in"), sem("staged"), sem("spread")
        a_done, sums_made, steps_s, u_done = sem("a_done"), sem("sums_made"), sem("steps"), sem("u_done")
        turned, ud_done, outer, st_new, out_done = sem("turned"), sem("ud_done"), sem("outer"), sem("st_new"), sem("out_done")
        with nc.Block() as block:
            @block.sync
            def _(sp):
                sp.dma_start(sel[:], consts[0:64, C_SEL:C_SEL + 8 * P].rearrange("p (l n) -> p l n", l=8)
                             ).then_inc(con_in, 16)
                for h in range(H):
                    sp.dma_start(st[:, B * h:B * h + B, :], state_in[:, h].rearrange("b d e -> d b e")).then_inc(st_in, 16)
                sp.wait_ge(st_new, J)
                for h in range(H):
                    sp.dma_start(state_out[:, h].rearrange("b d e -> d b e"), st[:, B * h:B * h + B, :]).then_inc(out_done, 16)
                sp.wait_ge(out_done, 16 * H)

            @block.tensor
            def _(pe):
                pe.wait_ge(con_in, 16)
                for n in range(8):
                    ins = pe.matmul(T.ps[:, 1, B * n:B * n + B], sel[:, n, :], gates[:, PROMPT:TOK], start=True, stop=True)
                ins.then_inc(spread, 1)
                pe.wait_ge(staged, 4)
                pe.wait_ge(st_in, 16 * H)
                for j in range(J):
                    pe.matmul(T.ps[:, 0, 2 * j:2 * j + 2], st[:, j, :], kq[:, j, :], start=True, stop=True)
                pe.matmul(T.ps[:, 2, 0:J], T.con[:, C_ONE:C_ONE + P], prod[:], start=True, stop=True).then_inc(sums_made, 1)
                pe.wait_ge(u_done, 1)
                pe.transpose(T.ps[0:J, 3, 0:P], srows[:], T.ident)
                pe.transpose(T.ps[0:J, 3, P:2 * P], u[:], T.ident).then_inc(turned, 1)
                for half in range(2):
                    pe.wait_ge(ud_done, 2)
                    pe.wait_ge(st_new, 16 * half)
                    for n in range(4):
                        j = 16 * half + 4 * n
                        pe.matmul(T.ps[:, 4 + n, :], kt[:], ud[:, j:j + 4, :].rearrange("p j n -> p (j n)"),
                                  start=True, stop=True).then_inc(outer, 1)

            @block.scalar
            def _(act):
                act.wait_ge(spread, 1)
                act.activation(a[:], T.ps[:, 1, J:2 * J], ACT.Exp).then_inc(a_done, 1)

            @block.vector
            def _(dve):
                steps = Steps(dve, steps_s)
                sample = lambda n: qkv[:, H * n:H * n + H, PROMPT:TOK]
                grid = lambda x: x.rearrange("p (h b) -> p h b", h=H)
                dve.tensor_copy(kq[:, :, 0].rearrange("p (h b) -> p h b", h=H), sample(1)).then_inc(staged, 1)
                dve.tensor_copy(kq[:, :, 1].rearrange("p (h b) -> p h b", h=H), sample(0)).then_inc(staged, 1)
                dve.tensor_tensor(grid(prod[:]), sample(0), sample(1), ALU.mult).then_inc(staged, 1)
                dve.tensor_copy(grid(srows[:]), sample(1)).then_inc(staged, 1)
                steps.note(dve.tensor_copy(grid(vs[:]), sample(2)))
                dve.wait_ge(spread, 1)
                dve.wait_ge(a_done, 1)
                steps.done(dve.tensor_copy(beta[:], T.ps[:, 1, 0:J]))
                dve.wait_ge(sums_made, 1)
                kqs = T.ps[:, 0, 0:2 * J].rearrange("p (j c) -> p c j", c=2)
                steps.done(dve.tensor_tensor(u[:], a[:], kqs[:, 0, :], ALU.mult))
                steps.done(dve.tensor_tensor(u[:], vs[:], u[:], ALU.subtract))
                steps.done(dve.tensor_tensor(u[:], u[:], beta[:], ALU.mult))
                u_val = steps.note(dve.tensor_tensor(o[:], a[:], kqs[:, 1, :], ALU.mult))
                dve.tensor_tensor(qk[:], u[:], T.ps[:, 2, 0:J], ALU.mult).then_inc(u_done, 1)
                dve.wait_ge(u_done, 1)
                dve.wait_ge(steps_s, u_val)
                dve.tensor_tensor(T.acc[:, H:2 * H, PROMPT:TOK], grid(o[:]), grid(qk[:]), ALU.add)
                dve.wait_ge(turned, 1)
                dve.tensor_copy(kt[:], T.ps[0:J, 3, 0:P]).then_inc(ud_done, 1)
                steps.done(dve.tensor_copy(ut[:], T.ps[0:J, 3, P:2 * P]))
                dve.tensor_tensor(ud, over(ut[:], J), per_column(T.ident[0:J, 0:J], P), ALU.mult).then_inc(ud_done, 1)
                for half in range(2):
                    for n in range(16):
                        j = 16 * half + n
                        dve.wait_ge(outer, 4 * half + n // 4 + 1)
                        dve.scalar_tensor_tensor(out=st[:, j, :], in0=st[:, j, :], scalar=a[:, j:j + 1],
                                                 in1=T.ps[:, 4 + n // 4, P * (n % 4):P * (n % 4) + P],
                                                 op0=ALU.mult, op1=ALU.add).then_inc(st_new, 1)


def stage_gate_z(nc, T, proj, g_out):
    H = HEADS_B
    with ExitStack() as ctx:
        z = ctx.enter_context(nc.sbuf_tensor("gz_z", [P, H, TOK], F32))
        gain = ctx.enter_context(nc.sbuf_tensor("gz_gain", [P, 1], F32))
        z_in, zs = (nc.alloc_semaphore("gz_" + n) for n in ("z_in", "zs"))
        with nc.Block() as block:
            @block.sync
            def _(sp):
                sp.dma_start(z[:], proj.rearrange("(m p) n -> p m n", p=P)[:, 20:24, :]).then_inc(z_in, 16)
                sp.dma_start(gain[:], g_out.rearrange("(a b) -> a b", b=1)).then_inc(z_in, 16)

            @block.scalar
            def _(act):
                act.wait_ge(z_in, 32)
                act.activation(z[:], z[:], ACT.Silu).then_inc(zs, 1)
        head_norms(nc, T, "gz", [T.acc[:, H + h, :] for h in range(H)], 1.0 / P, lambda k: gain[:], lambda k: z[:, k, :])


def mixer_even(nc, T, proj, ins, outs, consts):
    with ExitStack() as ctx:
        qkv = ctx.enter_context(nc.sbuf_tensor("qkv", [P, 3 * HEADS_B, TOK], F32))
        gates = ctx.enter_context(nc.sbuf_tensor("gates", [64, TOK], F32))
        stage_gmlp(nc, T, proj, qkv, ins["a_v_norm"][0], ins["a_w_s"][0], ins["a_b_s"][0],
                   outs["chunk_v"][0].rearrange("b s c -> (b s) c"))
        stage_gates(nc, T, proj, gates, ins["b_a_log"][0], ins["b_dt_bias"][0], consts)
        head_norms(nc, T, "qk", [qkv[:, m, :] for m in range(2 * HEADS_B)], 1.0,
                   lambda k: float(P) ** -0.5 if k < HEADS_B else 1.0)
        stage_delta(nc, T, qkv, gates, consts, outs["gdn_state_prompt"][0, 0])
        stage_delta_sample(nc, T, qkv, gates, consts, ins["state_gdn"][0], outs["gdn_state_sample"][0])
    stage_gate_z(nc, T, proj, ins["b_out_norm"][0])


def stage_lambda(nc, T, nlam, subln_cols, subln_rows, c_lambda, c_subln):
    with ExitStack() as ctx:
        sem = lambda n: nc.alloc_semaphore("lm_" + n)
        lq = ctx.enter_context(nc.sbuf_tensor("lm_lq", [P, 4, 64], F32))
        pr = ctx.enter_context(nc.sbuf_tensor("lm_pr", [P, 2, 64], F32))
        sm = ctx.enter_context(nc.sbuf_tensor("lm_sm", [P, 2], F32))
        par_in, own, exped = sem("par_in"), sem("own"), sem("exped")
        with nc.Block() as block:
            @block.sync
            def _(sp):
                sp.dma_start(lq[:], c_lambda.rearrange("a d -> (a d)").partition_broadcast(P)).then_inc(par_in, 16)
                sp.dma_start(subln_rows, c_subln.partition_broadcast(P)).then_inc(par_in, 16)
                sp.dma_start(subln_cols, c_subln.rearrange("(a b) -> a b", b=1)).then_inc(par_in, 16)

            @block.vector
            def _(dve):
                steps = Steps(dve, own)
                dve.wait_ge(par_in, 48)
                steps.note(dve.tensor_scalar(subln_rows, subln_rows, 1.0 - LAM_INIT, None, ALU.mult))
                steps.note(dve.tensor_scalar(subln_cols, subln_cols, 1.0 - LAM_INIT, None, ALU.mult))
                steps.done(dve.tensor_tensor(pr[:], lq[:, 0:4:2, :], lq[:, 1:4:2, :], ALU.mult))
                steps.note(dve.tensor_reduce(sm[:], pr[:], AX_X, ALU.add))
                dve.wait_ge(exped, 1)
                dve.scalar_tensor_tensor(out=nlam, in0=sm[:, 1:2], scalar=-LAM_INIT, in1=sm[:, 0:1], op0=ALU.add,
                                         op1=ALU.subtract)

            @block.scalar
            def _(act):
                act.wait_ge(own, 4)
                act.activation(sm[:], sm[:], ACT.Exp).then_inc(exped, 1)


def stage_attention(nc, T, proj, consts, nlam, subln_rows, k_out, v_out):
    H, NQ = HEADS_C, NCHUNK
    spans = [(i + 1) * P for i in range(NQ)]
    parts = [1 if s <= 512 else 2 for s in spans]
    LEAD = 4

    def ahead(h, p, i, d, more):
        n = i + d
        if n < 0 or (n >= NQ and not more):
            return None
        return (h, p, n) if n < NQ else (h + 1, 1 - p, n - NQ)

    def run_heads(eng, start, head):
        start()
        with eng.Fori(0, H // 2 - 1) as j:
            head(2 * j, 0, True)
            head(2 * j + 1, 1, True)
        head(H - 2, 0, True)
        head(H - 1, 1, False)

    with ExitStack() as ctx:
        sb = lambda n, s, d=F32: ctx.enter_context(nc.sbuf_tensor("at_" + n, s, d))
        sem = lambda n: nc.alloc_semaphore("at_" + n)
        qin, kin, vin = (sb(n, [P, PROMPT]) for n in ("qin", "kin", "vin"))
        split = lambda p, n: (T.wh, T.wl)[p][:, n * PROMPT:(n + 1) * PROMPT]
        kh, kl = [split(p, 0) for p in range(2)], [split(p, 1) for p in range(2)]
        qh = [[split(p, 2 + c) for c in range(2)] for p in range(2)]
        ql = [[split(p, 4 + c) for c in range(2)] for p in range(2)]
        vt, kt = sb("vt", [P, 2, NQ, P]), sb("kt", [P, NQ, P])
        dist = sb("dist", [P, PROMPT])
        bias = T.wraw[:, 0:2 * PROMPT].rearrange("p (r n) -> p r n", r=2)
        w = T.wraw[:, 2 * PROMPT:4 * PROMPT].rearrange("p (r n) -> p r n", r=2)
        wt = T.wraw[:, 4 * PROMPT:6 * PROMPT].rearrange("p (r t e) -> p r t e", r=2, e=P)
        slope, half = sb("slope", [P, H]), sb("half", [P, 2])
        s = sb("s", [P, 4, 2, PROMPT])
        o, junk = sb("o", [P, 2, NQ, P]), sb("junk", [P, P])
        mx, nmx, sm, rc = (sb(n, [P, 4, 2]) for n in ("mx", "nmx", "sm", "rc"))
        ms = sb("ms", [P, 2, NQ])
        con_in, half_done, seen = sem("con_in"), sem("half_done"), sem("seen")
        q_in, k_in, v_in = sem("q_in"), sem("k_in"), sem("v_in")
        q_hi, q_lo, k_hi, k_lo, bias_done = sem("q_hi"), sem("q_lo"), sem("k_hi"), sem("k_lo"), sem("bias_done")
        kv_turned, kv_taken, o_turned, o_taken = sem("kv_turned"), sem("kv_taken"), sem("o_turned"), sem("o_taken")
        v_stored, k_stored = sem("v_stored"), sem("k_stored")
        scored, maxed, negated, exped = sem("scored"), sem("maxed"), sem("negated"), sem("exped")
        inverted, coefs, w_first, weighted = sem("inverted"), sem("coefs"), sem("w_first"), sem("weighted")
        w_turned, wt_moved, av_made, o_moved, squared = (sem(n) for n in "w_turned wt_moved av_made o_moved squared".split())
        logged, rooted, normed = sem("logged"), sem("rooted"), sem("normed")
        mt = proj.rearrange("(m p) n -> m p n", p=P)
        k_rows = k_out.rearrange("(t p) (h e) -> h p t e", p=P, e=P)
        v_rows = v_out.rearrange("(t p) (h e) -> h p t e", p=P, e=P)
        first_bank = lambda c, i: 2 * c + (i % 2 if parts[i] == 1 else 0)
        scores = lambda c, i: T.ps[:, first_bank(c, i):first_bank(c, i) + parts[i], 0:spans[i] // parts[i]]
        av = T.ps[:, 6, 0:P]
        fold = lambda ap, i: ap[:, 0:spans[i]].rearrange("p (a n) -> p a n", a=parts[i])

        with nc.Block() as block:
            @block.sync
            def _(sp):
                sp.dma_start(dist[:], consts[:, C_DIST:C_DIST + PROMPT]).then_inc(con_in, 16)
                sp.dma_start(slope[:], consts[:, C_SLOPE:C_SLOPE + H]).then_inc(con_in, 16)
                sp.dma_start(half[:], consts[:, C_HALF:C_HALF + 2]).then_inc(con_in, 16)

            @block.vector
            def _(dve):
                dve.wait_ge(con_in, 48)
                dve.tensor_scalar(half[:], half[:], 64.0 ** -0.5, None, ALU.mult).then_inc(half_done, 1)

        with nc.Block() as block:
            @block.sync
            def _(sp):
                def load(h):
                    sp.wait_ge(q_lo, 2 * h)
                    sp.dma_start(qin[:], mt[bass.ds(h, 1), :, 0:PROMPT].rearrange("a p n -> p (a n)")).then_inc(q_in, 16)
                    sp.wait_ge(kv_turned, 4 * h)
                    sp.wait_ge(k_lo, h)
                    sp.dma_start(kin[:], mt[bass.ds(h + H, 1), :, 0:PROMPT].rearrange("a p n -> p (a n)")).then_inc(k_in, 16)
                    sp.dma_start(vin[:], mt[bass.ds(h + 2 * H, 1), :, 0:PROMPT].rearrange("a p n -> p (a n)")).then_inc(v_in, 16)

                def store(h, p):
                    sp.wait_ge(kv_taken, 4 * h + 2)
                    sp.dma_start(v_rows[bass.ds(h, 1), :, :, :].rearrange("a p t e -> p (a t) e"), vt[:, p]).then_inc(v_stored, 16)
                    sp.wait_ge(kv_taken, 4 * h + 4)
                    sp.dma_start(k_rows[bass.ds(h, 1), :, :, :].rearrange("a p t e -> p (a t) e"), kt[:]).then_inc(k_stored, 16)

                def head(h, p, more):
                    store(h, p)
                    if more:
                        load(h + 1)

                run_heads(sp, lambda: load(0), head)
                sp.wait_ge(v_stored, 16 * H)
                sp.wait_ge(k_stored, 16 * H)

            @block.tensor
            def _(pe):
                def turn_kv(h, n, outputs_before):
                    pe.wait_ge((v_in, v_in, k_in, k_in)[n], 16 * h + 16)
                    pe.wait_ge(kv_taken, 4 * h + n)
                    if outputs_before is not None:
                        pe.wait_ge(o_taken, outputs_before)
                    src = (vin, kin)[n // 2]
                    for j in range(4):
                        t = 4 * (n % 2) + j
                        ins = pe.transpose(T.ps[:, 7, P * j:P * j + P], src[:, P * t:P * t + P], T.ident)
                    ins.then_inc(kv_turned, 1)

                def turn_output(h, p, n, kv_before):
                    pe.wait_ge(normed, NQ * h + 4 * n + 4)
                    pe.wait_ge(o_taken, 2 * h + n)
                    pe.wait_ge(kv_taken, kv_before)
                    for j in range(4):
                        ins = pe.transpose(T.ps[:, 7, P * j:P * j + P], o[:, p, 4 * n + j, :], T.ident)
                    ins.then_inc(o_turned, 1)

                def score(h, p, i):
                    if i == 0:
                        pe.wait_ge(q_lo, 2 * h + 2)
                        pe.wait_ge(k_lo, h + 1)
                    width = spans[i] // parts[i]
                    for c in range(2):
                        before = 2 * (i - 2) if i in (2, 3) else -2 if i < 2 else 2 * (i - 1)
                        if not (isinstance(h, int) and h == 0 and before < 0):
                            pe.wait_ge(maxed, 2 * NQ * h + before + c + 1)
                        for part in range(parts[i]):
                            cols = slice(part * width, (part + 1) * width)
                            for n, (a, b) in enumerate(((qh[p][c], kh[p]), (qh[p][c], kl[p]), (ql[p][c], kh[p]))):
                                ins = pe.matmul(T.ps[:, first_bank(c, i) + part, 0:width], a[:, P * i:P * i + P], b[:, cols],
                                                start=n == 0, stop=n == 2)
                        ins.then_inc(scored, 1)

                def turn_weights(h, p, i):
                    pe.wait_ge(weighted, NQ * h + i + 1)
                    pe.wait_ge(wt_moved, NQ * h + i)
                    for t in range(i + 1):
                        ins = pe.transpose(T.ps[:, 4 + t // 4, P * (t % 4):P * (t % 4) + P],
                                           w[:, i % 2, P * t:P * t + P], T.ident)
                    ins.then_inc(w_turned, 1)

                def times_values(h, p, i):
                    pe.wait_ge(wt_moved, NQ * h + i + 1)
                    pe.wait_ge(o_moved, NQ * h + i)
                    if i == 0:
                        pe.wait_ge(kv_taken, 4 * h + 2)
                    for t in range(i + 1):
                        ins = pe.matmul(av, wt[:, i % 2, t, :], vt[:, p, t, :], start=t == 0, stop=t == i)
                    ins.then_inc(av_made, 1)

                def step(h, p, i, more):
                    if i >= 0:
                        times_values(h, p, i)
                    for f, d in ((turn_weights, 1), (score, LEAD)):
                        tile = ahead(h, p, i, d, more)
                        if tile is not None:
                            f(*tile)

                def head(h, p, more):
                    for i in range(NQ):
                        step(h, p, i, more)
                        n = {0: 0, 1: 1, 4: 2, 5: 3}.get(i)
                        if more and n is not None:
                            turn_kv(h + 1, n, 2 * h if p == 0 or n >= 2 else 2 * (h - 1))
                        if p == 1 and i in (2, 3):
                            turn_output(h - 1, 0, i - 2, 4 * (h + 1) + (2 if more else 0))
                    if p == 1:
                        for n in range(2):
                            turn_output(h, 1, n, 4 * (h + 1) + (4 if more else 0))

                def start():
                    for n in range(4):
                        turn_kv(0, n, None)
                    for i in range(-LEAD, 0):
                        step(0, 0, i, True)

                run_heads(pe, start, head)

            @block.scalar
            def _(act):
                def split_q(h, p):
                    act.wait_ge(q_in, 16 * h + 16)
                    for c in range(2):
                        act.activation(qh[p][c], qin[:], ACT.Copy, scale=half[:, c:c + 1]).then_inc(q_hi, 1)

                def split_k(h, p):
                    act.wait_ge(k_in, 16 * h + 16)
                    act.activation(kh[p], kin[:], ACT.Copy).then_inc(k_hi, 1)

                def make_bias(h, p):
                    act.activation(bias[:, p, :], dist[:], ACT.Copy, scale=slope[:, bass.ds(h, 1)]).then_inc(bias_done, 1)

                def take_kv(h, p, n):
                    act.wait_ge(kv_turned, 4 * h + n + 1)
                    dst = (vt[:, p], kt)[n // 2]
                    act.activation(dst[:, 4 * (n % 2):4 * (n % 2) + 4, :], T.ps[:, 7, :].rearrange("p (t e) -> p t e", t=4),
                                   ACT.Copy).then_inc(kv_taken, 1)

                def exponentials(h, p, i):
                    act.wait_ge(negated, NQ * h + i + 1)
                    for c in range(2):
                        x = s[:, i % 4, c, 0:spans[i]]
                        act.activation(x, x, ACT.Exp, bias=nmx[:, i % 4, c:c + 1],
                                       accum_out=sm[:, i % 4, c:c + 1]).then_inc(exped, 1)

                def square(h, p, i):
                    act.wait_ge(o_moved, NQ * h + i + 1)
                    act.wait_ge(squared, NQ * h + i)
                    if i == 0:
                        act.wait_ge(normed, NQ * h if p == 0 else NQ * (h - 1))
                    act.activation(junk[:], o[:, p, i, :], ACT.Square, accum_out=ms[:, p, i:i + 1]).then_inc(squared, 1)

                def take_weights(h, p, i):
                    act.wait_ge(w_turned, NQ * h + i + 1)
                    act.wait_ge(av_made, NQ * h + max(i - 1, 0))
                    for b in range(i // 4 + 1):
                        n = min(4, i + 1 - 4 * b)
                        ins = act.activation(wt[:, i % 2, 4 * b:4 * b + n, :],
                                             T.ps[:, 4 + b, 0:P * n].rearrange("p (t e) -> p t e", t=n), ACT.Copy)
                    ins.then_inc(wt_moved, 1)

                def step(h, p, i, more):
                    tile = ahead(h, p, i, 2, more)
                    if tile is not None:
                        exponentials(*tile)
                    tile = ahead(h, p, i, 1, more)
                    if tile is not None:
                        take_weights(*tile)
                    if i >= 0:
                        square(h, p, i)

                def root(h, p):
                    act.wait_ge(squared, NQ * h + NQ)
                    act.activation(ms[:, p, :], ms[:, p, :], ACT.Ln, scale=1.0 / P, bias=T.eps[:]).then_inc(logged, 1)
                    act.wait_ge(logged, h + 1)
                    act.activation(ms[:, p, :], ms[:, p, :], ACT.Exp, scale=-0.5).then_inc(rooted, 1)

                def take_output(h, n):
                    act.wait_ge(o_turned, 2 * h + n + 1)
                    act.activation(T.acc[:, bass.ds(h, 1), 512 * n:512 * n + 512].rearrange("p a n -> p (a n)"),
                                   T.ps[:, 7, :], ACT.Copy).then_inc(o_taken, 1)

                def head(h, p, more):
                    for i in range(NQ):
                        step(h, p, i, more)
                        if more and i == 0:
                            act.wait_ge(v_stored, 16 * h)
                            act.wait_ge(scored, 2 * NQ * h)
                            split_q(h + 1, 1 - p)
                        if p == 1 and i == 0:
                            root(h - 1, 0)
                        if more and i == 1:
                            split_k(h + 1, 1 - p)
                        if more and i == 2:
                            act.wait_ge(maxed, 2 * NQ * h)
                            make_bias(h + 1, 1 - p)
                        n = {0: 0, 1: 1, 4: 2, 5: 3}.get(i)
                        if more and n is not None:
                            if n == 2:
                                act.wait_ge(k_stored, 16 * h + 16)
                            take_kv(h + 1, 1 - p, n)
                        if p == 1 and i in (2, 3):
                            take_output(h - 1, i - 2)
                    if p == 1:
                        root(h, 1)
                        for n in range(2):
                            take_output(h, n)

                def start():
                    split_q(0, 0)
                    split_k(0, 0)
                    make_bias(0, 0)
                    for n in range(4):
                        take_kv(0, 0, n)
                    for i in range(-LEAD, 0):
                        step(0, 0, i, True)

                run_heads(act, start, head)

            @block.vector
            def _(dve):
                def split_q(h, p):
                    for c in range(2):
                        dve.wait_ge(q_hi, 2 * h + c + 1)
                        dve.scalar_tensor_tensor(out=ql[p][c], in0=qin[:], scalar=half[:, c:c + 1], in1=qh[p][c],
                                                 op0=ALU.mult, op1=ALU.subtract).then_inc(q_lo, 1)

                def weigh(h, p, i):
                    dve.wait_ge(w_first, NQ * h + i + 1)
                    x = w[:, i % 2, 0:spans[i]]
                    dve.scalar_tensor_tensor(out=x, in0=s[:, i % 4, 1, 0:spans[i]], scalar=rc[:, i % 4, 1:2], in1=x,
                                             op0=ALU.mult, op1=ALU.add).then_inc(weighted, 1)

                def maxima(h, p, i):
                    if i == 0:
                        dve.wait_ge(bias_done, h + 1)
                    for c in range(2):
                        dve.wait_ge(scored, 2 * NQ * h + 2 * i + c + 1)
                        dve.sem_inc(seen, 1)
                        dve.tensor_tensor_reduce(fold(s[:, i % 4, c, :], i), scores(c, i),
                                                 fold(bias[:, p, PROMPT - spans[i]:], i), 1.0,
                                                 -3e38, ALU.add, ALU.max, mx[:, i % 4, c:c + 1]).then_inc(maxed, 1)
                    dve.wait_ge(maxed, 2 * NQ * h + 2 * i + 2)
                    dve.tensor_scalar(nmx[:, i % 4, :], mx[:, i % 4, :], -1.0, None, ALU.mult).then_inc(negated, 1)

                def coefficients(h, p, i):
                    dve.wait_ge(exped, 2 * NQ * h + 2 * i + 2)
                    dve.reciprocal(rc[:, i % 4, :], sm[:, i % 4, :]).then_inc(inverted, 1)
                    dve.wait_ge(inverted, NQ * h + i + 1)
                    dve.tensor_scalar(rc[:, i % 4, 1:2], rc[:, i % 4, 1:2], nlam, None, ALU.mult).then_inc(coefs, 1)

                def take_output(h, p, i):
                    dve.wait_ge(av_made, NQ * h + i + 1)
                    if i == 0:
                        dve.wait_ge(o_turned, 2 * h if p == 0 else 2 * (h - 1))
                    dve.tensor_copy(o[:, p, i, :], av).then_inc(o_moved, 1)

                def norm(h, p):
                    dve.wait_ge(rooted, h + 1)
                    dve.wait_ge(o_moved, NQ * h + NQ)
                    for i in range(NQ):
                        dve.scalar_tensor_tensor(out=o[:, p, i, :], in0=o[:, p, i, :], scalar=ms[:, p, i:i + 1],
                                                 in1=subln_rows, op0=ALU.mult, op1=ALU.mult).then_inc(normed, 1)

                def step(h, p, i, more):
                    for f, d in ((weigh, 1), (maxima, 3), (coefficients, 2)):
                        tile = ahead(h, p, i, d, more)
                        if tile is not None:
                            f(*tile)
                    if i >= 0:
                        take_output(h, p, i)

                def head(h, p, more):
                    for i in range(NQ):
                        step(h, p, i, more)
                        if more and i == 1:
                            split_q(h + 1, 1 - p)
                        if p == 1 and i == 1:
                            norm(h - 1, 0)
                    if p == 1:
                        norm(h, 1)

                def start():
                    split_q(0, 0)
                    for i in range(-LEAD, 0):
                        step(0, 0, i, True)

                run_heads(dve, start, head)

            @block.gpsimd
            def _(pool):
                def split_k(h, p):
                    pool.wait_ge(k_hi, h + 1)
                    pool.tensor_tensor(kl[p], kin[:], kh[p], ALU.subtract).then_inc(k_lo, 1)

                def first(h, p, i):
                    pool.wait_ge(coefs, NQ * h + i + 1)
                    pool.wait_ge(w_turned, NQ * h + (i - 1 if i else 0))
                    pool.tensor_tensor(w[:, i % 2, 0:spans[i]], s[:, i % 4, 0, 0:spans[i]],
                                       rc[:, i % 4, 0:1].to_broadcast([P, spans[i]]), ALU.mult).then_inc(w_first, 1)

                def head(h, p, more):
                    for i in range(NQ):
                        tile = ahead(h, p, i, 2, more)
                        if tile is not None:
                            first(*tile)
                        if more and i == 2:
                            split_k(h + 1, 1 - p)

                def start():
                    split_k(0, 0)
                    for i in range(2):
                        first(0, 0, i)

                run_heads(pool, start, head)


def stage_attention_sample(nc, T, proj, consts, nlam, subln_cols, cache_k, cache_v, page_table, k_out, v_out):
    H, B = HEADS_C, SAMPLES
    J = H * B
    N_POOL = cache_k.shape[0]
    with ExitStack() as ctx:
        sb = lambda n, s, d=F32: ctx.enter_context(nc.sbuf_tensor("as_" + n, s, d))
        sem = lambda n: nc.alloc_semaphore("as_" + n)
        xs = sb("xs", [P, 3 * H, B])
        xrows, qrow, qm = sb("xrows", [B, 3 * D]), sb("qrow", [B, D]), sb("qm", [B, D])
        table = sb("table", [1, B * PAGES], I32)
        page, prod, qb = sb("page", [P, 2, PAGES, D]), sb("prod", [P, PAGES, D]), sb("qb", [P, 2, D])
        sc, scp = sb("sc", [P, PAGES, B, 2 * H]), sb("scp", [P, PAGES, P])
        sbias, half, pair = sb("sbias", [P, PAST + 1]), sb("half", [P, 2]), sb("pair", [P, J])
        s, pn, pq = sb("s", [P, PAST + 1]), sb("pn", [P, 2, J]), sb("pq", [P, J])
        mx, sm, wcol = sb("mx", [P, 2]), sb("sm", [P, 2]), sb("wcol", [P, P])
        wk, wb, av, sq, rs = sb("wk", [P, PAGES, J]), sb("wb", [P, SAMPLES, PAGES, H]), sb("av", [P, H, B]), sb("sq", [P, J]), sb("rs", [P, J])
        x_in, con_in, r_turned, r_moved, out_done = (sem(n) for n in "x_in con_in r_turned r_moved out_done".split())
        qm_done, qb_made, qb_moved, reduced, reduced_v = (sem(n) for n in "qm_done qb_made qb_moved reduced reduced_v".split())
        page_in, multiplied, multiplied_v, v_in, o_made, o_moved = (
            [sem(n + "0"), sem(n + "1")] for n in "page_in multiplied multiplied_v v_in o_made o_moved".split())
        own, t_made, s_moved, exped, p_turned, wc_done, wn_made = (sem(n) for n in "own t_made s_moved exped p_turned wc_done wn_made".split())
        wb_done, own2, ss_made, rooted, act_own = (sem(n) for n in "wb_done own2 ss_made rooted act_own".split())
        ptab = sem("ptab")

        def load_page(sp, cache, dst, i, signal):
            for j in range(PAGES):
                n = sp.value_load(table[0:1, bass.ds(PAGES * i + j, 1)], min_val=0, max_val=N_POOL - 1)
                sp.dma_start(dst[:, j, :], cache[bass.ds(n, 1), :, :].rearrange("a p n -> p (a n)")).then_inc(signal, 16)

        with nc.Block() as block:
            @block.sync
            def _(sp):
                sp.dma_start(xs[:], proj.rearrange("(m p) n -> p m n", p=P)[:, 0:3 * H, PROMPT:TOK]).then_inc(x_in, 16)
                sp.dma_start(table[:], page_table.rearrange("b j -> (b j)").unsqueeze(0)).then_inc(ptab, 16)
                sp.dma_start(sbias[:], consts[:, C_SBIAS:C_SBIAS + PAST + 1]).then_inc(con_in, 16)
                sp.dma_start(half[:], consts[:, C_HALF:C_HALF + 2]).then_inc(con_in, 16)
                sp.dma_start(pair[:], consts[:, C_PAIR:C_PAIR + J]).then_inc(con_in, 16)
                sp.wait_ge(r_moved, 1)
                sp.dma_start(k_out, xrows[:, D:2 * D]).then_inc(out_done, 16)
                sp.dma_start(v_out, xrows[:, 2 * D:3 * D]).then_inc(out_done, 16)
                sp.wait_ge(out_done, 32)
                sp.wait_ge(ptab, 16)

            @block.tensor
            def _(pe):
                pe.wait_ge(x_in, 16)
                flat = T.ps[0:B, 0:6, :].rearrange("r b n -> r (b n)")
                for m in range(3 * H):
                    ins = pe.transpose(flat[:, P * m:P * m + P], xs[:, m, :], T.ident)
                ins.then_inc(r_turned, 1)

            @block.vector
            def _(dve):
                dve.wait_ge(r_turned, 1)
                dve.tensor_copy(xrows[:], T.ps[0:B, 0:6, :].rearrange("r b n -> r (b n)")).then_inc(r_moved, 1)
                dve.wait_ge(r_moved, 1)
                dve.tensor_scalar(qrow[:], xrows[:, 0:D], 64.0 ** -0.5, None, ALU.mult)
                dve.wait_ge(con_in, 48)

        with nc.Block() as block:
            @block.sync
            def _(sp):
                with sp.Fori(0, B // 2) as i:
                    for r in range(2):
                        sp.wait_ge(multiplied[r], i)
                        sp.wait_ge(multiplied_v[r], i)
                        load_page(sp, cache_k, page[:, r], 2 * i + r, page_in[r])

            @block.vector
            def _(dve):
                def mask(b):
                    dve.tensor_scalar(qm[:], qrow[:], T.ident[0:B, bass.ds(b, 1)], None, ALU.mult).then_inc(qm_done, 1)

                def add_up(j, b):
                    return dve.tensor_reduce(sc[:, j, bass.ds(b, 1), :].rearrange("p a m -> p (a m)"),
                                             prod[:, j, :].rearrange("p (m d) -> p m d", d=64), AX_X, ALU.add)

                dve.tensor_scalar(qm[:], qrow[:], T.ident[0:B, 0:1], None, ALU.mult).then_inc(qm_done, 1)
                with dve.Fori(0, B // 2) as i:
                    for r in range(2):
                        b = 2 * i + r
                        dve.wait_ge(qb_made, b + 1)
                        mask(b + 1)
                        dve.wait_ge(qb_moved, b + 1)
                        dve.wait_ge(page_in[r], 16 * PAGES * i + 16 * PAGES)
                        dve.wait_ge(reduced_v, b)
                        dve.tensor_tensor(prod[:, 1, :], page[:, r, 1, :], qb[:, r, :], ALU.mult).then_inc(multiplied_v[r], 1)
                        dve.wait_ge(multiplied_v[r], i + 1)
                        add_up(1, b).then_inc(reduced_v, 1)
                        dve.wait_ge(multiplied[r], i + 1)
                        add_up(0, b).then_inc(reduced, 1)

            @block.tensor
            def _(pe):
                with pe.Fori(0, B) as b:
                    pe.wait_ge(qm_done, b + 1)
                    pe.wait_ge(qb_moved, b)
                    for n in range(2):
                        ins = pe.matmul(T.ps[:, n, :], T.con[0:B, C_ONE:C_ONE + P], qm[:, 512 * n:512 * n + 512],
                                        start=True, stop=True)
                    ins.then_inc(qb_made, 1)

            @block.scalar
            def _(act):
                with act.Fori(0, B // 2) as i:
                    for r in range(2):
                        act.wait_ge(qb_made, 2 * i + r + 1)
                        act.wait_ge(multiplied[r], i)
                        act.wait_ge(multiplied_v[r], i)
                        act.activation(qb[:, r, :], T.ps[:, 0:2, :].rearrange("p a n -> p (a n)"), ACT.Copy
                                       ).then_inc(qb_moved, 1)

            @block.gpsimd
            def _(pool):
                with pool.Fori(0, B // 2) as i:
                    for r in range(2):
                        pool.wait_ge(page_in[r], 16 * PAGES * i + 16 * PAGES)
                        pool.wait_ge(qb_moved, 2 * i + r + 1)
                        pool.wait_ge(reduced, 2 * i + r)
                        pool.tensor_tensor(prod[:, 0, :], page[:, r, 0, :], qb[:, r, :], ALU.mult).then_inc(multiplied[r], 1)

        with nc.Block() as block:
            @block.vector
            def _(dve):
                steps = Steps(dve, own)
                q, k = xs[:, 0:H, :], xs[:, H:2 * H, :]
                for j in range(PAGES):
                    steps.note(dve.tensor_copy(scp[:, j, :].rearrange("p (c h b) -> p c h b", c=2, h=H),
                                               sc[:, j].rearrange("p b (h c) -> p c h b", c=2)))
                steps.done(dve.scalar_tensor_tensor(out=pq[:].rearrange("p (h b) -> p h b", h=H), in0=q,
                                                    scalar=64.0 ** -0.5, in1=k, op0=ALU.mult, op1=ALU.mult))
                for c in range(2):
                    steps.note(dve.tensor_scalar(pn[:, c, :], pq[:], half[:, c:c + 1], None, ALU.mult))
                dve.wait_ge(t_made, 1)
                steps.done(dve.tensor_tensor_reduce(s[:], T.ps[:, 0, 0:PAST + 1], sbias[:], 1.0, -3e38, ALU.add, ALU.max,
                                                    mx[:, 0:1]))
                dve.tensor_scalar(mx[:, 1:2], mx[:, 0:1], -1.0, None, ALU.mult).then_inc(s_moved, 1)
                dve.wait_ge(exped, 1)
                steps.done(dve.reciprocal(sm[:, 1:2], sm[:, 0:1]))
                steps.done(dve.tensor_scalar(sm[64:P, 1:2], sm[64:P, 1:2], nlam[64:P, :], None, ALU.mult))
                steps.done(dve.tensor_scalar(s[:], s[:], sm[:, 1:2], None, ALU.mult))
                dve.tensor_copy(wcol[:], s[:, PAST:PAST + 1].to_broadcast([P, P])).then_inc(wc_done, 1)
                dve.wait_ge(p_turned, 1)
                x = T.ps[:, 1, 0:PAGES * P].rearrange("p (j c n) -> p j c n", j=PAGES, c=2)
                steps.done(dve.tensor_copy(wk[:], x[:, :, 0, :]))
                dve.tensor_tensor(wk[:], wk[:], x[:, :, 1, :], ALU.add)

            @block.scalar
            def _(act):
                act.wait_ge(s_moved, 1)
                act.activation(s[:], s[:], ACT.Exp, bias=mx[:, 1:2], accum_out=sm[:, 0:1]).then_inc(exped, 1)

            @block.tensor
            def _(pe):
                pe.wait_ge(own, 5)
                for j in range(PAGES):
                    pe.transpose(T.ps[:, 0, P * j:P * j + P], scp[:, j, :], T.ident)
                pe.matmul(T.ps[:, 0, PAST:PAST + 1], pn[:].rearrange("p c n -> p (c n)"), T.con[:, C_ONE:C_ONE + 1],
                          start=True, stop=True).then_inc(t_made, 1)
                pe.wait_ge(wc_done, 1)
                for j in range(PAGES):
                    ins = pe.transpose(T.ps[:, 1, P * j:P * j + P], s[:, P * j:P * j + P], T.ident)
                ins.then_inc(p_turned, 1)
                pe.matmul(T.ps[:, 2, 0:J], wcol[:], pair[:], start=True, stop=True).then_inc(wn_made, 1)

        with nc.Block() as block:
            @block.sync
            def _(sp):
                with sp.Fori(0, B // 2) as i:
                    for r in range(2):
                        sp.wait_ge(o_made[r], i)
                        load_page(sp, cache_v, page[:, r], 2 * i + r, v_in[r])

            @block.vector
            def _(dve):
                dve.tensor_copy(wb[:], wk[:].rearrange("p j (h b) -> p b j h", b=B)).then_inc(wb_done, 1)
                with dve.Fori(0, B // 2) as i:
                    for r in range(2):
                        dve.wait_ge(o_made[r], i + 1)
                        dve.tensor_copy(av[:, :, bass.ds(2 * i + r, 1)].rearrange("p h a -> p (h a)"),
                                        T.ps[:, 3 + r, 0:H]).then_inc(o_moved[r], 1)

            @block.tensor
            def _(pe):
                pe.wait_ge(wb_done, 1)
                with pe.Fori(0, B // 2) as i:
                    for r in range(2):
                        b = 2 * i + r
                        pe.wait_ge(v_in[r], 16 * PAGES * i + 16 * PAGES)
                        pe.wait_ge(o_moved[r], i)
                        for h in range(H):
                            for j in range(PAGES):
                                ins = pe.matmul(T.ps[:, 3 + r, h:h + 1], page[:, r, j, P * h:P * h + P],
                                                wb[:, bass.ds(b, 1), j, h:h + 1].rearrange("p a n -> p (a n)"),
                                                start=j == 0, stop=j == PAGES - 1)
                        ins.then_inc(o_made[r], 1)

        with nc.Block() as block:
            @block.vector
            def _(dve):
                steps = Steps(dve, own2)
                a = av[:].rearrange("p h b -> p (h b)")
                v = xs[:, 2 * H:3 * H, :].rearrange("p h b -> p (h b)")
                steps.done(dve.tensor_tensor(sq[:], v, T.ps[:, 2, 0:J], ALU.mult))
                steps.done(dve.tensor_tensor(a, a, sq[:], ALU.add))
                steps.done(dve.tensor_tensor(sq[:], a, a, ALU.mult))
                dve.wait_ge(rooted, 1)
                steps.done(dve.tensor_tensor(sq[:], a, rs[:], ALU.mult))
                dve.tensor_scalar(T.acc[:, :, PROMPT:TOK], sq[:].rearrange("p (h b) -> p h b", h=H), subln_cols, None,
                                  ALU.mult)

            @block.tensor
            def _(pe):
                pe.wait_ge(own2, 3)
                pe.matmul(T.ps[:, 4, 0:J], T.con[:, C_ONE:C_ONE + P], sq[:], start=True, stop=True).then_inc(ss_made, 1)

            @block.scalar
            def _(act):
                steps = Steps(act, act_own)
                act.wait_ge(ss_made, 1)
                rsqrt_of(act, steps, rs[:], T.ps[:, 4, 0:J], 1.0 / P, T.eps[:]).then_inc(rooted, 1)


def mixer_odd(nc, T, proj, ins, outs, consts):
    with ExitStack() as ctx:
        nlam = ctx.enter_context(nc.sbuf_tensor("nlam", [P, 1], F32))
        cols = ctx.enter_context(nc.sbuf_tensor("subln_cols", [P, 1], F32))
        rows = ctx.enter_context(nc.sbuf_tensor("subln_rows", [P, P], F32))
        stage_lambda(nc, T, nlam[:], cols[:], rows[:], ins["c_lambda"][0], ins["c_subln"][0])
        with split_weights(nc, T, "scores"):
            stage_attention(nc, T, proj, consts, nlam[:], rows[:],
                            outs["k_prompt"][0, 0].rearrange("t h c d -> t (h c d)"),
                            outs["v_prompt"][0, 0].rearrange("t h d -> t (h d)"))
        stage_attention_sample(nc, T, proj, consts, nlam[:], cols[:],
                               ins["cache_k"][0].rearrange("n t h c d -> n t (h c d)"),
                               ins["cache_v"][0].rearrange("n t h d -> n t (h d)"), ins["page_table"],
                               outs["k_sample"][0, :, 0].rearrange("b h c d -> b (h c d)"),
                               outs["v_sample"][0, :, 0].rearrange("b h d -> b (h d)"))


def stage_output(nc, T, y_prompt, y_sample):
    with ExitStack() as ctx:
        sb = lambda n, s, d=F32: ctx.enter_context(nc.sbuf_tensor("out_" + n, s, d))
        sem = lambda n: nc.alloc_semaphore("out_" + n)
        y, ys = sb("y", [P, 2, D]), sb("ys", [SAMPLES, D])
        turned, moved, stored, s_stored = sem("turned"), sem("moved"), [sem("stored0"), sem("stored1")], sem("s_stored")
        dst = y_prompt.rearrange("b (t p) d -> (b t) p d", p=P)
        with nc.Block() as block:
            @block.tensor
            def _(pe):
                for t in range(NCHUNK):
                    if t >= 2:
                        pe.wait_ge(moved, t - 1)
                    for k in range(KD):
                        ins = pe.transpose(T.ps[:, 2 * (t % 2) + k // 4, P * (k % 4):P * (k % 4) + P],
                                           T.acc[:, k, P * t:P * t + P], T.ident)
                    ins.then_inc(turned, 1)
                for k in range(KD):
                    ins = pe.transpose(T.ps[0:SAMPLES, 4 + k // 4, P * (k % 4):P * (k % 4) + P],
                                       T.acc[:, k, PROMPT:TOK], T.ident)
                ins.then_inc(turned, 1)

            @block.vector
            def _(dve):
                for t in range(NCHUNK):
                    dve.wait_ge(turned, t + 1)
                    if t >= 2:
                        dve.wait_ge(stored[t % 2], 16 * (t // 2))
                    dve.tensor_copy(y[:, t % 2, :], T.ps[:, 2 * (t % 2):2 * (t % 2) + 2, :].rearrange("p b n -> p (b n)")
                                    ).then_inc(moved, 1)
                dve.wait_ge(turned, NCHUNK + 1)
                dve.tensor_copy(ys[:], T.ps[0:SAMPLES, 4:6, :].rearrange("p b n -> p (b n)")).then_inc(moved, 1)

            @block.sync
            def _(sp):
                for t in range(NCHUNK):
                    sp.wait_ge(moved, t + 1)
                    sp.dma_start(dst[t], y[:, t % 2, :]).then_inc(stored[t % 2], 16)
                sp.wait_ge(moved, NCHUNK + 1)
                sp.dma_start(y_sample.rearrange("b s d -> (b s) d"), ys[:]).then_inc(s_stored, 16)
                for r in range(2):
                    sp.wait_ge(stored[r], 16 * NCHUNK // 2)
                sp.wait_ge(s_stored, 16)


def trunk_step(nc, ins, outs, consts):
    x_t = nc.dram_tensor("x_scratch", [D, TOK], F32, kind="Internal").ap()
    proj0 = nc.dram_tensor("proj_even", [25 * P, TOK], F32, kind="Internal").ap()
    proj1 = nc.dram_tensor("proj_odd", [24 * P, TOK], F32, kind="Internal").ap()
    with ExitStack() as ctx:
        T = open_trunk(nc, ctx)
        with nc.cleanup_on_exit():
            stage_load_x(nc, T, ins["x_prompt"], ins["x_sample"],
                         [ins[n] for n in ("norm_mix_pre", "norm_mix_post", "norm_ffn_pre", "norm_ffn_post")], consts)
        for layer in range(2):
            with nc.cleanup_on_exit():
                with split_weights(nc, T, f"in{layer}"), split_pair(nc, T, f"mix_in{layer}"):
                    feed = projection_feed(nc, T, f"in{layer}", ins["w_in_even" if layer == 0 else "w_in_odd"][0])
                    stage_norm(nc, T, f"nm{layer}", (None, 6)[layer], x_t, feed)
                    source = StageInput(nc, T, f"h{layer}", layer)
                    if layer == 0:
                        conv = QkvConv(ins["b_conv_w"][0], ins["state_gdn_conv"][0], outs["gdn_conv_prompt"][0],
                                       outs["gdn_conv_sample"][0])
                        stage_project(nc, T, "pe", source, feed, 24, proj0, tail=24 * P, conv=conv)
                    else:
                        stage_project(nc, T, "po", source, feed, 24, proj1)
            with nc.cleanup_on_exit():
                if layer == 0:
                    mixer_even(nc, T, proj0, ins, outs, consts)
                else:
                    mixer_odd(nc, T, proj1, ins, outs, consts)
            with nc.cleanup_on_exit(), split_weights(nc, T, f"rest{layer}"):
                with split_pair(nc, T, f"mix_out{layer}"):
                    feed = projection_feed(nc, T, f"out{layer}", ins["w_out_even" if layer == 0 else "w_out_odd"][0])
                    stage_project(nc, T, f"po{layer}_", StageInput(nc, T, f"mix{layer}"), feed, 8)
                with split_pair(nc, T, f"ffn_in{layer}"):
                    feed = ffn_feed(nc, T, f"ffn{layer}w", ins["w_ffn_gate"][layer], ins["w_ffn_up"][layer])
                    stage_norm(nc, T, f"nf{layer}", 2 + layer, x_t, feed)
                    source = StageInput(nc, T, f"hf{layer}", 4 + layer)
                    stage_ffn(nc, T, f"ffn{layer}", source, feed, layer, ins["w_ffn_down"][layer], ins["w_ffn_conv"][layer],
                              ins["b_ffn_conv"][layer:layer + 1], ins["state_ffn_conv"], outs["ffn_conv_prompt"],
                              outs["ffn_conv_sample"])
        stage_norm(nc, T, "nl", 7, x_t)
        stage_output(nc, T, outs["y_prompt"], outs["y_sample"])


_INS = ["x_prompt", "x_sample", "cache_k", "cache_v", "page_table", "state_gdn", "state_gdn_conv", "state_ffn_conv",
        "norm_mix_pre", "norm_mix_post", "norm_ffn_pre", "norm_ffn_post", "w_in_even", "a_v_norm", "a_w_s", "a_b_s",
        "b_conv_w", "b_a_log", "b_dt_bias", "b_out_norm", "w_out_even", "w_in_odd", "c_lambda", "c_subln",
        "w_out_odd", "w_ffn_gate", "w_ffn_up", "w_ffn_conv", "b_ffn_conv", "w_ffn_down"]
_OUTS = [("y_prompt", (1, PROMPT, D)), ("y_sample", (SAMPLES, 1, D)),
         ("gdn_state_prompt", (1, 1, HEADS_B, P, P)), ("gdn_state_sample", (1, SAMPLES, HEADS_B, P, P)),
         ("gdn_conv_prompt", (1, 1, 3, 12 * P)), ("gdn_conv_sample", (1, SAMPLES, 3, 12 * P)),
         ("chunk_v", (1, SAMPLES, 1, 4 * P)),
         ("k_prompt", (1, 1, PROMPT, HEADS_C, 2, 64)), ("v_prompt", (1, 1, PROMPT, HEADS_C, P)),
         ("k_sample", (1, SAMPLES, 1, HEADS_C, 2, 64)), ("v_sample", (1, SAMPLES, 1, HEADS_C, P)),
         ("ffn_conv_prompt", (2, 1, 2, FF)), ("ffn_conv_sample", (2, SAMPLES, 2, FF))]


def kernel(**inputs):
    import concourse.bacc as _bacc
    from concourse.bass_utils import run_bass_kernel_spmd as _run

    nc = _bacc.Bacc("TRN2", target_bir_lowering=False, num_devices=1)
    arrays, ins, outs = {}, {}, {}
    for name in _INS:
        a = np.ascontiguousarray(inputs[name])
        arrays[f"in_{name}"] = a
        ins[name] = nc.dram_tensor(f"in_{name}", a.shape, mybir.dt.from_np(a.dtype), kind="ExternalInput").ap()
    arrays["in_constants"] = shape_constants()
    consts = nc.dram_tensor("in_constants", [P, C_END], F32, kind="ExternalInput").ap()
    for name, shape in _OUTS:
        outs[name] = nc.dram_tensor(f"out_{name}", shape, F32, kind="ExternalOutput").ap()
    trunk_step(nc, ins, outs, consts)
    r = _run(nc, [arrays], core_ids=[0])
    return tuple(r.results[0][f"out_{name}"] for name, _ in _OUTS)
```

```python
import math
from contextlib import ExitStack

import numpy as np

import concourse.bass as bass
from concourse import mybir

ALU = mybir.AluOpType
ACT = mybir.ActivationFunctionType
F32 = mybir.dt.float32
F32R = mybir.dt.float32r
I32 = mybir.dt.int32
AX_X = mybir.AxisListType.X

P = 128
D = 1024
KD = D // P
PROMPT = 1024
SAMPLES = 8
TOK = PROMPT + SAMPLES
CH = TOK // 3
NCHUNK = PROMPT // P
FF = 2816
FT = FF // P
GROUPS = FT // 2
HEADS_B = 4
HEADS_C = 8
EPS = 1e-6
MASKED = -1e30
PAGES = 2
PAST = PAGES * P
LAM_INIT = 0.8 - 0.6 * math.exp(-0.3)

C_ID, C_INCL, C_STRICT, C_ONE = 0, 128, 256, 384
C_LEVEL = 512
C_SEL = C_LEVEL + 7 * 128
C_RESET = C_SEL + 8 * 128
C_DIST = C_RESET + PROMPT
C_SLOPE = C_DIST + PROMPT
C_SBIAS = C_SLOPE + HEADS_C
C_PAIR = C_SBIAS + PAST + 1
C_HALF = C_PAIR + 64
C_END = C_HALF + 2


def shape_constants():
    c = np.zeros((P, C_END), np.float32)
    i = np.arange(P)
    c[:, C_ID:C_ID + P] = np.eye(P)
    c[:, C_INCL:C_INCL + P] = i[:, None] <= i[None, :]
    c[:, C_STRICT:C_STRICT + P] = i[:, None] < i[None, :]
    c[:, C_ONE:C_ONE + P] = 1.0
    for n, s in enumerate((1, 2, 4, 8, 16, 32, 64)):
        col, row = i[:, None] // s, i[None, :] // s
        c[:, C_LEVEL + n * P:C_LEVEL + (n + 1) * P] = (row % 2 == 1) & (col == row - 1)
    for n in range(8):
        c[n if n < 4 else 32 + n - 4, C_SEL + n * P:C_SEL + (n + 1) * P] = 1.0
    c[:, C_RESET:C_RESET + PROMPT] = np.arange(PROMPT) % P != 0
    dist = (np.arange(PROMPT) - (PROMPT - P))[None, :] - i[:, None]
    c[:, C_DIST:C_DIST + PROMPT] = np.where(dist <= 0, dist, MASKED)
    slopes = np.exp2(-8.0 * np.arange(1, HEADS_C + 1, dtype=np.float32) / HEADS_C).astype(np.float32)
    c[:, C_SLOPE:C_SLOPE + HEADS_C] = slopes
    head = (i // SAMPLES) % HEADS_C
    c[:, C_SBIAS:C_SBIAS + PAST + 1] = slopes[head][:, None] * (np.arange(PAST + 1) - PAST)[None, :]
    c[:, C_PAIR:C_PAIR + 64] = (i % 64)[:, None] == np.arange(64)[None, :]
    c[:64, C_HALF] = 1.0
    c[64:, C_HALF + 1] = 1.0
    return c


class Steps:

    def __init__(self, eng, sem, base=0):
        self.eng, self.sem, self.base, self.n = eng, sem, base, 0

    def note(self, ins):
        ins.then_inc(self.sem, 1)
        self.n += 1
        return self.base + self.n

    def done(self, ins):
        self.eng.wait_ge(self.sem, self.note(ins))


class Trunk:
    pass


def one(t, i):
    if isinstance(i, int):
        return t[:, i, :]
    return t[:, bass.ds(i, 1), :].rearrange("p a w -> p (a w)")


def region(ps, r):
    return ps[:, 3 * r:3 * r + 3, 0:CH]


def chunks(ap):
    return ap.rearrange("p (c n) -> p c n", c=3)


def product(pe, ps, r, wh, wl, hh, hl, first, last):
    for n, (w, h) in enumerate(((wh, hh), (wh, hl), (wl, hh))):
        for c in range(3):
            ins = pe.matmul(ps[:, 3 * r + c, 0:CH], w, h[:, c * CH:(c + 1) * CH],
                            start=first and n == 0, stop=last and n == 2)
    return ins


def ones_times(pe, T, r, src, first=True, last=True):
    for c in range(3):
        ins = pe.matmul(T.ps[:, 3 * r + c, 0:CH], T.con[:, C_ONE:C_ONE + P], src[:, c * CH:(c + 1) * CH],
                        start=first, stop=last)
    return ins


def rsqrt_of(act, steps, out, sums, scale, eps_col):
    steps.done(act.activation(out, sums, ACT.Ln, scale=scale, bias=eps_col))
    return act.activation(out, out, ACT.Exp, scale=-0.5)


class TileSquares:

    def __init__(self, sem, T, bufs):
        self.T, self.bufs = T, bufs
        self.squared, self.summed = [sem("squared0"), sem("squared1")], [sem("summed0"), sem("summed1")]

    def scalar(self, act, m, n, r):
        act.wait_ge(self.summed[r], n)
        act.activation(self.bufs[r], one(self.T.acc, m), ACT.Square).then_inc(self.squared[r], 1)

    def gpsimd(self, pool, n, r, own):
        pool.wait_ge(self.squared[r], n + 1)
        own()
        pool.tensor_tensor(self.T.sqsum[:], self.T.sqsum[:], self.bufs[r], ALU.add).then_inc(self.summed[r], 1)


def stage_load_x(nc, T, x_prompt, x_sample, gains, consts):
    with ExitStack() as ctx:
        sb = lambda n, s, d=F32: ctx.enter_context(nc.sbuf_tensor("ld_" + n, s, d))
        sem = lambda n: nc.alloc_semaphore("ld_" + n)
        R = 4
        xin, xs, grow = sb("xin", [P, R, D]), sb("xs", [SAMPLES, D]), sb("grow", [8, D])
        const_in, small_in, landed = sem("const_in"), sem("small_in"), [sem(f"landed{r}") for r in range(R)]
        turned, moved = ([sem(f"{n}{r}") for r in range(R)] for n in ("turned", "moved"))
        small_turned, prepared = sem("small_turned"), sem("prepared")
        src = x_prompt.rearrange("b (t p) d -> (b t) p d", p=P)
        with nc.Block() as block:
            @block.sync
            def _(sp):
                sp.dma_start(T.con[:], consts[:, 0:512]).then_inc(const_in, 16)
                with sp.Fori(0, NCHUNK // R) as i:
                    for r in range(R):
                        sp.wait_ge(turned[r], i)
                        sp.dma_start(xin[:, r, :], src[bass.ds(R * i + r, 1), :, :].rearrange("a p d -> p (a d)")
                                     ).then_inc(landed[r], 16)
                sp.dma_start(xs[:], x_sample.rearrange("b s d -> (b s) d")).then_inc(small_in, 16)
                for n, g in enumerate(gains):
                    sp.dma_start(grow[2 * n:2 * n + 2, :], g).then_inc(small_in, 16)

            @block.tensor
            def _(pe):
                pe.wait_ge(const_in, 16)
                with pe.Fori(0, NCHUNK // R) as i:
                    for r in range(R):
                        pe.wait_ge(landed[r], 16 * i + 16)
                        pe.wait_ge(moved[r], i)
                        for k in range(KD):
                            ins = pe.transpose(T.ps[:, 2 * r + k // 4, P * (k % 4):P * (k % 4) + P],
                                               xin[:, r, P * k:P * k + P], T.ident)
                        ins.then_inc(turned[r], 1)
                pe.wait_ge(small_in, 16 * (1 + len(gains)))
                pe.wait_ge(moved[R - 1], NCHUNK // R)
                for k in range(KD):
                    pe.transpose(T.ps[:, 6, 8 * k:8 * k + 8], xs[:, P * k:P * k + P], T.ident[0:8, 0:8])
                for k in range(KD):
                    ins = pe.transpose(T.ps[:, 7, 8 * k:8 * k + 8], grow[:, P * k:P * k + P], T.ident[0:8, 0:8])
                ins.then_inc(small_turned, 1)

            @block.vector
            def _(dve):
                with dve.Fori(0, NCHUNK // R) as i:
                    for r in range(R):
                        dve.wait_ge(turned[r], i + 1)
                        dve.tensor_copy(T.acc[:, :, bass.ds((R * i + r) * P, P)],
                                        T.ps[:, 2 * r:2 * r + 2, :].rearrange("p b (k n) -> p (b k) n", n=P)
                                        ).then_inc(moved[r], 1)
                dve.wait_ge(small_turned, 1)
                dve.tensor_copy(T.acc[:, :, PROMPT:TOK], T.ps[:, 6, 0:64].rearrange("p (k n) -> p k n", n=8))
                dve.tensor_copy(T.gain[:], T.ps[:, 7, 0:64].rearrange("p (k n) -> p k n", n=8))
                dve.wait_ge(const_in, 16)
                dve.memset(T.one[:], 1.0)
                dve.memset(T.eps[:], EPS).then_inc(prepared, 1)


class StageInput:

    def __init__(self, nc, T, name, gain_row=None):
        sem = lambda n: nc.alloc_semaphore(name + n)
        self.T, self.gain_row, self.bufs = T, gain_row, None
        self.scaled, self.hi_done = sem("scaled"), sem("hi_done")
        self.lo_done = [sem("lo_done0"), sem("lo_done1")]

    def source(self, k):
        return self.T.acc[:, k, :] if self.gain_row is None else self.bufs[k % 2]

    def scalar(self, act, k):
        if self.gain_row is not None:
            act.wait_ge(self.scaled, k + 1)
        act.activation(self.T.hh[:, k, :], self.source(k), ACT.Copy).then_inc(self.hi_done, 1)

    def lo_half(self, eng, k):
        eng.wait_ge(self.hi_done, k + 1)
        eng.tensor_tensor(self.T.hl[:, k, :], self.source(k), self.T.hh[:, k, :], ALU.subtract
                          ).then_inc(self.lo_done[k % 2], 1)

    def scale(self, dve, k):
        if k >= 2:
            dve.wait_ge(self.lo_done[k % 2], k // 2)
        dve.scalar_tensor_tensor(out=self.bufs[k % 2], in0=self.T.acc[:, k, :],
                                 scalar=self.T.gain[:, k, self.gain_row:self.gain_row + 1], in1=self.T.sqsum[:],
                                 op0=ALU.mult, op1=ALU.mult).then_inc(self.scaled, 1)

    def vector(self, dve):
        if self.gain_row is None:
            for k in range(KD):
                self.lo_half(dve, k)
        else:
            self.scale(dve, 0)
            for k in range(1, KD, 2):
                self.scale(dve, k)
                if k + 1 < KD:
                    self.scale(dve, k + 1)
                self.lo_half(dve, k)

    def gpsimd(self, pool):
        for k in range(0, KD if self.gain_row is not None else 0, 2):
            self.lo_half(pool, k)

    def ready(self, pe, k):
        pe.wait_ge(self.lo_done[k % 2], k // 2 + 1)


def stage_norm(nc, T, name, post_row, x_scratch, feed):
    with ExitStack() as ctx:
        sb = lambda n, s, d=F32: ctx.enter_context(nc.sbuf_tensor(name + n, s, d))
        sem = lambda n: nc.alloc_semaphore(name + n)
        post = post_row is not None
        sq, xold, rstd = sb("sq", [P, 2, TOK]), sb("xold", [P, 4, TOK]), sb("rstd", [P, TOK])
        root1, normed, act_own = sem("root1"), sem("normed"), sem("act_own")
        summed1, squared, summed2 = sem("summed1"), sem("squared"), sem("summed2")
        x_in = [sem(f"x_in{n}") for n in range(4)]
        x_new, x_out, dve_own = sem("x_new"), sem("x_out"), sem("dve_own")
        xs = x_scratch.rearrange("(k p) n -> k p n", p=P)
        with nc.Block() as block:
            @block.sync
            def _(sp):
                for k in range(KD if post else 0):
                    if k >= 4:
                        sp.wait_ge(x_new, k - 3)
                    sp.dma_start(xold[:, k % 4, :], xs[k]).then_inc(x_in[k % 4], 16)
                    if k == 3:
                        feed.first_sync(sp)
                if not post:
                    feed.first_sync(sp)
                for k in range(KD):
                    if post:
                        sp.wait_ge(x_new, k + 1)
                    sp.dma_start(xs[k], T.acc[:, k, :]).then_inc(x_out, 16)
                sp.wait_ge(x_out, 16 * KD)

            @block.scalar
            def _(act):
                steps = Steps(act, act_own)
                if post:
                    act.wait_ge(summed1, 1)
                    rsqrt_of(act, steps, chunks(rstd[:]), region(T.ps, 0), 1.0 / D, T.eps[:]).then_inc(root1, 1)
                for k in range(KD):
                    if k >= KD - feed.SLOTS:
                        feed.hi_half(act, k - (KD - feed.SLOTS), 0)
                    if post:
                        act.wait_ge(x_new, k + 1)
                    if k >= 2:
                        act.wait_ge(summed2, k - 1)
                    act.activation(sq[:, k % 2, :], T.acc[:, k, :], ACT.Square).then_inc(squared, 1)
                act.wait_ge(summed2, KD)
                rsqrt_of(act, steps, chunks(T.sqsum[:]), region(T.ps, 1), 1.0 / D, T.eps[:])

            @block.vector
            def _(dve):
                steps = Steps(dve, dve_own)

                if post:
                    dve.wait_ge(root1, 1)
                    for k in range(KD):
                        if k % 2 == 0:
                            steps.done(dve.tensor_tensor(T.acc[:, k, :], T.acc[:, k, :], rstd[:], ALU.mult))
                        else:
                            dve.wait_ge(normed, k // 2 + 1)
                        dve.wait_ge(x_in[k % 4], 16 * (k // 4 + 1))
                        dve.scalar_tensor_tensor(out=T.acc[:, k, :], in0=T.acc[:, k, :],
                                                 scalar=T.gain[:, k, post_row:post_row + 1],
                                                 in1=xold[:, k % 4, :], op0=ALU.mult, op1=ALU.add).then_inc(x_new, 1)

            @block.gpsimd
            def _(pool):
                if post:
                    pool.wait_ge(root1, 1)
                    for k in range(1, KD, 2):
                        pool.tensor_tensor(T.acc[:, k, :], T.acc[:, k, :], rstd[:], ALU.mult).then_inc(normed, 1)
                feed.first_gpsimd(pool)

            @block.tensor
            def _(pe):
                if post:
                    ones_times(pe, T, 0, T.sqsum[:]).then_inc(summed1, 1)
                for k in range(KD):
                    pe.wait_ge(squared, k + 1)
                    ones_times(pe, T, 1, sq[:, k % 2, :], k == 0, k == KD - 1).then_inc(summed2, 1)


class WeightFeed:
    SLOTS = 4

    def __init__(self, nc, T, name, matrices, column, buf, half):
        sem = lambda n: nc.alloc_semaphore(name + n)
        self.landed = [sem(f"landed{b}") for b in range(2)]
        self.hi, self.lo, self.made = ([sem(f"{n}{j}") for j in range(self.SLOTS)] for n in ("hi", "lo", "made"))
        self.raw = [T.wraw[:, 2048 * b:2048 * b + 2048].rearrange("p (k n) -> p k n", k=KD) for b in range(2)]
        self.slot_h, self.slot_l = ([t[:, 1024 * j:1024 * j + 1024].rearrange("p (k n) -> p k n", k=KD)
                                     for j in range(self.SLOTS)] for t in (T.wh, T.wl))
        self.w = [m.rearrange("(k p) m -> p k m", p=P) for m in matrices]
        self.column, self.buf, self.half = column, buf, half
        self.users = [[j for j in range(self.SLOTS) if buf(j) == b] for b in range(2)]

    def source(self, j):
        return self.raw[self.buf(j)][:, :, P * self.half(j):P * self.half(j) + P]

    def load(self, sp, i):
        for b in range(2):
            for j in self.users[b]:
                sp.wait_ge(self.lo[j], i)
            sp.dma_start(self.raw[b], self.w[b][:, :, bass.ds(self.column(b, i), 256)]).then_inc(self.landed[b], 16)

    def hi_half(self, act, j, i):
        act.wait_ge(self.landed[self.buf(j)], 16 * i + 16)
        act.wait_ge(self.made[j], i)
        act.activation(self.slot_h[j], self.source(j), ACT.Copy).then_inc(self.hi[j], 1)

    def lo_half(self, pool, j, i):
        pool.wait_ge(self.hi[j], i + 1)
        pool.tensor_tensor(self.slot_l[j], self.source(j), self.slot_h[j], ALU.subtract).then_inc(self.lo[j], 1)

    def first_sync(self, sp):
        self.load(sp, 0)

    def first_scalar(self, act):
        for j in range(self.SLOTS):
            self.hi_half(act, j, 0)

    def first_gpsimd(self, pool):
        for j in range(self.SLOTS):
            self.lo_half(pool, j, 0)


def projection_feed(nc, T, name, w):
    return WeightFeed(nc, T, name, (w, w), lambda b, i: (2 * i + b) * 256, lambda j: j // 2, lambda j: j % 2)


class QkvConv:
    TAPS, ROWS, KEEP = 4, 3 * SAMPLES + 4, 3 + SAMPLES
    FIRST, LAST = 2, 5
    BEFORE, AFTER = ACT.Gelu_apprx_tanh, ACT.Silu

    def __init__(self, w_conv, state, out_prompt, out_sample):
        self.w_conv, self.state, self.out_prompt, self.out_sample = w_conv, state, out_prompt, out_sample


def stage_project(nc, T, name, source, feed, m_tiles, out_scratch=None, tail=None, conv=None):
    BODY = 4
    n_iter = m_tiles // BODY
    c0, c1 = (conv.FIRST, conv.LAST) if conv is not None else (n_iter, n_iter)
    PAD = 3
    with ExitStack() as ctx:
        sb = lambda n, s, d=F32: ctx.enter_context(nc.sbuf_tensor(name + n, s, d))
        sem = lambda n: nc.alloc_semaphore(name + n)
        out = sb("out", [P, 2, PAD + TOK])
        squares = TileSquares(sem, T, [out[:, r, PAD:] for r in range(2)]) if out_scratch is None else None
        source.bufs = [out[:, r, PAD:] for r in range(2)]
        fed = source.gain_row is not None
        sqsum_own = sem("sqsum_own")
        hi, lo, made, slot_h, slot_l = feed.hi, feed.lo, feed.made, feed.slot_h, feed.slot_l
        moved = [sem(f"moved{j}") for j in range(BODY)]
        stored = [sem(f"stored{j}") for j in range(BODY)]
        activated = [sem(f"activated{j}") for j in range(BODY)]
        t_in, t_zero = sem("t_in"), sem("t_zero")
        traw = T.wraw[:, 4096:4096 + 1024].rearrange("p (k n) -> p k n", k=KD)
        if out_scratch is not None:
            rows = out_scratch.rearrange("(m p) n -> m p n", p=P)
        if conv is not None:
            M, ROWS, KEEP, TAPS = 3 * HEADS_B, conv.ROWS, conv.KEEP, conv.TAPS
            cv = sb("cv", [P, 2, TOK])
            prm, last = sb("prm", [P, M, ROWS]), sb("last", [P, M, KEEP])
            small_rows = cv[0:ROWS, :, :].rearrange("p a n -> p (a n)")[:, 0:M * P]
            kept_rows = T.wraw[0:KEEP, 0:M * P]
            rows_in, turned, conv_own = sem("rows_in"), sem("turned"), sem("conv_own")
            conved, silued, kept = sem("conved"), sem("silued"), sem("kept")
            k_turned, k_moved, k_out = sem("k_turned"), sem("k_moved"), sem("k_out")
            flat = T.ps[0:KEEP, 3:6, :].rearrange("r b n -> r (b n)")

        def iterations(eng, body, lag):
            for a, b in ((0, c0), (c0, c1), (c1, n_iter)):
                b = min(b, n_iter - lag)
                if b > a:
                    with eng.Fori(a + lag, b + lag) as i:
                        body(i, conv is not None and a == c0, conv is not None and a == c1)

        with nc.Block() as block:
            @block.sync
            def _(sp):
                def store(j, i, convolved, acted):
                    if out_scratch is not None:
                        if convolved:
                            sp.wait_ge(silued, BODY * (i - c0) + j + 1)
                            src = cv[:, j % 2, :]
                        elif acted is not None:
                            sp.wait_ge(activated[j], acted)
                            src = out[:, j % 2, PAD:]
                        else:
                            sp.wait_ge(moved[j], i + 1)
                            src = out[:, j % 2, PAD:]
                        sp.dma_start(rows[bass.ds(BODY * i + j, 1), :, :].rearrange("a p n -> p (a n)"), src
                                     ).then_inc(stored[j], 16)

                def iteration(i, convolved, after):
                    feed.load(sp, i)
                    for j in range(BODY):
                        store(j, i - 1, convolved, i if conv is not None else None)

                if not fed:
                    feed.first_sync(sp)
                if conv is not None:
                    n = (TAPS - 1) * SAMPLES
                    sp.dma_start(small_rows[0:n, :], conv.state.rearrange("b j c -> (b j) c")).then_inc(rows_in, 16)
                    sp.dma_start(small_rows[n:ROWS, :], conv.w_conv).then_inc(rows_in, 16)
                iterations(sp, iteration, 1)
                if tail is not None:
                    sp.wait_ge(t_zero, 1)
                    sp.dma_start(traw[:, :, 0:4], feed.w[0][:, :, tail:tail + 4]).then_inc(t_in, 16)
                    sp.dma_start(traw[:, :, 32:36], feed.w[0][:, :, tail + 4:tail + 8]).then_inc(t_in, 16)
                for j in range(BODY):
                    store(j, n_iter - 1, False, n_iter - (c1 - c0) if conv is not None else None)
                if tail is not None:
                    store(0, n_iter, False, None)
                if conv is not None:
                    sp.dma_start(conv.out_sample[:, 0:TAPS - 2, :], conv.state[:, 1:TAPS - 1, :]).then_inc(k_out, 16)
                    sp.wait_ge(k_moved, 1)
                    sp.dma_start(conv.out_prompt[0], kept_rows[0:TAPS - 1, :]).then_inc(k_out, 16)
                    sp.dma_start(conv.out_sample[:, TAPS - 2, :], kept_rows[TAPS - 1:KEEP, :]).then_inc(k_out, 16)
                    sp.wait_ge(k_out, 48)
                if out_scratch is not None:
                    for j in range(BODY):
                        sp.wait_ge(stored[j], 16 * (n_iter + (tail is not None and j == 0)))

            @block.gpsimd
            def _(pool):
                def add(j, i):
                    squares.gpsimd(pool, 2 * i + j // 2, j % 2, lambda: pool.wait_ge(sqsum_own, BODY * i + j + 1))
                    pool.wait_ge(squares.summed[j % 2], 2 * i + j // 2 + 1)
                    pool.sem_inc(sqsum_own, 1)

                def keep(j, i):
                    pool.wait_ge(moved[j], i + 1)
                    pool.tensor_copy(last[:, bass.ds(BODY * (i - c0) + j, 1), :].rearrange("p a n -> p (a n)"),
                                     out[:, j % 2, PROMPT:PAD + TOK]).then_inc(kept, 1)

                def iteration(i, convolved, after):
                    for j in range(BODY):
                        feed.lo_half(pool, j, i)
                        if squares is not None:
                            add(j, i - 1)
                        if convolved:
                            keep(j, i - 1)

                if not fed:
                    feed.first_gpsimd(pool)
                source.gpsimd(pool)
                if tail is not None:
                    pool.memset(traw, 0.0).then_inc(t_zero, 1)
                if squares is not None:
                    pool.memset(T.sqsum[:], 0.0).then_inc(sqsum_own, 1)
                iterations(pool, iteration, 1)
                if squares is not None:
                    for j in range(BODY):
                        add(j, n_iter - 1)
                if tail is not None:
                    pool.wait_ge(hi[0], n_iter + 1)
                    pool.tensor_tensor(slot_l[0], traw, slot_h[0], ALU.subtract).then_inc(lo[0], 1)

            @block.scalar
            def _(act):
                def activate(j, i, function):
                    act.wait_ge(moved[j], i + 1)
                    x = out[:, j % 2, PAD:]
                    act.activation(x, x, function).then_inc(activated[j], 1)

                def square(j, i):
                    act.wait_ge(moved[j], i + 1)
                    squares.scalar(act, BODY * i + j, 2 * i + j // 2, j % 2)

                def iteration(i, convolved, after):
                    for j in range(BODY):
                        feed.hi_half(act, j, i)
                        if squares is not None:
                            square(j, i - 1)
                        if convolved:
                            act.wait_ge(conved, BODY * (i - 1 - c0) + j + 1)
                            act.activation(cv[:, j % 2, :], cv[:, j % 2, :], ACT.Silu).then_inc(silued, 1)
                        elif conv is not None:
                            activate(j, i - 1, conv.BEFORE)

                for k in range(KD):
                    source.scalar(act, k)
                    if not fed and k >= KD - feed.SLOTS:
                        feed.hi_half(act, k - (KD - feed.SLOTS), 0)
                iterations(act, iteration, 1)
                if squares is not None:
                    for j in range(BODY):
                        square(j, n_iter - 1)
                for j in range(BODY):
                    if conv is not None:
                        activate(j, n_iter - 1, conv.AFTER)
                    if tail is not None and j == 0:
                        act.wait_ge(t_in, 32)
                        act.wait_ge(made[0], n_iter)
                        act.activation(slot_h[0], traw, ACT.Copy).then_inc(hi[0], 1)

            @block.tensor
            def _(pe):
                def tile(j, i):
                    pe.wait_ge(lo[j], i + 1)
                    if j >= 2:
                        pe.wait_ge(moved[j - 2], i + 1)
                    else:
                        pe.wait_ge(moved[j + 2], i)
                    for k in range(KD):
                        if j == 0:
                            source.ready(pe, k)
                        ins = product(pe, T.ps, j % 2, slot_h[j][:, k, :], slot_l[j][:, k, :],
                                      T.hh[:, k, :], T.hl[:, k, :], k == 0, k == KD - 1)
                    ins.then_inc(made[j], 1)

                if conv is not None:
                    pe.wait_ge(rows_in, 32)
                    for t in range(M):
                        ins = pe.transpose(T.ps[:, 6, ROWS * t:ROWS * t + ROWS], small_rows[:, P * t:P * t + P],
                                           T.ident[0:ROWS, 0:ROWS])
                    ins.then_inc(turned, 1)
                with pe.Fori(0, n_iter) as i:
                    for j in range(BODY):
                        tile(j, i)
                if tail is not None:
                    tile(0, n_iter)
                if conv is not None:
                    pe.wait_ge(kept, M)
                    pe.wait_ge(moved[3], n_iter)
                    for t in range(M):
                        ins = pe.transpose(flat[:, P * t:P * t + P], last[:, t, :], T.ident)
                    ins.then_inc(k_turned, 1)

            @block.vector
            def _(dve):
                def move(j, i):
                    dve.wait_ge(made[j], i + 1)
                    if out_scratch is None:
                        dst = one(T.acc, BODY * i + j)
                    else:
                        dst = out[:, j % 2, PAD:]
                        if j >= 2:
                            dve.wait_ge(stored[j - 2], 16 * i + 16)
                        else:
                            dve.wait_ge(stored[j + 2], 16 * i)
                    dve.tensor_copy(chunks(dst), region(T.ps, j % 2)).then_inc(moved[j], 1)

                def convolve(steps, j, i):
                    m = BODY * (i - c0) + j
                    tap = [prm[:, bass.ds(m, 1), ROWS - TAPS + n:ROWS - TAPS + n + 1].rearrange("p a n -> p (a n)")
                           for n in range(TAPS)]
                    st = [prm[:, bass.ds(m, 1), n:ROWS - TAPS:TAPS - 1].rearrange("p a b -> p (a b)")
                          for n in range(TAPS - 1)]
                    pv, sv = cv[:, j % 2, 0:PROMPT], cv[:, j % 2, PROMPT:TOK]
                    dve.wait_ge(moved[j], i + 1)
                    steps.note(dve.tensor_scalar(pv, out[:, j % 2, 0:PROMPT], tap[0], None, ALU.mult))
                    steps.done(dve.tensor_scalar(sv, st[0], tap[0], None, ALU.mult))
                    for n in range(1, TAPS - 1):
                        steps.note(dve.scalar_tensor_tensor(out=pv, in0=out[:, j % 2, n:n + PROMPT], scalar=tap[n],
                                                            in1=pv, op0=ALU.mult, op1=ALU.add))
                        steps.done(dve.scalar_tensor_tensor(out=sv, in0=st[n], scalar=tap[n], in1=sv,
                                                            op0=ALU.mult, op1=ALU.add))
                    dve.scalar_tensor_tensor(out=cv[:, j % 2, :], in0=out[:, j % 2, PAD:], scalar=tap[TAPS - 1],
                                             in1=cv[:, j % 2, :], op0=ALU.mult, op1=ALU.add).then_inc(conved, 1)

                def iteration(i, convolving, after):
                    steps = Steps(dve, conv_own, 24 * (i - c0)) if convolving else None
                    for j in range(BODY):
                        if convolving:
                            dve.wait_ge(kept, BODY * (i - c0) + max(j - 1, 0))
                        elif after:
                            dve.wait_ge(kept, M)
                        move(j, i)
                        if convolving:
                            convolve(steps, j, i)

                source.vector(dve)
                dve.wait_ge(source.lo_done[0], KD // 2)
                if conv is not None:
                    dve.memset(out[:, :, 0:PAD], 0.0)
                    dve.wait_ge(turned, 1)
                    dve.tensor_copy(prm[:], T.ps[:, 6, 0:M * ROWS].rearrange("p (t r) -> p t r", r=ROWS))
                iterations(dve, iteration, 0)
                if tail is not None:
                    move(0, n_iter)
                if conv is not None:
                    dve.wait_ge(k_turned, 1)
                    dve.tensor_copy(kept_rows, flat[:, 0:M * P]).then_inc(k_moved, 1)


def ffn_feed(nc, T, name, w_gate, w_up):
    return WeightFeed(nc, T, name, (w_gate, w_up), lambda b, g: 256 * g, lambda j: j % 2, lambda j: j // 2)


def stage_ffn(nc, T, name, source, feed, layer, w_down, w_conv, b_conv, state, out_prompt, out_sample):
    ROWS = 2 * SAMPLES + 4
    with ExitStack() as ctx:
        sb = lambda n, s, d=F32: ctx.enter_context(nc.sbuf_tensor(name + n, s, d))
        sem = lambda n: nc.alloc_semaphore(name + n)
        raw_d = T.wraw[:, 4096:6144]
        slot_h, slot_l, lo, made = feed.slot_h, feed.slot_l, feed.lo, feed.made
        down_h, down_l = T.wh[:, 4096:6144], T.wl[:, 4096:6144]
        prm = sb("prm", [P, FT, ROWS])
        last = sb("last", [P, FT, 2 + SAMPLES])
        ah, al = sb("ah", [P, 2, TOK], F32R), sb("al", [P, 2, TOK], F32R)
        gate, conv = sb("gate", [P, 2 + TOK]), sb("conv", [P, TOK])
        rows_in, turned, prm_done = sem("rows_in"), sem("turned"), sem("prm_done")
        in_d = sem("in_d")
        hi_d, lo_d, made_d = sem("hi_d"), sem("lo_d"), sem("made_d")
        gate_in, conved, activated = sem("gate_in"), sem("conved"), sem("activated")
        multiplied, collected, acc_zero = sem("multiplied"), sem("collected"), sem("acc_zero")
        kept, a_ready, dve_own = sem("kept"), sem("a_ready"), sem("dve_own")
        out_done, keep_turned, keep_moved = sem("out_done"), sem("keep_turned"), sem("keep_moved")
        squares, sqsum_own = TileSquares(sem, T, [gate[:, 2:2 + TOK], conv[:]]), sem("sqsum_own")
        wd = w_down.rearrange("(g j p) m -> g p j m", p=P, j=2)
        KEEP = 2 + SAMPLES
        flat, kept_rows = T.ps[0:KEEP, 0:6, :].rearrange("r b n -> r (b n)"), T.wraw[0:KEEP, 0:FF]
        source.bufs = [gate[:, 2:2 + TOK], conv[:]]
        rows = ((slice(0, 2048), raw_d[0:ROWS, :]), (slice(2048, FF), sb("more_rows", [ROWS, FF - 2048])[:]))

        with nc.Block() as block:
            @block.sync
            def _(sp):
                def load_d(g):
                    sp.wait_ge(lo_d, g)
                    sp.dma_start(raw_d.rearrange("p (j m) -> p j m", j=2),
                                 wd[bass.ds(g, 1), :, :, :].rearrange("a p j m -> p (a j) m")).then_inc(in_d, 16)

                for cols, dst in rows:
                    for first, src in ((0, state[layer].rearrange("b j c -> (b j) c")), (2 * SAMPLES, w_conv),
                                       (2 * SAMPLES + 3, b_conv)):
                        sp.dma_start(dst[first:first + src.shape[0], :], src[:, cols]).then_inc(rows_in, 16)
                sp.dma_start(out_sample[layer, :, 0, :], state[layer, :, 1, :]).then_inc(out_done, 16)
                sp.wait_ge(turned, 1)
                with sp.Fori(0, GROUPS - 1) as g:
                    load_d(g)
                    feed.load(sp, g + 1)
                load_d(GROUPS - 1)
                sp.wait_ge(keep_moved, 1)
                sp.dma_start(out_prompt[layer, 0], kept_rows[0:2, :]).then_inc(out_done, 16)
                sp.dma_start(out_sample[layer, :, 1, :], kept_rows[2:KEEP, :]).then_inc(out_done, 16)
                sp.wait_ge(out_done, 48)

            @block.scalar
            def _(act):
                def split(s, g):
                    feed.hi_half(act, s, g)

                def tile(t, g):
                    act.wait_ge(made[2 * t], g + 1)
                    act.wait_ge(kept, 2 * g + t)
                    act.wait_ge(conved, 2 * g + t)
                    act.activation(chunks(gate[:, 2:2 + TOK]), region(T.ps, 0), ACT.Copy).then_inc(gate_in, 1)

                def gelu(t, g):
                    act.wait_ge(conved, 2 * g + t + 1)
                    act.activation(conv[:], conv[:], ACT.Gelu_apprx_tanh,
                                   bias=prm[:, bass.ds(2 * g + t, 1), ROWS - 1:ROWS].rearrange("p a n -> p (a n)")
                                   ).then_inc(activated, 1)

                def split_down(g):
                    act.wait_ge(in_d, 16 * g + 16)
                    act.wait_ge(made_d, KD * g)
                    act.activation(down_h, raw_d, ACT.Copy).then_inc(hi_d, 1)

                def group(g, more):
                    tile(0, g)
                    if more:
                        split(0, g + 1)
                    gelu(0, g)
                    if more:
                        split(1, g + 1)
                    split_down(g)
                    tile(1, g)
                    if more:
                        split(2, g + 1)
                    gelu(1, g)
                    if more:
                        split(3, g + 1)

                for k in range(KD):
                    source.scalar(act, k)
                with act.Fori(0, GROUPS - 1) as g:
                    group(g, True)
                group(GROUPS - 1, False)
                act.wait_ge(kept, 2 * GROUPS)
                act.wait_ge(a_ready, 2 * GROUPS)
                for m in range(KD):
                    act.wait_ge(collected, KD * (GROUPS - 1) + m + 1)
                    squares.scalar(act, m, m // 2, m % 2)

            @block.gpsimd
            def _(pool):
                def split(s, g):
                    feed.lo_half(pool, s, g)

                def keep(t, g):
                    pool.wait_ge(gate_in, 2 * g + t + 1)
                    pool.tensor_copy(last[:, bass.ds(2 * g + t, 1), :].rearrange("p a n -> p (a n)"),
                                     gate[:, PROMPT:2 + TOK]).then_inc(kept, 1)

                def group(g, more):
                    keep(0, g)
                    if more:
                        split(0, g + 1)
                        split(1, g + 1)
                    pool.wait_ge(hi_d, g + 1)
                    pool.tensor_tensor(down_l, raw_d, down_h, ALU.subtract).then_inc(lo_d, 1)
                    keep(1, g)
                    if more:
                        split(2, g + 1)
                        split(3, g + 1)

                source.gpsimd(pool)
                pool.wait_ge(source.scaled, KD)
                pool.memset(T.acc[:], 0.0).then_inc(acc_zero, 1)
                with pool.Fori(0, GROUPS - 1) as g:
                    group(g, True)
                group(GROUPS - 1, False)
                pool.memset(T.sqsum[:], 0.0).then_inc(sqsum_own, 1)
                for m in range(KD):
                    squares.gpsimd(pool, m // 2, m % 2, lambda: pool.wait_ge(
                        *((squares.summed[(m - 1) % 2], (m + 1) // 2) if m else (sqsum_own, 1))))

            @block.tensor
            def _(pe):
                def hidden(s, g):
                    pe.wait_ge(lo[s], g + 1)
                    for k in range(KD):
                        if s == 0 and isinstance(g, int) and g == 0:
                            source.ready(pe, k)
                        ins = product(pe, T.ps, s % 2, slot_h[s][:, k, :], slot_l[s][:, k, :],
                                      T.hh[:, k, :], T.hl[:, k, :], k == 0, k == KD - 1)
                    ins.then_inc(made[s], 1)

                def tile0(g):
                    pe.wait_ge(gate_in, 2 * g)
                    hidden(0, g)
                    pe.wait_ge(multiplied, 2 * g)
                    hidden(1, g)

                def down(g, taken):
                    pe.wait_ge(lo_d, g + 1)
                    pe.wait_ge(a_ready, 2 * g + 2)
                    for m in range(KD):
                        if m >= 2:
                            pe.wait_ge(collected, KD * g + m - 1)
                        for j in range(2):
                            cols = slice(1024 * j + P * m, 1024 * j + P * m + P)
                            ins = product(pe, T.ps, m % 2, down_h[:, cols], down_l[:, cols], ah[:, j, :], al[:, j, :],
                                          j == 0, j == 1)
                        ins.then_inc(made_d, 1)
                        if m == 0:
                            pe.wait_ge(multiplied, taken)

                pe.wait_ge(rows_in, 16 * 6)
                for t in range(FT):
                    ins = pe.transpose(T.ps[:, 6, ROWS * t:ROWS * t + ROWS],
                                       rows[t // 16][1][:, P * (t % 16):P * (t % 16) + P], T.ident[0:ROWS, 0:ROWS])
                ins.then_inc(turned, 1)
                tile0(0)
                pe.wait_ge(gate_in, 1)
                hidden(2, 0)
                pe.wait_ge(multiplied, 1)
                hidden(3, 0)
                with pe.Fori(1, GROUPS) as g:
                    tile0(g)
                    pe.wait_ge(gate_in, 2 * g + 1)
                    down(g - 1, 2 * g + 1)
                    pe.wait_ge(collected, KD * g - 1)
                    hidden(2, g)
                    pe.wait_ge(collected, KD * g)
                    hidden(3, g)
                pe.wait_ge(gate_in, 2 * GROUPS)
                down(GROUPS - 1, 2 * GROUPS)
                pe.wait_ge(collected, KD * GROUPS)
                pe.wait_ge(kept, 2 * GROUPS)
                for t in range(FT):
                    ins = pe.transpose(flat[:, P * t:P * t + P], last[:, t, :], T.ident)
                ins.then_inc(keep_turned, 1)

            @block.vector
            def _(dve):
                def tap(g, t, r):
                    return prm[:, bass.ds(2 * g + t, 1), r:r + 1].rearrange("p a n -> p (a n)")

                def convolve(steps, t, g):
                    dve.wait_ge(gate_in, 2 * g + t + 1)
                    pv, sv = conv[:, 0:PROMPT], conv[:, PROMPT:TOK]
                    st = [prm[:, bass.ds(2 * g + t, 1), j:2 * SAMPLES:2].rearrange("p a b -> p (a b)") for j in range(2)]
                    first, second, third = (tap(g, t, 2 * SAMPLES + j) for j in range(3))
                    steps.note(dve.tensor_scalar(pv, gate[:, 0:PROMPT], first, None, ALU.mult))
                    steps.done(dve.tensor_scalar(sv, st[0], first, None, ALU.mult))
                    steps.note(dve.scalar_tensor_tensor(out=pv, in0=gate[:, 1:1 + PROMPT], scalar=second, in1=pv,
                                                        op0=ALU.mult, op1=ALU.add))
                    steps.done(dve.scalar_tensor_tensor(out=sv, in0=st[1], scalar=second, in1=sv,
                                                        op0=ALU.mult, op1=ALU.add))
                    dve.scalar_tensor_tensor(out=conv[:], in0=gate[:, 2:2 + TOK], scalar=third, in1=conv[:],
                                             op0=ALU.mult, op1=ALU.add).then_inc(conved, 1)

                def multiply(t, g):
                    dve.wait_ge(activated, 2 * g + t + 1)
                    dve.wait_ge(made[2 * t + 1], g + 1)
                    dve.tensor_tensor(chunks(conv[:]), chunks(conv[:]), region(T.ps, 1), ALU.mult).then_inc(multiplied, 1)

                def split(steps, t, g):
                    dve.wait_ge(multiplied, 2 * g + t + 1)
                    steps.done(dve.tensor_copy(ah[:, t, :], conv[:]))
                    dve.tensor_tensor(al[:, t, :], conv[:], ah[:, t, :], ALU.subtract).then_inc(a_ready, 1)
                    dve.wait_ge(a_ready, 2 * g + t + 1)

                def collect(g):
                    for m in range(KD):
                        dve.wait_ge(made_d, KD * g + m + 1)
                        a = chunks(T.acc[:, m, :])
                        dve.tensor_tensor(a, a, region(T.ps, m % 2), ALU.add).then_inc(collected, 1)
                    dve.wait_ge(collected, KD * g + KD)

                def group(g, with_down):
                    steps = Steps(dve, dve_own, 10 * g)
                    convolve(steps, 0, g)
                    multiply(0, g)
                    if with_down:
                        collect(g - 1)
                    split(steps, 0, g)
                    convolve(steps, 1, g)
                    multiply(1, g)
                    split(steps, 1, g)
                    assert steps.n == 10

                source.vector(dve)
                dve.wait_ge(source.lo_done[0], KD // 2)
                dve.memset(gate[:, 0:2], 0.0)
                dve.wait_ge(turned, 1)
                dve.tensor_copy(prm[:], T.ps[:, 6, 0:FT * ROWS].rearrange("p (t r) -> p t r", r=ROWS)).then_inc(prm_done, 1)
                dve.wait_ge(prm_done, 1)
                group(0, False)
                dve.wait_ge(acc_zero, 1)
                with dve.Fori(1, GROUPS) as g:
                    group(g, True)
                collect(GROUPS - 1)
                dve.wait_ge(keep_turned, 1)
                dve.tensor_copy(kept_rows, flat[:, 0:FF]).then_inc(keep_moved, 1)


def open_trunk(nc, ctx):
    T = Trunk()
    sb = lambda n, s, d=F32: ctx.enter_context(nc.sbuf_tensor(n, s, d))
    T.ps = ctx.enter_context(nc.psum_tensor("ps", [P, 8, 512], F32))
    T.wraw = sb("wraw", [P, 6144])
    T.con, T.eps = sb("con_sb", [P, 512]), sb("eps", [P, 1])
    T.ident = T.con[:, C_ID:C_ID + P]
    T.one = sb("one", [P, 1])
    T.gain = sb("gain", [P, KD, 8])
    T.acc = sb("acc", [P, KD, TOK])
    T.sqsum = sb("sqsum", [P, TOK])
    return T


class split_weights:

    def __init__(self, nc, T, name):
        self.ctx, self.nc, self.T, self.name = ExitStack(), nc, T, name

    def __enter__(self):
        self.T.wh = self.ctx.enter_context(self.nc.sbuf_tensor(self.name + "wh", [P, 6144], F32R))
        self.T.wl = self.ctx.enter_context(self.nc.sbuf_tensor(self.name + "wl", [P, 6144], F32R))

    def __exit__(self, *exc):
        return self.ctx.__exit__(*exc)


class split_pair:

    def __init__(self, nc, T, name):
        self.ctx, self.nc, self.T, self.name = ExitStack(), nc, T, name

    def __enter__(self):
        self.T.hh = self.ctx.enter_context(self.nc.sbuf_tensor(self.name + "hi", [P, KD, TOK], F32R))
        self.T.hl = self.ctx.enter_context(self.nc.sbuf_tensor(self.name + "lo", [P, KD, TOK], F32R))

    def __exit__(self, *exc):
        return self.ctx.__exit__(*exc)


def over(ap, n):
    return ap.unsqueeze(1).to_broadcast([ap.shape[0], n, ap.shape[-1]])


def per_column(ap, w):
    return ap.unsqueeze(2).to_broadcast([ap.shape[0], ap.shape[1], w])


def stage_gmlp(nc, T, proj, qkv, v_gain, w_s, b_s, chunk_v):
    G = 4
    with ExitStack() as ctx:
        sb = lambda n, s, d=F32: ctx.enter_context(nc.sbuf_tensor("ga_" + n, s, d))
        sem = lambda n: nc.alloc_semaphore("ga_" + n)
        u, v, rstd = sb("u", [P, G, TOK]), sb("v", [P, G, TOK]), sb("rstd", [P, TOK])
        vt, mixed = sb("vt", [P, 2, G, P]), sb("mixed", [P, 2, G, P])
        wn, wt, bias = sb("wn", [P, G, P]), sb("wt", [P, G, P]), sb("bias", [P, G, P])
        w00, gain, incl = sb("w00", [P, G]), sb("gain", [P, G]), T.con[:, C_INCL:C_INCL + P]
        sm, cv = sb("sm", [P, G, SAMPLES]), sb("cv", [SAMPLES, G * P])
        sq = T.wraw[:, 0:G * TOK].rearrange("p (a n) -> p a n", a=G)
        squared, summed, qkv_in = sem("squared"), sem("summed"), sem("qkv_in")
        v_in, u_in, par_in, out_done = sem("v_in"), sem("u_in"), sem("par_in"), sem("out_done")
        rstd_done, act_own = sem("rstd_done"), sem("act_own")
        normed, w_turned, w_masked = sem("normed"), sem("w_turned"), sem("w_masked")
        turned, vt_moved, mixed_made, mix_moved = sem("turned"), sem("vt_moved"), sem("mixed_made"), sem("mix_moved")
        cv_turned, cv_moved, dve_own = sem("cv_turned"), sem("cv_moved"), sem("dve_own")
        rows = proj.rearrange("(m p) n -> p m n", p=P)
        with nc.Block() as block:
            @block.sync
            def _(sp):
                sp.dma_start(v[:], rows[:, G:2 * G, :]).then_inc(v_in, 16)
                sp.dma_start(u[:], rows[:, 0:G, :]).then_inc(u_in, 16)
                sp.dma_start(wn[:], w_s.rearrange("g t s -> t g s")).then_inc(par_in, 16)
                sp.dma_start(bias[:], b_s.rearrange("g t -> (g t)").partition_broadcast(P)).then_inc(par_in, 16)
                sp.dma_start(w00[:], w_s[:, 0, 0].partition_broadcast(P), allow_slow_non_contiguous=True).then_inc(par_in, 16)
                sp.dma_start(gain[:], v_gain.rearrange("(g p) -> p g", p=P), allow_slow_non_contiguous=True).then_inc(par_in, 16)
                sp.dma_start(qkv[:], rows[:, 2 * G:5 * G, :]).then_inc(qkv_in, 16)
                sp.wait_ge(qkv_in, 16)
                sp.wait_ge(cv_moved, 1)
                sp.dma_start(chunk_v, cv[:]).then_inc(out_done, 16)
                sp.wait_ge(out_done, 16)

            @block.scalar
            def _(act):
                steps = Steps(act, act_own)
                act.wait_ge(v_in, 16)
                for g in range(G):
                    act.activation(sq[:, g, :], v[:, g, :], ACT.Square).then_inc(squared, 1)
                act.wait_ge(summed, G)
                rsqrt_of(act, steps, chunks(rstd[:]), region(T.ps, 0), 1.0 / (G * P), T.eps[:]).then_inc(rstd_done, 1)
                for c in range(NCHUNK):
                    act.wait_ge(turned, c + 1)
                    if c >= 2:
                        act.wait_ge(mixed_made, c - 1)
                    act.activation(vt[:, c % 2], T.ps[:, 6 + c % 2, :].rearrange("p (g n) -> p g n", g=G),
                                   ACT.Copy).then_inc(vt_moved, 1)

            @block.tensor
            def _(pe):
                pe.wait_ge(par_in, 64)
                for g in range(G):
                    ins = pe.transpose(T.ps[:, 3, P * g:P * g + P], wn[:, g, :], T.ident)
                ins.then_inc(w_turned, 1)
                for g in range(G):
                    pe.wait_ge(squared, g + 1)
                    ones_times(pe, T, 0, sq[:, g, :], g == 0, g == G - 1).then_inc(summed, 1)
                pe.wait_ge(normed, G)
                pe.wait_ge(w_masked, 1)
                for g in range(G):
                    ins = pe.transpose(T.ps[0:SAMPLES, 3, P * g:P * g + P], v[:, g, PROMPT:TOK], T.ident)
                ins.then_inc(cv_turned, 1)

                def turn(c):
                    if c >= 2:
                        pe.wait_ge(vt_moved, c - 1)
                    for g in range(G):
                        ins = pe.transpose(T.ps[:, 6 + c % 2, P * g:P * g + P], v[:, g, P * c:P * c + P], T.ident)
                    ins.then_inc(turned, 1)

                turn(0)
                for c in range(NCHUNK):
                    if c + 1 < NCHUNK:
                        turn(c + 1)
                    pe.wait_ge(vt_moved, c + 1)
                    if c >= 2:
                        pe.wait_ge(mix_moved, c - 1)
                    for g in range(G):
                        ins = pe.matmul(T.ps[:, 4 + c % 2, P * g:P * g + P], vt[:, c % 2, g, :], wt[:, g, :],
                                        start=True, stop=True)
                    ins.then_inc(mixed_made, 1)

            @block.vector
            def _(dve):
                steps = Steps(dve, dve_own)
                dve.wait_ge(w_turned, 1)
                dve.tensor_tensor(wt[:], T.ps[:, 3, :].rearrange("p (g n) -> p g n", g=G), over(incl, G),
                                  ALU.mult).then_inc(w_masked, 1)
                dve.wait_ge(rstd_done, 1)
                for g in range(G):
                    dve.scalar_tensor_tensor(out=v[:, g, :], in0=v[:, g, :], scalar=gain[:, g:g + 1], in1=rstd[:],
                                             op0=ALU.mult, op1=ALU.mult).then_inc(normed, 1)
                dve.wait_ge(normed, G)
                dve.wait_ge(u_in, 16)
                for g in range(G):
                    steps.note(dve.tensor_scalar(sm[:, g, :], v[:, g, PROMPT:TOK], w00[:, g:g + 1], bias[:, g, 0:1],
                                                 ALU.mult, ALU.add))
                steps.eng.wait_ge(steps.sem, steps.n)
                dve.tensor_tensor(T.acc[:, 0:G, PROMPT:TOK], sm[:], u[:, :, PROMPT:TOK], ALU.mult)
                dve.wait_ge(cv_turned, 1)
                dve.tensor_copy(cv[:], T.ps[0:SAMPLES, 3, :]).then_inc(cv_moved, 1)
                for c in range(NCHUNK):
                    dve.wait_ge(mixed_made, c + 1)
                    if c >= 2:
                        dve.wait_ge(dve_own, steps.n - 1)
                    dve.tensor_tensor(mixed[:, c % 2], T.ps[:, 4 + c % 2, :].rearrange("p (g n) -> p g n", g=G),
                                      bias[:], ALU.add).then_inc(mix_moved, 1)
                    dve.wait_ge(mix_moved, c + 1)
                    steps.note(dve.tensor_tensor(T.acc[:, 0:G, P * c:P * c + P], mixed[:, c % 2],
                                                 u[:, :, P * c:P * c + P], ALU.mult))


def head_norms(nc, T, name, tiles, scale, factor, after=None, loads=()):
    n = len(tiles)
    with ExitStack() as ctx:
        sb = lambda s_, s, d=F32: ctx.enter_context(nc.sbuf_tensor(name + s_, s, d))
        sem = lambda s_: nc.alloc_semaphore(name + s_)
        rstd = sb("rstd", [P, 4, TOK])
        sq = T.wraw[:, 0:4 * TOK].rearrange("p (a n) -> p a n", a=4)
        squared, summed, logged, rooted, scaled = (sem(s_) for s_ in "squared summed logged rooted scaled".split())
        loaded = sem("loaded")
        with nc.Block() as block:
            @block.sync
            def _(sp):
                for dst, src in loads:
                    sp.dma_start(dst, src).then_inc(loaded, 16)

            @block.scalar
            def _(act):
                for k in range(0, n, 2):
                    for j in (k, k + 1):
                        act.wait_ge(summed, j + 1)
                        if j >= 4:
                            act.wait_ge(scaled, j - 3)
                        act.activation(chunks(rstd[:, j % 4, :]), region(T.ps, j % 2), ACT.Ln, scale=scale, bias=T.eps[:]
                                       ).then_inc(logged, 1)
                    for j in (k, k + 1):
                        act.wait_ge(logged, j + 1)
                        act.activation(rstd[:, j % 4, :], rstd[:, j % 4, :], ACT.Exp, scale=-0.5).then_inc(rooted, 1)

            @block.vector
            def _(dve):
                def square(k):
                    if k >= 4:
                        dve.wait_ge(summed, k - 3)
                    dve.tensor_tensor(sq[:, k % 4, :], tiles[k], tiles[k], ALU.mult).then_inc(squared, 1)

                for k in range(min(4, n)):
                    square(k)
                if loads:
                    dve.wait_ge(loaded, 16 * len(loads))
                for k in range(n):
                    if k + 4 < n:
                        square(k + 4)
                    dve.wait_ge(rooted, k + 1)
                    dve.wait_ge(squared, k + 1)
                    dve.scalar_tensor_tensor(out=tiles[k], in0=tiles[k], scalar=factor(k), in1=rstd[:, k % 4, :],
                                             op0=ALU.mult, op1=ALU.mult).then_inc(scaled, 1)
                    if after is not None:
                        dve.wait_ge(scaled, k + 1)
                        dve.tensor_tensor(tiles[k], tiles[k], after(k), ALU.mult)

            @block.tensor
            def _(pe):
                for k in range(n):
                    pe.wait_ge(squared, k + 1)
                    if k >= 2:
                        pe.wait_ge(logged, k - 1)
                    ones_times(pe, T, k % 2, sq[:, k % 4, :]).then_inc(summed, 1)


def stage_gates(nc, T, proj, gates, a_log, dt_bias, consts):
    with ExitStack() as ctx:
        sb = lambda n, s, d=F32: ctx.enter_context(nc.sbuf_tensor("cb_" + n, s, d))
        sem = lambda n: nc.alloc_semaphore("cb_" + n)
        reset = sb("reset", [P, PROMPT])
        x, t1, t2 = (sb(n, [P, TOK]) for n in ("x", "t1", "t2"))
        col = sb("col", [P, 3])
        hr = slice(32, 32 + HEADS_B)
        gates_in, dve_own, act_own, g1, g2 = sem("gates_in"), sem("dve_own"), sem("act_own"), sem("g1"), sem("g2")
        with nc.Block() as block:
            @block.sync
            def _(sp):
                sp.dma_start(gates[:], proj.rearrange("(m p) n -> m p n", p=P)[24, 0:64, :]).then_inc(gates_in, 16)
                sp.dma_start(col[hr, 0:1], a_log.rearrange("(a b) -> a b", b=1)).then_inc(gates_in, 16)
                sp.dma_start(col[hr, 1:2], dt_bias.rearrange("(a b) -> a b", b=1)).then_inc(gates_in, 16)
                sp.dma_start(reset[:], consts[:, C_RESET:C_RESET + PROMPT]).then_inc(gates_in, 16)

            @block.scalar
            def _(act):
                steps = Steps(act, act_own)
                act.wait_ge(gates_in, 64)
                act.activation(gates[0:HEADS_B, :], gates[0:HEADS_B, :], ACT.Sigmoid)
                act.wait_ge(g1, 1)
                steps.done(act.activation(t1[hr, :], t1[hr, :], ACT.Exp, scale=-1.0))
                steps.note(act.activation(t1[hr, :], t1[hr, :], ACT.Ln, bias=T.one[hr, :]))
                act.activation(col[hr, 2:3], col[hr, 0:1], ACT.Exp).then_inc(g2, 1)
                act.wait_ge(act_own, steps.n)

            @block.vector
            def _(dve):
                steps = Steps(dve, dve_own)
                dve.wait_ge(gates_in, 64)
                steps.done(dve.tensor_scalar(x[hr, :], gates[hr, :], col[hr, 1:2], None, ALU.add))
                steps.done(dve.tensor_scalar(t1[hr, :], x[hr, :], -1.0, None, ALU.mult))
                dve.tensor_tensor(t1[hr, :], t1[hr, :], x[hr, :], ALU.max).then_inc(g1, 1)
                dve.wait_ge(g2, 1)
                dve.wait_ge(act_own, 2)
                steps.done(dve.scalar_tensor_tensor(out=t2[hr, :], in0=x[hr, :], scalar=0.0, in1=t1[hr, :],
                                                    op0=ALU.max, op1=ALU.add))
                steps.done(dve.tensor_scalar(gates[hr, :], t2[hr, :], col[hr, 2:3], -1.0, ALU.mult, ALU.mult))
                steps.done(dve.tensor_tensor_scan(x[hr, 0:PROMPT], reset[hr, :], gates[hr, 0:PROMPT], 0.0,
                                                  ALU.mult, ALU.add))
                dve.tensor_copy(gates[hr, 0:PROMPT], x[hr, 0:PROMPT])


def stage_delta(nc, T, qkv, gates, consts, state_out):
    H = HEADS_B
    LV = 7
    UP = 2 * LV - 3
    with ExitStack() as ctx:
        sb = lambda n, s, d=F32: ctx.enter_context(nc.sbuf_tensor("gd_" + n, s, d))
        sem = lambda n: nc.alloc_semaphore("gd_" + n)
        both = lambda n: [sem(n + "0"), sem(n + "1")]
        masks, sel, cap = sb("masks", [P, LV, P]), sb("sel", [64, 8, P]), sb("cap", [P, P])
        tiles, rows = sb("tiles", [P, 2, 3 * H, P]), sb("rows", [64, 2, P])
        col, eg_col, beg, wend = (sb(n, [P, 2, w]) for n, w in (("col", 64), ("eg_col", H), ("beg", H), ("wend", H)))
        names = "eg dm pt lt qe t tt p1 w2 u kbe vb kw first".split()
        eg, dm, pt, lt, qe, t, tt, p1, w2, u, kbe, vb, kw, first = (sb(n, [P, 2, H, P]) for n in names)
        state = sb("state", [P, H, P])
        am = T.wraw[:].rearrange("p (x l h n) -> p x l h n", x=2, l=LV - 1, h=H)
        bank = [[T.ps[:, 4 * x + n, :].rearrange("p (h n) -> p h n", h=H) for n in range(4)] for x in range(2)]
        heads = range(H)
        K = lambda x, h: tiles[:, x, H + h, :]
        Q = lambda x, h: tiles[:, x, h, :]
        V = lambda x, h: tiles[:, x, 2 * H + h, :]
        con_in, cap_done, out_done = sem("con_in"), sem("cap_done"), sem("out_done")
        staged, spread, v_turned, k_turned = both("staged"), both("spread"), both("v_turned"), both("k_turned")
        col_copied, diffed, decayed, beg_done = both("col_copied"), both("diffed"), both("decayed"), both("beg_done")
        beta_used, kk_made, kq_made, lt_done, pt_done = (both(n) for n in "beta_used kk_made kq_made lt_done pt_done".split())
        masked, qe_done, scaled, tt_first, t_turned = (both(n) for n in "masked qe_done scaled tt_first t_turned".split())
        t_first, p1_made, p1_moved, merged, updated = (both(n) for n in "t_first p1_made p1_moved merged updated".split())
        w2_made, w2_moved, u_made, u_moved, o_made, o_moved, s_made, s_updated = (
            both(n) for n in "w2_made w2_moved u_made u_moved o_made o_moved s_made s_updated".split())

        def run_pairs(eng, body):
            with eng.Fori(0, NCHUNK // 2 - 1) as i:
                body(i, True)
            body(NCHUNK // 2 - 1, False)

        with nc.Block() as block:
            @block.sync
            def _(sp):
                sp.dma_start(masks[:], consts[:, C_LEVEL:C_LEVEL + LV * P].rearrange("p (l n) -> p l n", l=LV)
                             ).then_inc(con_in, 16)
                sp.dma_start(sel[:], consts[0:64, C_SEL:C_SEL + 8 * P].rearrange("p (l n) -> p l n", l=8)
                             ).then_inc(con_in, 16)

            @block.vector
            def _(dve):
                dve.memset(state[:], 0.0)
                dve.tensor_scalar(cap[:], T.con[:, C_INCL:C_INCL + P], -MASKED, MASKED, ALU.mult, ALU.add
                                  ).then_inc(cap_done, 1)
                dve.wait_ge(con_in, 32)

        with nc.Block() as block:
            @block.tensor
            def _(pe):
                def spread_gates(x, i):
                    pe.wait_ge(staged[x], 2 * i + 2)
                    pe.wait_ge(o_moved[x], i)
                    pe.wait_ge(u_moved[x], i)
                    pe.wait_ge(w2_moved[x], i)
                    pe.wait_ge(s_updated[x], H * i)
                    for n in range(8):
                        pe.matmul(bank[x][n // H][:, n % H, :], sel[:, n, :], rows[:, x, :], start=True, stop=True)
                    pe.transpose(T.ps[:, 4 * x + 2, 0:64], rows[:, x, :], T.ident[0:64, 0:64]).then_inc(spread[x], 1)
                    for h in heads:
                        ins = pe.transpose(bank[x][3][:, h, :], K(x, h), T.ident)
                    ins.then_inc(k_turned[x], 1)

                def products(x, i):
                    pe.wait_ge(col_copied[x], i + 1)
                    for h in heads:
                        ins = pe.transpose(bank[x][2][:, h, :], V(x, h), T.ident)
                    ins.then_inc(v_turned[x], 1)
                    pe.wait_ge(decayed[x], 4 * i + 4)
                    for h in heads:
                        ins = pe.matmul(bank[x][1][:, h, :], K(x, h), K(x, h), start=True, stop=True)
                    ins.then_inc(kk_made[x], 1)
                    pe.wait_ge(beta_used[x], i + 1)
                    for h in heads:
                        ins = pe.matmul(bank[x][0][:, h, :], K(x, h), Q(x, h), start=True, stop=True)
                    ins.then_inc(kq_made[x], 1)

                def turn_first(x, i):
                    pe.wait_ge(tt_first[x], i + 1)
                    for h in heads:
                        ins = pe.transpose(bank[x][1][:, h, :], tt[:, x, h, :], T.ident)
                    ins.then_inc(t_turned[x], 1)

                def off_block(x, i, l):
                    if l == 1:
                        pe.wait_ge(t_first[x], i + 1)
                    else:
                        pe.wait_ge(updated[x], UP * i + 2 * (l - 1))
                    pe.wait_ge(masked[x], LV * i + l + 1)
                    for h in heads:
                        ins = pe.matmul(bank[x][1][:, h, :], am[:, x, l - 1, h, :], t[:, x, h, :], start=True, stop=True)
                    ins.then_inc(p1_made[x], 1)

                def merge(x, i, l):
                    pe.wait_ge(p1_moved[x], (LV - 1) * i + l)
                    if l == 1:
                        pe.wait_ge(pt_done[x], i + 1)
                        pe.wait_ge(scaled[x], 3 * i + 3)
                    if l < LV - 1:
                        for h in heads:
                            ins = pe.matmul(bank[x][0][:, h, :], tt[:, x, h, :], p1[:, x, h, :], start=True, stop=True)
                        ins.then_inc(merged[x], 1)
                    for h in heads:
                        ins = pe.matmul(bank[x][2][:, h, :], p1[:, x, h, :], tt[:, x, h, :], start=True, stop=True)
                    ins.then_inc(merged[x], 1)

                def keys(x, i):
                    pe.wait_ge(updated[x], UP * i + UP)
                    for h in heads:
                        ins = pe.matmul(bank[x][3][:, h, :], kbe[:, x, h, :], tt[:, x, h, :], start=True, stop=True)
                    ins.then_inc(w2_made[x], 1)

                def recur(x, i):
                    pe.wait_ge(w2_moved[x], i + 1)
                    pe.wait_ge(s_updated[1 - x], H * i + (H if x else 0))
                    for h in heads:
                        pe.matmul(bank[x][1][:, h, :], tt[:, x, h, :], vb[:, x, h, :], start=True, stop=False)
                        ins = pe.matmul(bank[x][1][:, h, :], w2[:, x, h, :], state[:, h, :], start=False, stop=True)
                    ins.then_inc(u_made[x], 1)
                    pe.wait_ge(u_moved[x], i + 1)
                    for h in heads:
                        ins = pe.matmul(bank[x][2][:, h, :], kw[:, x, h, :], u[:, x, h, :], start=True, stop=True)
                    ins.then_inc(s_made[x], 1)
                    pe.wait_ge(qe_done[x], i + 1)
                    for h in heads:
                        pe.matmul(bank[x][0][:, h, :], state[:, h, :], qe[:, x, h, :], start=True, stop=False)
                        ins = pe.matmul(bank[x][0][:, h, :], u[:, x, h, :], pt[:, x, h, :], start=False, stop=True)
                    ins.then_inc(o_made[x], 1)

                def pair(i, more):
                    for f in (spread_gates, products, turn_first):
                        for x in range(2):
                            f(x, i)
                    for l in range(1, LV):
                        for f in (off_block, merge):
                            for x in range(2):
                                f(x, i, l)
                    for x in range(2):
                        keys(x, i)
                    for x in range(2):
                        recur(x, i)

                run_pairs(pe, pair)

            @block.vector
            def _(dve):
                def differences(x, i):
                    dve.wait_ge(spread[x], i + 1)
                    dve.tensor_copy(col[:, x, :], T.ps[:, 4 * x + 2, 0:64]).then_inc(col_copied[x], 1)
                    dve.wait_ge(col_copied[x], i + 1)
                    for h in heads:
                        dve.scalar_tensor_tensor(out=dm[:, x, h, :], in0=bank[x][1][:, h, :], scalar=col[:, x, 32 + h:33 + h],
                                                 in1=cap[:], op0=ALU.subtract, op1=ALU.min)
                    dve.tensor_tensor(wend[:, x, :], bank[x][1][:, :, P - 1], col[:, x, 32:32 + H], ALU.subtract
                                      ).then_inc(diffed[x], 1)

                def scores(x, i):
                    dve.wait_ge(decayed[x], 4 * i + 4)
                    dve.tensor_tensor(beg[:, x, :], col[:, x, 0:H], eg_col[:, x, :], ALU.mult).then_inc(beg_done[x], 1)
                    dve.tensor_tensor(lt[:, x], dm[:, x], bank[x][0], ALU.mult).then_inc(beta_used[x], 1)
                    dve.wait_ge(beta_used[x], i + 1)
                    dve.wait_ge(kk_made[x], i + 1)
                    dve.tensor_tensor(lt[:, x], lt[:, x], bank[x][1], ALU.mult).then_inc(lt_done[x], 1)
                    dve.wait_ge(kq_made[x], i + 1)
                    dve.tensor_tensor(pt[:, x], dm[:, x], bank[x][0], ALU.mult).then_inc(pt_done[x], 1)

                def first_tt(x, i):
                    dve.wait_ge(masked[x], LV * i + 1)
                    dve.tensor_tensor(tt[:, x], over(T.ident, H), first[:, x], ALU.subtract).then_inc(tt_first[x], 1)

                def first_t(x, i):
                    dve.wait_ge(t_turned[x], i + 1)
                    dve.tensor_copy(t[:, x], bank[x][1]).then_inc(t_first[x], 1)

                def update(x, i, l):
                    if l < LV - 1:
                        dve.wait_ge(merged[x], UP * i + 2 * l - 1)
                        if l == 1:
                            dve.wait_ge(t_first[x], i + 1)
                        dve.tensor_tensor(t[:, x], t[:, x], bank[x][0], ALU.subtract).then_inc(updated[x], 1)
                        dve.wait_ge(merged[x], UP * i + 2 * l)
                    else:
                        dve.wait_ge(merged[x], UP * i + UP)
                    dve.tensor_tensor(tt[:, x], tt[:, x], bank[x][2], ALU.subtract).then_inc(updated[x], 1)
                    dve.wait_ge(updated[x], UP * i + min(2 * l, UP))

                def recur(x, i):
                    dve.wait_ge(u_made[x], i + 1)
                    dve.tensor_copy(u[:, x], bank[x][1]).then_inc(u_moved[x], 1)
                    dve.wait_ge(s_made[x], i + 1)
                    dve.wait_ge(o_made[x], i + 1)
                    for h in heads:
                        dve.scalar_tensor_tensor(out=state[:, h, :], in0=state[:, h, :], scalar=eg[:, x, h, P - 1:P],
                                                 in1=bank[x][2][:, h, :], op0=ALU.mult, op1=ALU.add
                                                 ).then_inc(s_updated[x], 1)
                    dve.wait_ge(s_updated[x], H * i + H)

                def pair(i, more):
                    for f in (differences, scores, first_tt, first_t):
                        for x in range(2):
                            f(x, i)
                    for l in range(1, LV):
                        for x in range(2):
                            update(x, i, l)
                    for x in range(2):
                        recur(x, i)

                run_pairs(dve, pair)

            @block.scalar
            def _(act):
                def decay(x, i):
                    act.wait_ge(diffed[x], i + 1)
                    act.activation(eg_col[:, x, :], col[:, x, 32:32 + H], ACT.Exp).then_inc(decayed[x], 1)
                    act.activation(dm[:, x], dm[:, x], ACT.Exp).then_inc(decayed[x], 1)
                    act.activation(wend[:, x, :], wend[:, x, :], ACT.Exp).then_inc(decayed[x], 1)
                    act.activation(eg[:, x], bank[x][1], ACT.Exp).then_inc(decayed[x], 1)

                def scale(x, i):
                    act.wait_ge(k_turned[x], i + 1)
                    act.wait_ge(v_turned[x], i + 1)
                    act.wait_ge(beg_done[x], i + 1)
                    act.wait_ge(decayed[x], 4 * i + 4)
                    for dst, src, factor in ((vb, 2, col), (kbe, 3, beg), (kw, 3, wend)):
                        for h in heads:
                            ins = act.activation(dst[:, x, h, :], bank[x][src][:, h, :], ACT.Copy,
                                                 scale=factor[:, x, h:h + 1])
                        ins.then_inc(scaled[x], 1)

                def move_p1(x, i, l):
                    act.wait_ge(p1_made[x], (LV - 1) * i + l)
                    act.activation(p1[:, x], bank[x][1], ACT.Copy).then_inc(p1_moved[x], 1)

                def pair(i, more):
                    for f in (decay, scale):
                        for x in range(2):
                            f(x, i)
                    for l in range(1, LV):
                        for x in range(2):
                            move_p1(x, i, l)
                    for x in range(2):
                        act.wait_ge(w2_made[x], i + 1)
                        act.activation(w2[:, x], bank[x][3], ACT.Copy, scale=-1.0).then_inc(w2_moved[x], 1)
                    for x in range(2):
                        act.wait_ge(o_made[x], i + 1)
                        act.activation(T.acc[:, H:2 * H, bass.ds(2 * P * i + P * x, P)], bank[x][0], ACT.Copy
                                       ).then_inc(o_moved[x], 1)

                run_pairs(act, pair)

            @block.gpsimd
            def _(pool):
                def stage(x, i):
                    cols = bass.ds(2 * P * i + P * x, P)
                    pool.tensor_copy(tiles[:, x], qkv[:, :, cols]).then_inc(staged[x], 1)
                    pool.tensor_copy(rows[:, x, :], gates[:, cols]).then_inc(staged[x], 1)

                def pair(i, more):
                    for l in range(LV):
                        for x in range(2):
                            if l == 0:
                                pool.wait_ge(lt_done[x], i + 1)
                            dst = first[:, x] if l == 0 else am[:, x, l - 1]
                            pool.tensor_tensor(dst, lt[:, x], over(masks[:, l, :], H), ALU.mult).then_inc(masked[x], 1)
                    for x in range(2):
                        pool.wait_ge(decayed[x], 4 * i + 4)
                        pool.tensor_tensor(qe[:, x], tiles[:, x, 0:H, :], eg[:, x], ALU.mult).then_inc(qe_done[x], 1)
                    if more:
                        for x in range(2):
                            pool.wait_ge(kq_made[x], i + 1)
                            pool.wait_ge(qe_done[x], i + 1)
                            stage(x, i + 1)

                for x in range(2):
                    stage(x, 0)
                run_pairs(pool, pair)

            @block.sync
            def _(sp):
                sp.wait_ge(s_updated[1], H * (NCHUNK // 2))
                sp.dma_start(state_out.rearrange("h d e -> d h e"), state[:]).then_inc(out_done, 16)
                sp.wait_ge(out_done, 16)


def stage_delta_sample(nc, T, qkv, gates, consts, state_in, state_out):
    H, B = HEADS_B, SAMPLES
    J = H * B
    with ExitStack() as ctx:
        sb = lambda n, s, d=F32: ctx.enter_context(nc.sbuf_tensor("gs_" + n, s, d))
        sem = lambda n: nc.alloc_semaphore("gs_" + n)
        sel, st, kq = sb("sel", [64, 8, P]), sb("st", [P, J, P]), sb("kq", [P, J, 2])
        beta, a, qk, prod, u, o, vs, srows = (sb(n, [P, J]) for n in "beta a qk prod u o vs srows".split())
        kt, ut = sb("kt", [J, P]), sb("ut", [J, P])
        ud = T.wraw[0:J, 0:J * P].rearrange("p (j n) -> p j n", j=J)
        con_in, staged, spread = sem("con_in"), sem("staged"), sem("spread")
        st_in = [sem(f"st_in{h}") for h in range(H)]
        a_done, sums_made, steps_s, u_done = sem("a_done"), sem("sums_made"), sem("steps"), sem("u_done")
        turned, ud_done, outer, st_new, out_done = sem("turned"), sem("ud_done"), sem("outer"), sem("st_new"), sem("out_done")
        with nc.Block() as block:
            @block.sync
            def _(sp):
                sp.dma_start(sel[:], consts[0:64, C_SEL:C_SEL + 8 * P].rearrange("p (l n) -> p l n", l=8)
                             ).then_inc(con_in, 16)
                for h in range(H):
                    sp.dma_start(st[:, B * h:B * h + B, :], state_in[:, h].rearrange("b d e -> d b e")).then_inc(st_in[h], 16)
                for h in range(H):
                    sp.wait_ge(st_new, B * h + B)
                    sp.dma_start(state_out[:, h].rearrange("b d e -> d b e"), st[:, B * h:B * h + B, :]).then_inc(out_done, 16)
                sp.wait_ge(out_done, 16 * H)

            @block.tensor
            def _(pe):
                pe.wait_ge(con_in, 16)
                for n in range(8):
                    ins = pe.matmul(T.ps[:, 1, B * n:B * n + B], sel[:, n, :], gates[:, PROMPT:TOK], start=True, stop=True)
                ins.then_inc(spread, 1)
                pe.wait_ge(staged, 4)
                for j in range(J):
                    if j % B == 0:
                        pe.wait_ge(st_in[j // B], 16)
                    pe.matmul(T.ps[:, 0, 2 * j:2 * j + 2], st[:, j, :], kq[:, j, :], start=True, stop=True)
                pe.matmul(T.ps[:, 2, 0:J], T.con[:, C_ONE:C_ONE + P], prod[:], start=True, stop=True).then_inc(sums_made, 1)
                pe.wait_ge(u_done, 1)
                pe.transpose(T.ps[0:J, 3, 0:P], srows[:], T.ident)
                pe.transpose(T.ps[0:J, 3, P:2 * P], u[:], T.ident).then_inc(turned, 1)
                for half in range(2):
                    pe.wait_ge(ud_done, 2)
                    pe.wait_ge(st_new, 16 * half)
                    for n in range(4):
                        j = 16 * half + 4 * n
                        pe.matmul(T.ps[:, 4 + n, :], kt[:], ud[:, j:j + 4, :].rearrange("p j n -> p (j n)"),
                                  start=True, stop=True).then_inc(outer, 1)

            @block.scalar
            def _(act):
                act.wait_ge(spread, 1)
                act.activation(a[:], T.ps[:, 1, J:2 * J], ACT.Exp).then_inc(a_done, 1)

            @block.vector
            def _(dve):
                steps = Steps(dve, steps_s)
                sample = lambda n: qkv[:, H * n:H * n + H, PROMPT:TOK]
                grid = lambda x: x.rearrange("p (h b) -> p h b", h=H)
                dve.tensor_copy(kq[:, :, 0].rearrange("p (h b) -> p h b", h=H), sample(1)).then_inc(staged, 1)
                dve.tensor_copy(kq[:, :, 1].rearrange("p (h b) -> p h b", h=H), sample(0)).then_inc(staged, 1)
                dve.tensor_tensor(grid(prod[:]), sample(0), sample(1), ALU.mult).then_inc(staged, 1)
                dve.tensor_copy(grid(srows[:]), sample(1)).then_inc(staged, 1)
                steps.note(dve.tensor_copy(grid(vs[:]), sample(2)))
                dve.wait_ge(spread, 1)
                dve.wait_ge(a_done, 1)
                steps.done(dve.tensor_copy(beta[:], T.ps[:, 1, 0:J]))
                dve.wait_ge(sums_made, 1)
                kqs = T.ps[:, 0, 0:2 * J].rearrange("p (j c) -> p c j", c=2)
                steps.done(dve.tensor_tensor(u[:], a[:], kqs[:, 0, :], ALU.mult))
                steps.done(dve.tensor_tensor(u[:], vs[:], u[:], ALU.subtract))
                steps.done(dve.tensor_tensor(u[:], u[:], beta[:], ALU.mult))
                u_val = steps.note(dve.tensor_tensor(o[:], a[:], kqs[:, 1, :], ALU.mult))
                dve.tensor_tensor(qk[:], u[:], T.ps[:, 2, 0:J], ALU.mult).then_inc(u_done, 1)
                dve.wait_ge(u_done, 1)
                dve.wait_ge(steps_s, u_val)
                dve.tensor_tensor(T.acc[:, H:2 * H, PROMPT:TOK], grid(o[:]), grid(qk[:]), ALU.add)
                dve.wait_ge(turned, 1)
                dve.tensor_copy(kt[:], T.ps[0:J, 3, 0:P]).then_inc(ud_done, 1)
                steps.done(dve.tensor_copy(ut[:], T.ps[0:J, 3, P:2 * P]))
                dve.tensor_tensor(ud, over(ut[:], J), per_column(T.ident[0:J, 0:J], P), ALU.mult).then_inc(ud_done, 1)
                for half in range(2):
                    for n in range(16):
                        j = 16 * half + n
                        dve.wait_ge(outer, 4 * half + n // 4 + 1)
                        dve.scalar_tensor_tensor(out=st[:, j, :], in0=st[:, j, :], scalar=a[:, j:j + 1],
                                                 in1=T.ps[:, 4 + n // 4, P * (n % 4):P * (n % 4) + P],
                                                 op0=ALU.mult, op1=ALU.add).then_inc(st_new, 1)


def stage_gate_z(nc, T, proj, g_out):
    H = HEADS_B
    with ExitStack() as ctx:
        z = ctx.enter_context(nc.sbuf_tensor("gz_z", [P, H, TOK], F32))
        gain = ctx.enter_context(nc.sbuf_tensor("gz_gain", [P, 1], F32))
        head_norms(nc, T, "gz", [T.acc[:, H + h, :] for h in range(H)], 1.0 / P, lambda k: gain[:], lambda k: z[:, k, :],
                   ((z[:], proj.rearrange("(m p) n -> p m n", p=P)[:, 20:24, :]),
                    (gain[:], g_out.rearrange("(a b) -> a b", b=1))))


def mixer_even(nc, T, proj, ins, outs, consts):
    with ExitStack() as ctx:
        qkv = ctx.enter_context(nc.sbuf_tensor("qkv", [P, 3 * HEADS_B, TOK], F32))
        gates = ctx.enter_context(nc.sbuf_tensor("gates", [64, TOK], F32))
        stage_gmlp(nc, T, proj, qkv, ins["a_v_norm"][0], ins["a_w_s"][0], ins["a_b_s"][0],
                   outs["chunk_v"][0].rearrange("b s c -> (b s) c"))
        stage_gates(nc, T, proj, gates, ins["b_a_log"][0], ins["b_dt_bias"][0], consts)
        head_norms(nc, T, "qk", [qkv[:, m, :] for m in range(2 * HEADS_B)], 1.0,
                   lambda k: float(P) ** -0.5 if k < HEADS_B else 1.0)
        stage_delta(nc, T, qkv, gates, consts, outs["gdn_state_prompt"][0, 0])
        stage_delta_sample(nc, T, qkv, gates, consts, ins["state_gdn"][0], outs["gdn_state_sample"][0])
    stage_gate_z(nc, T, proj, ins["b_out_norm"][0])


def stage_lambda(nc, T, nlam, subln_cols, subln_rows, c_lambda, c_subln):
    with ExitStack() as ctx:
        sem = lambda n: nc.alloc_semaphore("lm_" + n)
        lq = ctx.enter_context(nc.sbuf_tensor("lm_lq", [P, 4, 64], F32))
        pr = ctx.enter_context(nc.sbuf_tensor("lm_pr", [P, 2, 64], F32))
        sm = ctx.enter_context(nc.sbuf_tensor("lm_sm", [P, 2], F32))
        par_in, own, exped = sem("par_in"), sem("own"), sem("exped")
        with nc.Block() as block:
            @block.sync
            def _(sp):
                sp.dma_start(lq[:], c_lambda.rearrange("a d -> (a d)").partition_broadcast(P)).then_inc(par_in, 16)
                sp.dma_start(subln_rows, c_subln.partition_broadcast(P)).then_inc(par_in, 16)
                sp.dma_start(subln_cols, c_subln.rearrange("(a b) -> a b", b=1)).then_inc(par_in, 16)

            @block.vector
            def _(dve):
                steps = Steps(dve, own)
                dve.wait_ge(par_in, 48)
                steps.note(dve.tensor_scalar(subln_rows, subln_rows, 1.0 - LAM_INIT, None, ALU.mult))
                steps.note(dve.tensor_scalar(subln_cols, subln_cols, 1.0 - LAM_INIT, None, ALU.mult))
                steps.done(dve.tensor_tensor(pr[:], lq[:, 0:4:2, :], lq[:, 1:4:2, :], ALU.mult))
                steps.note(dve.tensor_reduce(sm[:], pr[:], AX_X, ALU.add))
                dve.wait_ge(exped, 1)
                dve.scalar_tensor_tensor(out=nlam, in0=sm[:, 1:2], scalar=-LAM_INIT, in1=sm[:, 0:1], op0=ALU.add,
                                         op1=ALU.subtract)

            @block.scalar
            def _(act):
                act.wait_ge(own, 4)
                act.activation(sm[:], sm[:], ACT.Exp).then_inc(exped, 1)


class SampleRows:

    def __init__(self, nc, ctx, cache_k, q_rows):
        sb = lambda n, s, d=F32: ctx.enter_context(nc.sbuf_tensor("sr_" + n, s, d))
        self.xs, self.table = sb("xs", [P, 3 * HEADS_C, SAMPLES]), sb("table", [1, SAMPLES * PAGES], I32)
        self.sc = sb("sc", [P, PAGES, SAMPLES, 2 * HEADS_C])
        self.cache_k, self.q_rows, self.pages = cache_k, q_rows, cache_k.shape[0]

    def buffers(self, nc, ctx):
        sb = lambda n, s, d=F32: ctx.enter_context(nc.sbuf_tensor("sr_" + n, s, d))
        self.page, self.prod, self.query = sb("page", [P, PAGES, D]), sb("prod", [P, PAGES, D]), sb("query", [P, D])
        self.arrived, self.multiplied, self.reduced = (nc.alloc_semaphore("sr_" + n)
                                                       for n in ("arrived", "multiplied", "reduced"))

    def load_page(self, sp, cache, dst, i, signal):
        for j in range(PAGES):
            n = sp.value_load(self.table[0:1, bass.ds(PAGES * i + j, 1)], min_val=0, max_val=self.pages - 1)
            sp.dma_start(dst[:, j, :], cache[bass.ds(n, 1), :, :].rearrange("a p n -> p (a n)")).then_inc(signal, 16)

    def sync(self, sp, b):
        sp.wait_ge(self.multiplied, PAGES * b)
        self.load_page(sp, self.cache_k, self.page, b, self.arrived)
        sp.dma_start(self.query[:], self.q_rows[bass.ds(b, 1), :].rearrange("a n -> (a n)").partition_broadcast(P)
                     ).then_inc(self.arrived, 16)

    def gpsimd(self, pool, b, j):
        pool.wait_ge(self.arrived, 16 * (PAGES + 1) * b + 16 * (PAGES + 1))
        pool.wait_ge(self.reduced, PAGES * b)
        pool.tensor_tensor(self.prod[:, j, :], self.page[:, j, :], self.query[:], ALU.mult).then_inc(self.multiplied, 1)

    def vector(self, dve, b, j):
        dve.wait_ge(self.multiplied, PAGES * b + j + 1)
        dve.tensor_reduce(self.sc[:, j, bass.ds(b, 1), :].rearrange("p a m -> p (a m)"),
                          self.prod[:, j, :].rearrange("p (m d) -> p m d", d=64), AX_X, ALU.add).then_inc(self.reduced, 1)


def stage_sample_rows(nc, T, samples, proj, page_table, k_out, v_out):
    B = SAMPLES
    with ExitStack() as ctx:
        sb = lambda n, s, d=F32: ctx.enter_context(nc.sbuf_tensor("rw_" + n, s, d))
        x_in, table_in, turned, moved, q_scaled, out_done = (
            nc.alloc_semaphore("rw_" + n) for n in "x_in table_in turned moved q_scaled out_done".split())
        rows, q_row = sb("rows", [B, 3 * D]), sb("q_row", [B, D])
        flat = T.ps[0:B, 0:6, :].rearrange("r b n -> r (b n)")
        with nc.Block() as block:
            @block.sync
            def _(sp):
                sp.dma_start(samples.xs[:], proj.rearrange("(m p) n -> p m n", p=P)[:, 0:3 * HEADS_C, PROMPT:TOK]
                             ).then_inc(x_in, 16)
                sp.dma_start(samples.table[:], page_table.rearrange("b j -> (b j)").unsqueeze(0)).then_inc(table_in, 16)
                sp.wait_ge(moved, 1)
                sp.dma_start(k_out, rows[:, D:2 * D]).then_inc(out_done, 16)
                sp.dma_start(v_out, rows[:, 2 * D:3 * D]).then_inc(out_done, 16)
                sp.wait_ge(q_scaled, 1)
                sp.dma_start(samples.q_rows, q_row[:]).then_inc(out_done, 16)
                sp.wait_ge(out_done, 48)
                sp.wait_ge(table_in, 16)

            @block.tensor
            def _(pe):
                pe.wait_ge(x_in, 16)
                for m in range(3 * HEADS_C):
                    ins = pe.transpose(flat[:, P * m:P * m + P], samples.xs[:, m, :], T.ident)
                ins.then_inc(turned, 1)

            @block.vector
            def _(dve):
                dve.wait_ge(turned, 1)
                dve.tensor_copy(rows[:], flat).then_inc(moved, 1)
                dve.wait_ge(moved, 1)
                dve.tensor_scalar(q_row[:], rows[:, 0:D], 64.0 ** -0.5, None, ALU.mult).then_inc(q_scaled, 1)


def stage_attention(nc, T, proj, samples, consts, nlam, subln_rows, k_out, v_out):
    H, NQ = HEADS_C, NCHUNK
    spans = [(i + 1) * P for i in range(NQ)]
    parts = [1 if s <= 512 else 2 for s in spans]
    LEAD = 4

    def ahead(h, p, i, d, more):
        n = i + d
        if n < 0 or (n >= NQ and not more):
            return None
        return (h, p, n) if n < NQ else (h + 1, 1 - p, n - NQ)

    def run_heads(eng, start, head):
        start()
        with eng.Fori(0, H // 2 - 1) as j:
            head(2 * j, 0, True)
            head(2 * j + 1, 1, True)
        head(H - 2, 0, True)
        head(H - 1, 1, False)

    with ExitStack() as ctx:
        sb = lambda n, s, d=F32: ctx.enter_context(nc.sbuf_tensor("at_" + n, s, d))
        sem = lambda n: nc.alloc_semaphore("at_" + n)
        assert SAMPLES == H
        samples.buffers(nc, ctx)
        qin, kin, vin = (sb(n, [P, PROMPT]) for n in ("qin", "kin", "vin"))
        split = lambda p, n: (T.wh, T.wl)[p][:, n * PROMPT:(n + 1) * PROMPT]
        kh, kl = [split(p, 0) for p in range(2)], [split(p, 1) for p in range(2)]
        qh = [[split(p, 2 + c) for c in range(2)] for p in range(2)]
        ql = [[split(p, 4 + c) for c in range(2)] for p in range(2)]
        vt, kt = sb("vt", [P, 2, NQ, P]), sb("kt", [P, NQ, P])
        dist = sb("dist", [P, PROMPT])
        bias = T.wraw[:, 0:2 * PROMPT].rearrange("p (r n) -> p r n", r=2)
        w = T.wraw[:, 2 * PROMPT:4 * PROMPT].rearrange("p (r n) -> p r n", r=2)
        wt = T.wraw[:, 4 * PROMPT:6 * PROMPT].rearrange("p (r t e) -> p r t e", r=2, e=P)
        slope, half = sb("slope", [P, H]), sb("half", [P, 2])
        s = sb("s", [P, 4, 2, PROMPT])
        o, junk = sb("o", [P, 2, NQ, P]), sb("junk", [P, P])
        mx, nmx, sm, rc = (sb(n, [P, 4, 2]) for n in ("mx", "nmx", "sm", "rc"))
        ms = sb("ms", [P, 2, NQ])
        half_in, bias_in, half_done, seen = sem("half_in"), sem("bias_in"), sem("half_done"), sem("seen")
        q_in, k_in, v_in = sem("q_in"), sem("k_in"), sem("v_in")
        q_hi, q_lo, k_hi, k_lo, bias_done = sem("q_hi"), sem("q_lo"), sem("k_hi"), sem("k_lo"), sem("bias_done")
        kv_turned, kv_taken, o_turned, o_taken = sem("kv_turned"), sem("kv_taken"), sem("o_turned"), sem("o_taken")
        v_stored, k_stored = sem("v_stored"), sem("k_stored")
        scored, maxed, negated, exped = sem("scored"), sem("maxed"), sem("negated"), sem("exped")
        inverted, coefs, w_first, weighted = sem("inverted"), sem("coefs"), sem("w_first"), sem("weighted")
        w_turned, wt_moved, av_made, o_moved, squared = (sem(n) for n in "w_turned wt_moved av_made o_moved squared".split())
        logged, rooted, normed = sem("logged"), sem("rooted"), sem("normed")
        mt = proj.rearrange("(m p) n -> m p n", p=P)
        k_rows = k_out.rearrange("(t p) (h e) -> h p t e", p=P, e=P)
        v_rows = v_out.rearrange("(t p) (h e) -> h p t e", p=P, e=P)
        first_bank = lambda c, i: 2 * c + (i % 2 if parts[i] == 1 else 0)
        scores = lambda c, i: T.ps[:, first_bank(c, i):first_bank(c, i) + parts[i], 0:spans[i] // parts[i]]
        av = T.ps[:, 6, 0:P]
        fold = lambda ap, i: ap[:, 0:spans[i]].rearrange("p (a n) -> p a n", a=parts[i])

        with nc.Block() as block:
            @block.sync
            def _(sp):
                def load(h):
                    sp.wait_ge(q_lo, 2 * h)
                    sp.dma_start(qin[:], mt[bass.ds(h, 1), :, 0:PROMPT].rearrange("a p n -> p (a n)")).then_inc(q_in, 16)
                    sp.wait_ge(kv_turned, 4 * h)
                    sp.wait_ge(k_lo, h)
                    sp.dma_start(kin[:], mt[bass.ds(h + H, 1), :, 0:PROMPT].rearrange("a p n -> p (a n)")).then_inc(k_in, 16)
                    sp.dma_start(vin[:], mt[bass.ds(h + 2 * H, 1), :, 0:PROMPT].rearrange("a p n -> p (a n)")).then_inc(v_in, 16)

                def store(h, p):
                    sp.wait_ge(kv_taken, 4 * h + 2)
                    sp.dma_start(v_rows[bass.ds(h, 1), :, :, :].rearrange("a p t e -> p (a t) e"), vt[:, p]).then_inc(v_stored, 16)
                    sp.wait_ge(kv_taken, 4 * h + 4)
                    sp.dma_start(k_rows[bass.ds(h, 1), :, :, :].rearrange("a p t e -> p (a t) e"), kt[:]).then_inc(k_stored, 16)

                def head(h, p, more):
                    store(h, p)
                    if more:
                        load(h + 1)
                    samples.sync(sp, h)

                def start():
                    sp.dma_start(half[:], consts[:, C_HALF:C_HALF + 2]).then_inc(half_in, 16)
                    load(0)
                    sp.dma_start(dist[:], consts[:, C_DIST:C_DIST + PROMPT]).then_inc(bias_in, 16)
                    sp.dma_start(slope[:], consts[:, C_SLOPE:C_SLOPE + H]).then_inc(bias_in, 16)

                run_heads(sp, start, head)
                sp.wait_ge(v_stored, 16 * H)
                sp.wait_ge(k_stored, 16 * H)

            @block.tensor
            def _(pe):
                def turn_kv(h, n, outputs_before):
                    pe.wait_ge((v_in, v_in, k_in, k_in)[n], 16 * h + 16)
                    pe.wait_ge(kv_taken, 4 * h + n)
                    if outputs_before is not None:
                        pe.wait_ge(o_taken, outputs_before)
                    src = (vin, kin)[n // 2]
                    for j in range(4):
                        t = 4 * (n % 2) + j
                        ins = pe.transpose(T.ps[:, 7, P * j:P * j + P], src[:, P * t:P * t + P], T.ident)
                    ins.then_inc(kv_turned, 1)

                def turn_output(h, p, n, kv_before):
                    pe.wait_ge(normed, NQ * h + 4 * n + 4)
                    pe.wait_ge(o_taken, 2 * h + n)
                    pe.wait_ge(kv_taken, kv_before)
                    for j in range(4):
                        ins = pe.transpose(T.ps[:, 7, P * j:P * j + P], o[:, p, 4 * n + j, :], T.ident)
                    ins.then_inc(o_turned, 1)

                def score(h, p, i):
                    if i == 0:
                        pe.wait_ge(q_lo, 2 * h + 2)
                        pe.wait_ge(k_lo, h + 1)
                    width = spans[i] // parts[i]
                    for c in range(2):
                        before = 2 * (i - 2) if i in (2, 3) else -2 if i < 2 else 2 * (i - 1)
                        if not (isinstance(h, int) and h == 0 and before < 0):
                            pe.wait_ge(maxed, 2 * NQ * h + before + c + 1)
                        for part in range(parts[i]):
                            cols = slice(part * width, (part + 1) * width)
                            for n, (a, b) in enumerate(((qh[p][c], kh[p]), (qh[p][c], kl[p]), (ql[p][c], kh[p]))):
                                ins = pe.matmul(T.ps[:, first_bank(c, i) + part, 0:width], a[:, P * i:P * i + P], b[:, cols],
                                                start=n == 0, stop=n == 2)
                        ins.then_inc(scored, 1)

                def turn_weights(h, p, i):
                    pe.wait_ge(weighted, NQ * h + i + 1)
                    pe.wait_ge(wt_moved, NQ * h + i)
                    for t in range(i + 1):
                        ins = pe.transpose(T.ps[:, 4 + t // 4, P * (t % 4):P * (t % 4) + P],
                                           w[:, i % 2, P * t:P * t + P], T.ident)
                    ins.then_inc(w_turned, 1)

                def times_values(h, p, i):
                    pe.wait_ge(wt_moved, NQ * h + i + 1)
                    pe.wait_ge(o_moved, NQ * h + i)
                    if i == 0:
                        pe.wait_ge(kv_taken, 4 * h + 2)
                    for t in range(i + 1):
                        ins = pe.matmul(av, wt[:, i % 2, t, :], vt[:, p, t, :], start=t == 0, stop=t == i)
                    ins.then_inc(av_made, 1)

                def step(h, p, i, more):
                    if i >= 0:
                        times_values(h, p, i)
                    for f, d in ((turn_weights, 1), (score, LEAD)):
                        tile = ahead(h, p, i, d, more)
                        if tile is not None:
                            f(*tile)

                def head(h, p, more):
                    for i in range(NQ):
                        step(h, p, i, more)
                        n = {0: 0, 1: 1, 4: 2, 5: 3}.get(i)
                        if more and n is not None:
                            turn_kv(h + 1, n, 2 * h if p == 0 or n >= 2 else 2 * (h - 1))
                        if p == 1 and i in (2, 3):
                            turn_output(h - 1, 0, i - 2, 4 * (h + 1) + (2 if more else 0))
                    if p == 1:
                        for n in range(2):
                            turn_output(h, 1, n, 4 * (h + 1) + (4 if more else 0))

                def start():
                    for n in range(4):
                        turn_kv(0, n, None)
                    for i in range(-LEAD, 0):
                        step(0, 0, i, True)

                run_heads(pe, start, head)

            @block.scalar
            def _(act):
                def split_q(h, p):
                    act.wait_ge(q_in, 16 * h + 16)
                    for c in range(2):
                        act.activation(qh[p][c], qin[:], ACT.Copy, scale=half[:, c:c + 1]).then_inc(q_hi, 1)

                def split_k(h, p):
                    act.wait_ge(k_in, 16 * h + 16)
                    act.activation(kh[p], kin[:], ACT.Copy).then_inc(k_hi, 1)

                def make_bias(h, p):
                    act.activation(bias[:, p, :], dist[:], ACT.Copy, scale=slope[:, bass.ds(h, 1)]).then_inc(bias_done, 1)

                def take_kv(h, p, n):
                    act.wait_ge(kv_turned, 4 * h + n + 1)
                    dst = (vt[:, p], kt)[n // 2]
                    act.activation(dst[:, 4 * (n % 2):4 * (n % 2) + 4, :], T.ps[:, 7, :].rearrange("p (t e) -> p t e", t=4),
                                   ACT.Copy).then_inc(kv_taken, 1)

                def exponentials(h, p, i):
                    act.wait_ge(negated, NQ * h + i + 1)
                    for c in range(2):
                        x = s[:, i % 4, c, 0:spans[i]]
                        act.activation(x, x, ACT.Exp, bias=nmx[:, i % 4, c:c + 1],
                                       accum_out=sm[:, i % 4, c:c + 1]).then_inc(exped, 1)

                def square(h, p, i):
                    act.wait_ge(o_moved, NQ * h + i + 1)
                    act.wait_ge(squared, NQ * h + i)
                    if i == 0:
                        act.wait_ge(normed, NQ * h if p == 0 else NQ * (h - 1))
                    act.activation(junk[:], o[:, p, i, :], ACT.Square, accum_out=ms[:, p, i:i + 1]).then_inc(squared, 1)

                def take_weights(h, p, i):
                    act.wait_ge(w_turned, NQ * h + i + 1)
                    act.wait_ge(av_made, NQ * h + max(i - 1, 0))
                    for b in range(i // 4 + 1):
                        n = min(4, i + 1 - 4 * b)
                        ins = act.activation(wt[:, i % 2, 4 * b:4 * b + n, :],
                                             T.ps[:, 4 + b, 0:P * n].rearrange("p (t e) -> p t e", t=n), ACT.Copy)
                    ins.then_inc(wt_moved, 1)

                def step(h, p, i, more):
                    tile = ahead(h, p, i, 2, more)
                    if tile is not None:
                        exponentials(*tile)
                    tile = ahead(h, p, i, 1, more)
                    if tile is not None:
                        take_weights(*tile)
                    if i >= 0:
                        square(h, p, i)

                def root(h, p):
                    act.wait_ge(squared, NQ * h + NQ)
                    act.activation(ms[:, p, :], ms[:, p, :], ACT.Ln, scale=1.0 / P, bias=T.eps[:]).then_inc(logged, 1)
                    act.wait_ge(logged, h + 1)
                    act.activation(ms[:, p, :], ms[:, p, :], ACT.Exp, scale=-0.5).then_inc(rooted, 1)

                def take_output(h, n):
                    act.wait_ge(o_turned, 2 * h + n + 1)
                    act.activation(T.acc[:, bass.ds(h, 1), 512 * n:512 * n + 512].rearrange("p a n -> p (a n)"),
                                   T.ps[:, 7, :], ACT.Copy).then_inc(o_taken, 1)

                def head(h, p, more):
                    for i in range(NQ):
                        step(h, p, i, more)
                        if more and i == 0:
                            act.wait_ge(v_stored, 16 * h)
                            act.wait_ge(scored, 2 * NQ * h)
                            split_q(h + 1, 1 - p)
                        if p == 1 and i == 0:
                            root(h - 1, 0)
                        if more and i == 1:
                            split_k(h + 1, 1 - p)
                        if more and i == 2:
                            act.wait_ge(maxed, 2 * NQ * h)
                            make_bias(h + 1, 1 - p)
                        n = {0: 0, 1: 1, 4: 2, 5: 3}.get(i)
                        if more and n is not None:
                            if n == 2:
                                act.wait_ge(k_stored, 16 * h + 16)
                            take_kv(h + 1, 1 - p, n)
                        if p == 1 and i in (2, 3):
                            take_output(h - 1, i - 2)
                    if p == 1:
                        root(h, 1)
                        for n in range(2):
                            take_output(h, n)

                def start():
                    act.wait_ge(half_done, 1)
                    split_q(0, 0)
                    split_k(0, 0)
                    act.wait_ge(bias_in, 32)
                    make_bias(0, 0)
                    for n in range(4):
                        take_kv(0, 0, n)
                    for i in range(-LEAD, 0):
                        step(0, 0, i, True)

                run_heads(act, start, head)

            @block.vector
            def _(dve):
                def split_q(h, p):
                    for c in range(2):
                        dve.wait_ge(q_hi, 2 * h + c + 1)
                        dve.scalar_tensor_tensor(out=ql[p][c], in0=qin[:], scalar=half[:, c:c + 1], in1=qh[p][c],
                                                 op0=ALU.mult, op1=ALU.subtract).then_inc(q_lo, 1)

                def weigh(h, p, i):
                    dve.wait_ge(w_first, NQ * h + i + 1)
                    x = w[:, i % 2, 0:spans[i]]
                    dve.scalar_tensor_tensor(out=x, in0=s[:, i % 4, 1, 0:spans[i]], scalar=rc[:, i % 4, 1:2], in1=x,
                                             op0=ALU.mult, op1=ALU.add).then_inc(weighted, 1)

                def maxima(h, p, i):
                    if i == 0:
                        dve.wait_ge(bias_done, h + 1)
                    for c in range(2):
                        dve.wait_ge(scored, 2 * NQ * h + 2 * i + c + 1)
                        dve.sem_inc(seen, 1)
                        dve.tensor_tensor_reduce(fold(s[:, i % 4, c, :], i), scores(c, i),
                                                 fold(bias[:, p, PROMPT - spans[i]:], i), 1.0,
                                                 -3e38, ALU.add, ALU.max, mx[:, i % 4, c:c + 1]).then_inc(maxed, 1)
                    dve.wait_ge(maxed, 2 * NQ * h + 2 * i + 2)
                    dve.tensor_scalar(nmx[:, i % 4, :], mx[:, i % 4, :], -1.0, None, ALU.mult).then_inc(negated, 1)

                def coefficients(h, p, i):
                    dve.wait_ge(exped, 2 * NQ * h + 2 * i + 2)
                    dve.reciprocal(rc[:, i % 4, :], sm[:, i % 4, :]).then_inc(inverted, 1)
                    dve.wait_ge(inverted, NQ * h + i + 1)
                    dve.tensor_scalar(rc[:, i % 4, 1:2], rc[:, i % 4, 1:2], nlam, None, ALU.mult).then_inc(coefs, 1)

                def take_output(h, p, i):
                    dve.wait_ge(av_made, NQ * h + i + 1)
                    if i == 0:
                        dve.wait_ge(o_turned, 2 * h if p == 0 else 2 * (h - 1))
                    dve.tensor_copy(o[:, p, i, :], av).then_inc(o_moved, 1)

                def norm(h, p):
                    dve.wait_ge(rooted, h + 1)
                    dve.wait_ge(o_moved, NQ * h + NQ)
                    for i in range(NQ):
                        dve.scalar_tensor_tensor(out=o[:, p, i, :], in0=o[:, p, i, :], scalar=ms[:, p, i:i + 1],
                                                 in1=subln_rows, op0=ALU.mult, op1=ALU.mult).then_inc(normed, 1)

                def step(h, p, i, more):
                    for f, d in ((weigh, 1), (maxima, 3), (coefficients, 2)):
                        tile = ahead(h, p, i, d, more)
                        if tile is not None:
                            f(*tile)
                    if i >= 0:
                        take_output(h, p, i)

                def head(h, p, more):
                    for i in range(NQ):
                        step(h, p, i, more)
                        if more and i == 1:
                            split_q(h + 1, 1 - p)
                        if p == 1 and i == 1:
                            norm(h - 1, 0)
                        if i in (4, 6):
                            samples.vector(dve, h, (i - 4) // 2)
                    if p == 1:
                        norm(h, 1)

                def start():
                    dve.wait_ge(half_in, 16)
                    dve.tensor_scalar(half[:], half[:], 64.0 ** -0.5, None, ALU.mult).then_inc(half_done, 1)
                    dve.wait_ge(half_done, 1)
                    split_q(0, 0)
                    for i in range(-LEAD, 0):
                        step(0, 0, i, True)

                run_heads(dve, start, head)

            @block.gpsimd
            def _(pool):
                def split_k(h, p):
                    pool.wait_ge(k_hi, h + 1)
                    pool.tensor_tensor(kl[p], kin[:], kh[p], ALU.subtract).then_inc(k_lo, 1)

                def first(h, p, i):
                    pool.wait_ge(coefs, NQ * h + i + 1)
                    pool.wait_ge(w_turned, NQ * h + (i - 1 if i else 0))
                    pool.tensor_tensor(w[:, i % 2, 0:spans[i]], s[:, i % 4, 0, 0:spans[i]],
                                       rc[:, i % 4, 0:1].to_broadcast([P, spans[i]]), ALU.mult).then_inc(w_first, 1)

                def head(h, p, more):
                    for i in range(NQ):
                        tile = ahead(h, p, i, 2, more)
                        if tile is not None:
                            first(*tile)
                        if more and i == 2:
                            split_k(h + 1, 1 - p)
                        if i in (3, 5):
                            samples.gpsimd(pool, h, (i - 3) // 2)

                def start():
                    split_k(0, 0)
                    for i in range(2):
                        first(0, 0, i)

                run_heads(pool, start, head)


def stage_attention_sample(nc, T, samples, consts, nlam, subln_cols, cache_v):
    H, B = HEADS_C, SAMPLES
    J = H * B
    xs, sc = samples.xs, samples.sc
    with ExitStack() as ctx:
        sb = lambda n, s, d=F32: ctx.enter_context(nc.sbuf_tensor("as_" + n, s, d))
        sem = lambda n: nc.alloc_semaphore("as_" + n)
        R = 4
        page, scp = sb("page", [P, R, PAGES, D]), sb("scp", [P, PAGES, P])
        sbias, half, pair = sb("sbias", [P, PAST + 1]), sb("half", [P, 2]), sb("pair", [P, J])
        s, pn, pq = sb("s", [P, PAST + 1]), sb("pn", [P, 2, J]), sb("pq", [P, J])
        mx, sm, wcol = sb("mx", [P, 2]), sb("sm", [P, 2]), sb("wcol", [P, P])
        wk, wb, spread = sb("wk", [P, PAGES, J]), sb("wb", [P, R, PAGES, H, B]), sb("spread", [P, PAGES, H, B * B])
        o_rows = sb("o_rows", [B, D])
        av, sq, rs = sb("av", [P, H, B]), sb("sq", [P, J]), sb("rs", [P, J])
        con_in, own, t_made, s_moved, exped, p_turned, wc_done, wn_made = (
            sem(n) for n in "con_in own t_made s_moved exped p_turned wc_done wn_made".split())
        v_in, o_made, wb_done = ([sem(f"{n}{r}") for r in range(R)] for n in "v_in o_made wb_done".split())
        zeroed, spread_done, o_moved, o_turned = (sem(n) for n in "zeroed spread_done o_moved o_turned".split())
        own2, ss_made, rooted, act_own = (sem(n) for n in "own2 ss_made rooted act_own".split())

        with nc.Block() as block:
            @block.sync
            def _(sp):
                sp.dma_start(half[:], consts[:, C_HALF:C_HALF + 2]).then_inc(con_in, 16)
                sp.dma_start(sbias[:], consts[:, C_SBIAS:C_SBIAS + PAST + 1]).then_inc(con_in, 16)
                sp.dma_start(pair[:], consts[:, C_PAIR:C_PAIR + J]).then_inc(con_in, 16)
                for r in range(R):
                    samples.load_page(sp, cache_v, page[:, r], r, v_in[r])

            @block.vector
            def _(dve):
                steps = Steps(dve, own)
                dve.wait_ge(con_in, 48)
                q, k = xs[:, 0:H, :], xs[:, H:2 * H, :]
                for j in range(PAGES):
                    steps.note(dve.tensor_copy(scp[:, j, :].rearrange("p (c h b) -> p c h b", c=2, h=H),
                                               sc[:, j].rearrange("p b (h c) -> p c h b", c=2)))
                steps.done(dve.scalar_tensor_tensor(out=pq[:].rearrange("p (h b) -> p h b", h=H), in0=q,
                                                    scalar=64.0 ** -0.5, in1=k, op0=ALU.mult, op1=ALU.mult))
                for c in range(2):
                    steps.note(dve.tensor_scalar(pn[:, c, :], pq[:], half[:, c:c + 1], None, ALU.mult))
                dve.wait_ge(t_made, 1)
                steps.done(dve.tensor_tensor_reduce(s[:], T.ps[:, 0, 0:PAST + 1], sbias[:], 1.0, -3e38, ALU.add, ALU.max,
                                                    mx[:, 0:1]))
                dve.tensor_scalar(mx[:, 1:2], mx[:, 0:1], -1.0, None, ALU.mult).then_inc(s_moved, 1)
                dve.wait_ge(exped, 1)
                steps.done(dve.reciprocal(sm[:, 1:2], sm[:, 0:1]))
                steps.done(dve.tensor_scalar(sm[64:P, 1:2], sm[64:P, 1:2], nlam[64:P, :], None, ALU.mult))
                steps.done(dve.tensor_scalar(s[:], s[:], sm[:, 1:2], None, ALU.mult))
                dve.tensor_copy(wcol[:], s[:, PAST:PAST + 1].to_broadcast([P, P])).then_inc(wc_done, 1)
                dve.wait_ge(p_turned, 1)
                x = T.ps[:, 1, 0:PAGES * P].rearrange("p (j c n) -> p j c n", j=PAGES, c=2)
                steps.done(dve.tensor_copy(wk[:], x[:, :, 0, :]))
                dve.tensor_tensor(wk[:], wk[:], x[:, :, 1, :], ALU.add)

            @block.scalar
            def _(act):
                act.wait_ge(s_moved, 1)
                act.activation(s[:], s[:], ACT.Exp, bias=mx[:, 1:2], accum_out=sm[:, 0:1]).then_inc(exped, 1)

            @block.tensor
            def _(pe):
                pe.wait_ge(own, 5)
                for j in range(PAGES):
                    pe.transpose(T.ps[:, 0, P * j:P * j + P], scp[:, j, :], T.ident)
                pe.matmul(T.ps[:, 0, PAST:PAST + 1], pn[:].rearrange("p c n -> p (c n)"), T.con[:, C_ONE:C_ONE + 1],
                          start=True, stop=True).then_inc(t_made, 1)
                pe.wait_ge(wc_done, 1)
                for j in range(PAGES):
                    ins = pe.transpose(T.ps[:, 1, P * j:P * j + P], s[:, P * j:P * j + P], T.ident)
                ins.then_inc(p_turned, 1)
                pe.wait_ge(con_in, 48)
                pe.matmul(T.ps[:, 2, 0:J], wcol[:], pair[:], start=True, stop=True).then_inc(wn_made, 1)

        with nc.Block() as block:
            @block.sync
            def _(sp):
                with sp.Fori(1, B // R) as i:
                    for r in range(R):
                        sp.wait_ge(o_made[r], i)
                        samples.load_page(sp, cache_v, page[:, r], R * i + r, v_in[r])

            @block.vector
            def _(dve):
                dve.memset(spread[:], 0.0).then_inc(zeroed, 1)
                dve.wait_ge(zeroed, 1)
                dve.tensor_copy(spread[:, :, :, 0:B * B:B + 1], wk[:].rearrange("p j (h b) -> p j h b", b=B)
                                ).then_inc(spread_done, 1)
                dve.wait_ge(spread_done, 1)
                with dve.Fori(0, B // R) as i:
                    for r in range(R):
                        dve.wait_ge(o_made[r], i)
                        dve.tensor_copy(wb[:, r], spread[:, :, :, bass.ds(R * B * i + B * r, B)]).then_inc(wb_done[r], 1)
                for r in range(R):
                    dve.wait_ge(o_made[r], B // R)
                dve.tensor_copy(o_rows[:], T.ps[0:B, 3:5, :].rearrange("b a n -> b (a n)")).then_inc(o_moved, 1)
                dve.wait_ge(o_turned, 1)
                dve.tensor_copy(av[:].rearrange("p h b -> p (h b)"), T.ps[:, 5, 0:J])

            @block.tensor
            def _(pe):
                def sample(i, r, first, last):
                    pe.wait_ge(wb_done[r], i + 1)
                    pe.wait_ge(v_in[r], 16 * PAGES * i + 16 * PAGES)
                    for h in range(H):
                        for j in range(PAGES):
                            ins = pe.matmul(T.ps[0:B, 3 + h // 4, P * (h % 4):P * (h % 4) + P], wb[:, r, j, h, :],
                                            page[:, r, j, P * h:P * h + P], start=first and j == 0 and h % 4 == 0,
                                            stop=last and j == PAGES - 1 and h % 4 == 3)
                    ins.then_inc(o_made[r], 1)

                for i in range(B // R):
                    for r in range(R):
                        sample(i, r, R * i + r == 0, R * i + r == B - 1)
                pe.wait_ge(o_moved, 1)
                for h in range(H):
                    ins = pe.transpose(T.ps[:, 5, B * h:B * h + B], o_rows[:, P * h:P * h + P], T.ident[0:B, 0:B])
                ins.then_inc(o_turned, 1)

        with nc.Block() as block:
            @block.vector
            def _(dve):
                steps = Steps(dve, own2)
                a = av[:].rearrange("p h b -> p (h b)")
                v = xs[:, 2 * H:3 * H, :].rearrange("p h b -> p (h b)")
                steps.done(dve.tensor_tensor(sq[:], v, T.ps[:, 2, 0:J], ALU.mult))
                steps.done(dve.tensor_tensor(a, a, sq[:], ALU.add))
                steps.done(dve.tensor_tensor(sq[:], a, a, ALU.mult))
                dve.wait_ge(rooted, 1)
                steps.done(dve.tensor_tensor(sq[:], a, rs[:], ALU.mult))
                dve.tensor_scalar(T.acc[:, :, PROMPT:TOK], sq[:].rearrange("p (h b) -> p h b", h=H), subln_cols, None,
                                  ALU.mult)

            @block.tensor
            def _(pe):
                pe.wait_ge(own2, 3)
                pe.matmul(T.ps[:, 4, 0:J], T.con[:, C_ONE:C_ONE + P], sq[:], start=True, stop=True).then_inc(ss_made, 1)

            @block.scalar
            def _(act):
                steps = Steps(act, act_own)
                act.wait_ge(ss_made, 1)
                rsqrt_of(act, steps, rs[:], T.ps[:, 4, 0:J], 1.0 / P, T.eps[:]).then_inc(rooted, 1)


def mixer_odd(nc, T, proj, q_rows, ins, outs, consts):
    with ExitStack() as ctx:
        nlam = ctx.enter_context(nc.sbuf_tensor("nlam", [P, 1], F32))
        cols = ctx.enter_context(nc.sbuf_tensor("subln_cols", [P, 1], F32))
        rows = ctx.enter_context(nc.sbuf_tensor("subln_rows", [P, P], F32))
        samples = SampleRows(nc, ctx, ins["cache_k"][0].rearrange("n t h c d -> n t (h c d)"), q_rows)
        stage_lambda(nc, T, nlam[:], cols[:], rows[:], ins["c_lambda"][0], ins["c_subln"][0])
        stage_sample_rows(nc, T, samples, proj, ins["page_table"],
                          outs["k_sample"][0, :, 0].rearrange("b h c d -> b (h c d)"),
                          outs["v_sample"][0, :, 0].rearrange("b h d -> b (h d)"))
        with split_weights(nc, T, "scores"):
            stage_attention(nc, T, proj, samples, consts, nlam[:], rows[:],
                            outs["k_prompt"][0, 0].rearrange("t h c d -> t (h c d)"),
                            outs["v_prompt"][0, 0].rearrange("t h d -> t (h d)"))
        stage_attention_sample(nc, T, samples, consts, nlam[:], cols[:],
                               ins["cache_v"][0].rearrange("n t h d -> n t (h d)"))


def stage_output(nc, T, post_row, x_scratch, y_prompt, y_sample):
    with ExitStack() as ctx:
        sb = lambda n, s, d=F32: ctx.enter_context(nc.sbuf_tensor("out_" + n, s, d))
        sem = lambda n: nc.alloc_semaphore("out_" + n)
        y, ys = sb("y", [P, 2, NCHUNK, P]), sb("ys", [SAMPLES, D])
        xold, rstd = sb("xold", [P, KD, TOK]), sb("rstd", [P, TOK])
        summed, act_own, root, normed, dve_own = (sem(n) for n in "summed act_own root normed dve_own".split())
        x_in = [sem(f"x_in{k}") for k in range(KD)]
        x_new, turned, moved, s_moved = sem("x_new"), sem("turned"), sem("moved"), sem("s_moved")
        stored, s_stored = [sem("stored0"), sem("stored1")], sem("s_stored")
        xs = x_scratch.rearrange("(k p) n -> k p n", p=P)
        dst = y_prompt.rearrange("b (t p) (k e) -> k p (b t) e", p=P, e=P)
        sample_bank = lambda k: 3 - k // 4
        with nc.Block() as block:
            @block.sync
            def _(sp):
                for k in range(KD):
                    sp.dma_start(xold[:, k, :], xs[k]).then_inc(x_in[k], 16)
                for k in range(KD):
                    sp.wait_ge(moved, k + 1)
                    sp.dma_start(dst[k], y[:, k % 2]).then_inc(stored[k % 2], 16)
                sp.wait_ge(s_moved, 1)
                sp.dma_start(y_sample.rearrange("b s d -> (b s) d"), ys[:]).then_inc(s_stored, 16)
                for r in range(2):
                    sp.wait_ge(stored[r], 16 * KD // 2)
                sp.wait_ge(s_stored, 16)

            @block.tensor
            def _(pe):
                ones_times(pe, T, 0, T.sqsum[:]).then_inc(summed, 1)
                for k in range(KD):
                    pe.wait_ge(x_new, k + 1)
                    if k >= 2:
                        pe.wait_ge(moved, k - 1)
                    pe.transpose(T.ps[0:SAMPLES, sample_bank(k), P * (k % 4):P * (k % 4) + P], T.acc[:, k, PROMPT:TOK],
                                 T.ident)
                    for t in range(NCHUNK):
                        ins = pe.transpose(T.ps[:, 4 + 2 * (k % 2) + t // 4, P * (t % 4):P * (t % 4) + P],
                                           T.acc[:, k, P * t:P * t + P], T.ident)
                    ins.then_inc(turned, 1)

            @block.scalar
            def _(act):
                steps = Steps(act, act_own)
                act.wait_ge(summed, 1)
                rsqrt_of(act, steps, chunks(rstd[:]), region(T.ps, 0), 1.0 / D, T.eps[:]).then_inc(root, 1)
                for k in range(KD):
                    act.wait_ge(turned, k + 1)
                    if k >= 2:
                        act.wait_ge(stored[k % 2], 16 * (k // 2))
                    b = 4 + 2 * (k % 2)
                    act.activation(y[:, k % 2], T.ps[:, b:b + 2, :].rearrange("p b (t e) -> p (b t) e", e=P), ACT.Copy
                                   ).then_inc(moved, 1)

            @block.gpsimd
            def _(pool):
                pool.wait_ge(root, 1)
                for k in range(1, KD, 2):
                    pool.tensor_tensor(T.acc[:, k, :], T.acc[:, k, :], rstd[:], ALU.mult).then_inc(normed, 1)

            @block.vector
            def _(dve):
                steps = Steps(dve, dve_own)
                dve.wait_ge(root, 1)
                for k in range(KD):
                    if k % 2 == 0:
                        steps.done(dve.tensor_tensor(T.acc[:, k, :], T.acc[:, k, :], rstd[:], ALU.mult))
                    else:
                        dve.wait_ge(normed, k // 2 + 1)
                    dve.wait_ge(x_in[k], 16)
                    dve.scalar_tensor_tensor(out=T.acc[:, k, :], in0=T.acc[:, k, :],
                                             scalar=T.gain[:, k, post_row:post_row + 1],
                                             in1=xold[:, k, :], op0=ALU.mult, op1=ALU.add).then_inc(x_new, 1)
                dve.wait_ge(turned, KD)
                for n in range(2):
                    ins = dve.tensor_copy(ys[:, 512 * n:512 * n + 512], T.ps[0:SAMPLES, 3 - n, :])
                ins.then_inc(s_moved, 1)


def trunk_step(nc, ins, outs, consts):
    x_t = nc.dram_tensor("x_scratch", [D, TOK], F32, kind="Internal").ap()
    proj0 = nc.dram_tensor("proj_even", [25 * P, TOK], F32, kind="Internal").ap()
    proj1 = nc.dram_tensor("proj_odd", [24 * P, TOK], F32, kind="Internal").ap()
    q_rows = nc.dram_tensor("q_rows", [SAMPLES, D], F32, kind="Internal").ap()
    with ExitStack() as ctx:
        T = open_trunk(nc, ctx)
        with nc.cleanup_on_exit():
            stage_load_x(nc, T, ins["x_prompt"], ins["x_sample"],
                         [ins[n] for n in ("norm_mix_pre", "norm_mix_post", "norm_ffn_pre", "norm_ffn_post")], consts)
        for layer in range(2):
            with nc.cleanup_on_exit():
                with split_weights(nc, T, f"in{layer}"), split_pair(nc, T, f"mix_in{layer}"):
                    feed = projection_feed(nc, T, f"in{layer}", ins["w_in_even" if layer == 0 else "w_in_odd"][0])
                    stage_norm(nc, T, f"nm{layer}", (None, 6)[layer], x_t, feed)
                    source = StageInput(nc, T, f"h{layer}", layer)
                    if layer == 0:
                        conv = QkvConv(ins["b_conv_w"][0], ins["state_gdn_conv"][0], outs["gdn_conv_prompt"][0],
                                       outs["gdn_conv_sample"][0])
                        stage_project(nc, T, "pe", source, feed, 24, proj0, tail=24 * P, conv=conv)
                    else:
                        stage_project(nc, T, "po", source, feed, 24, proj1)
            with nc.cleanup_on_exit():
                if layer == 0:
                    mixer_even(nc, T, proj0, ins, outs, consts)
                else:
                    mixer_odd(nc, T, proj1, q_rows, ins, outs, consts)
            with nc.cleanup_on_exit(), split_weights(nc, T, f"rest{layer}"):
                with split_pair(nc, T, f"mix_out{layer}"):
                    feed = projection_feed(nc, T, f"out{layer}", ins["w_out_even" if layer == 0 else "w_out_odd"][0])
                    stage_project(nc, T, f"po{layer}_", StageInput(nc, T, f"mix{layer}"), feed, 8)
                with split_pair(nc, T, f"ffn_in{layer}"):
                    feed = ffn_feed(nc, T, f"ffn{layer}w", ins["w_ffn_gate"][layer], ins["w_ffn_up"][layer])
                    stage_norm(nc, T, f"nf{layer}", 2 + layer, x_t, feed)
                    source = StageInput(nc, T, f"hf{layer}", 4 + layer)
                    stage_ffn(nc, T, f"ffn{layer}", source, feed, layer, ins["w_ffn_down"][layer], ins["w_ffn_conv"][layer],
                              ins["b_ffn_conv"][layer:layer + 1], ins["state_ffn_conv"], outs["ffn_conv_prompt"],
                              outs["ffn_conv_sample"])
        stage_output(nc, T, 7, x_t, outs["y_prompt"], outs["y_sample"])


_INS = ["x_prompt", "x_sample", "cache_k", "cache_v", "page_table", "state_gdn", "state_gdn_conv", "state_ffn_conv",
        "norm_mix_pre", "norm_mix_post", "norm_ffn_pre", "norm_ffn_post", "w_in_even", "a_v_norm", "a_w_s", "a_b_s",
        "b_conv_w", "b_a_log", "b_dt_bias", "b_out_norm", "w_out_even", "w_in_odd", "c_lambda", "c_subln",
        "w_out_odd", "w_ffn_gate", "w_ffn_up", "w_ffn_conv", "b_ffn_conv", "w_ffn_down"]
_OUTS = [("y_prompt", (1, PROMPT, D)), ("y_sample", (SAMPLES, 1, D)),
         ("gdn_state_prompt", (1, 1, HEADS_B, P, P)), ("gdn_state_sample", (1, SAMPLES, HEADS_B, P, P)),
         ("gdn_conv_prompt", (1, 1, 3, 12 * P)), ("gdn_conv_sample", (1, SAMPLES, 3, 12 * P)),
         ("chunk_v", (1, SAMPLES, 1, 4 * P)),
         ("k_prompt", (1, 1, PROMPT, HEADS_C, 2, 64)), ("v_prompt", (1, 1, PROMPT, HEADS_C, P)),
         ("k_sample", (1, SAMPLES, 1, HEADS_C, 2, 64)), ("v_sample", (1, SAMPLES, 1, HEADS_C, P)),
         ("ffn_conv_prompt", (2, 1, 2, FF)), ("ffn_conv_sample", (2, SAMPLES, 2, FF))]


def kernel(**inputs):
    import concourse.bacc as _bacc
    from concourse.bass_utils import run_bass_kernel_spmd as _run

    nc = _bacc.Bacc("TRN2", target_bir_lowering=False, num_devices=1)
    arrays, ins, outs = {}, {}, {}
    for name in _INS:
        a = np.ascontiguousarray(inputs[name])
        arrays[f"in_{name}"] = a
        ins[name] = nc.dram_tensor(f"in_{name}", a.shape, mybir.dt.from_np(a.dtype), kind="ExternalInput").ap()
    arrays["in_constants"] = shape_constants()
    consts = nc.dram_tensor("in_constants", [P, C_END], F32, kind="ExternalInput").ap()
    for name, shape in _OUTS:
        outs[name] = nc.dram_tensor(f"out_{name}", shape, F32, kind="ExternalOutput").ap()
    trunk_step(nc, ins, outs, consts)
    r = _run(nc, [arrays], core_ids=[0])
    return tuple(r.results[0][f"out_{name}"] for name, _ in _OUTS)
```
